# Optimizing a Trainium2 kernel written in Bass

```python
import math
import jax, jax.numpy as jnp
from jax import lax
import numpy as np
import jax
import jax.numpy as jnp

D_MODEL = 1024
BATCH = 1
SEQ = 256
DEPTH = 2

N_MIXERS = 2
PLE_DIM = 256
FFN_HIDDEN = ((8 * D_MODEL // 3 + 255) // 256) * 256
DA_HEADS = 8
DA_HEAD_DIM = D_MODEL // (2 * DA_HEADS)
Q_BLOCK = 128
NA_HEADS = 16
NA_HEAD_DIM = D_MODEL // NA_HEADS
GRID_W = 64
NA_KR = 8
NA_KC = 16
NORM_EPS = 1e-6
SUBLN_EPS = 1e-5


def rmsnorm(x, g, eps=NORM_EPS):
    xf = x.astype(jnp.float32)
    y = xf * lax.rsqrt(jnp.mean(xf * xf, axis=-1, keepdims=True) + eps)
    return (y * g.astype(jnp.float32)).astype(x.dtype)

def alibi_slopes(n_heads):
    return jnp.array([2.0 ** (-8.0 * (h + 1) / n_heads) for h in range(n_heads)], dtype=jnp.float32)

def diff_attention(h, w_qkv, w_o, lq1, lk1, lq2, lk2, subln, layer_idx):
    B, S, _ = h.shape
    qkv = h @ w_qkv
    q, k, v = jnp.split(qkv, 3, axis=-1)
    q = q.reshape(B, S, DA_HEADS, 2, DA_HEAD_DIM).transpose(3, 0, 2, 1, 4)
    k = k.reshape(B, S, DA_HEADS, 2, DA_HEAD_DIM).transpose(3, 0, 2, 1, 4)
    v = v.reshape(B, S, DA_HEADS, 2 * DA_HEAD_DIM).transpose(0, 2, 1, 3)
    lam_init = 0.8 - 0.6 * math.exp(-0.3 * layer_idx)
    lam = (jnp.exp(jnp.sum(lq1.astype(jnp.float32) * lk1.astype(jnp.float32)))
           - jnp.exp(jnp.sum(lq2.astype(jnp.float32) * lk2.astype(jnp.float32)))
           + lam_init)
    slopes = alibi_slopes(DA_HEADS)
    scale = DA_HEAD_DIM ** -0.5
    nblk = S // Q_BLOCK
    qb = q.reshape(2, B, DA_HEADS, nblk, Q_BLOCK, DA_HEAD_DIM).transpose(3, 0, 1, 2, 4, 5)
    kpos = jnp.arange(S)

    def block(args):
        qblk, bi = args
        qpos = bi * Q_BLOCK + jnp.arange(Q_BLOCK)
        dist = jnp.abs(qpos[:, None] - kpos[None, :]).astype(jnp.float32)
        bias = -slopes[:, None, None] * dist
        s = jnp.einsum('mbhqd,mbhkd->mbhqk', qblk, k).astype(jnp.float32) * scale + bias
        a = jax.nn.softmax(s, axis=-1)
        a = a[0] - lam * a[1]
        return jnp.einsum('bhqk,bhkd->bhqd', a.astype(v.dtype), v)

    o = lax.map(block, (qb, jnp.arange(nblk)))
    o = o.transpose(1, 0, 3, 2, 4).reshape(B, S, DA_HEADS, 2 * DA_HEAD_DIM)
    o = rmsnorm(o, subln, eps=SUBLN_EPS) * (1.0 - lam_init)
    return o.reshape(B, S, D_MODEL) @ w_o

def neighborhood_attention(h, w_qkv, b_qkv, rpb, w_o):
    B, S, _ = h.shape
    rows = S // GRID_W
    kr = min(NA_KR, rows)
    W = GRID_W
    qkv = h @ w_qkv + b_qkv
    qkv = qkv.reshape(B, rows, W, 3, NA_HEADS, NA_HEAD_DIM).transpose(3, 0, 4, 1, 2, 5)
    q = qkv[0] * (NA_HEAD_DIM ** -0.5)
    k = qkv[1]
    v = qkv[2]
    cols = jnp.arange(W)
    cstart = jnp.clip(cols - NA_KC // 2, 0, W - NA_KC)
    col_mask = (cols[None, :] >= cstart[:, None]) & (cols[None, :] < cstart[:, None] + NA_KC)
    col_off = jnp.clip(cols[None, :] - cols[:, None], -(NA_KC - 1), NA_KC - 1) + (NA_KC - 1)
    rpb_cols = rpb[:, :, col_off]
    key_mask = jnp.tile(col_mask, (1, kr))

    def row_block(r):
        rs = jnp.clip(r - kr // 2, 0, rows - kr)
        kb = lax.dynamic_slice_in_dim(k, rs, kr, axis=2).reshape(B, NA_HEADS, kr * W, NA_HEAD_DIM)
        vb = lax.dynamic_slice_in_dim(v, rs, kr, axis=2).reshape(B, NA_HEADS, kr * W, NA_HEAD_DIM)
        qr = lax.dynamic_index_in_dim(q, r, axis=2, keepdims=False)
        row_off = rs + jnp.arange(kr) - r + (NA_KR - 1)
        bias = jnp.take(rpb_cols, row_off, axis=1)
        bias = bias.transpose(0, 2, 1, 3).reshape(NA_HEADS, W, kr * W).astype(jnp.float32)
        s = jnp.einsum('bhqd,bhkd->bhqk', qr, kb).astype(jnp.float32) + bias
        s = jnp.where(key_mask, s, -jnp.inf)
        a = jax.nn.softmax(s, axis=-1)
        return jnp.einsum('bhqk,bhkd->bhqd', a.astype(vb.dtype), vb)

    o = lax.map(row_block, jnp.arange(rows))
    o = o.transpose(1, 0, 3, 2, 4).reshape(B, S, D_MODEL)
    return o @ w_o

def swiglu(h, w_gate, w_up, w_down):
    return (jax.nn.silu(h @ w_gate) * (h @ w_up)) @ w_down

def first_inputs(seed: int = 0) -> dict:
    key = jax.random.key(seed)
    ks = jax.random.split(key, 24)
    n_a = (DEPTH + 1) // 2
    n_b = DEPTH // 2
    D, F = D_MODEL, FFN_HIDDEN
    f32 = jnp.float32

    def nrm(k, shape, scale):
        return jax.random.normal(k, shape, f32) * scale

    return {
        "x": nrm(ks[0], (BATCH, SEQ, D), 1.0),
        "p": nrm(ks[1], (DEPTH, BATCH, SEQ, PLE_DIM), 1.0),
        "norm_mix": 1.0 + nrm(ks[2], (DEPTH, D), 0.05),
        "norm_ffn": 1.0 + nrm(ks[3], (DEPTH, D), 0.05),
        "norm_ple": 1.0 + nrm(ks[4], (DEPTH, D), 0.05),
        "norm_final": 1.0 + nrm(ks[5], (D,), 0.05),
        "da_w_qkv": nrm(ks[6], (n_a, D, 3 * D), D ** -0.5),
        "da_w_o": nrm(ks[7], (n_a, D, D), D ** -0.5),
        "da_lambda_q1": nrm(ks[8], (n_a, DA_HEAD_DIM), 0.1),
        "da_lambda_k1": nrm(ks[9], (n_a, DA_HEAD_DIM), 0.1),
        "da_lambda_q2": nrm(ks[10], (n_a, DA_HEAD_DIM), 0.1),
        "da_lambda_k2": nrm(ks[11], (n_a, DA_HEAD_DIM), 0.1),
        "da_subln": 1.0 + nrm(ks[12], (n_a, 2 * DA_HEAD_DIM), 0.05),
        "na_w_qkv": nrm(ks[13], (n_b, D, 3 * D), D ** -0.5),
        "na_b_qkv": nrm(ks[14], (n_b, 3 * D), 0.02),
        "na_rpb": nrm(ks[15], (n_b, NA_HEADS, 2 * NA_KR - 1, 2 * NA_KC - 1), 0.5),
        "na_w_o": nrm(ks[16], (n_b, D, D), D ** -0.5),
        "ffn_w_gate": nrm(ks[17], (DEPTH, D, F), D ** -0.5),
        "ffn_w_up": nrm(ks[18], (DEPTH, D, F), D ** -0.5),
        "ffn_w_down": nrm(ks[19], (DEPTH, F, D), F ** -0.5),
        "ple_w_proj": nrm(ks[20], (DEPTH, PLE_DIM, D), PLE_DIM ** -0.5),
        "ple_w_gate": nrm(ks[21], (DEPTH, D, D), D ** -0.5),
    }

def first_block(x, p, norm_mix, norm_ffn, norm_ple, norm_final,
              da_w_qkv, da_w_o, da_lambda_q1, da_lambda_k1, da_lambda_q2, da_lambda_k2, da_subln,
              na_w_qkv, na_b_qkv, na_rpb, na_w_o,
              ffn_w_gate, ffn_w_up, ffn_w_down, ple_w_proj, ple_w_gate):
    h = x
    for i in range(DEPTH):
        hn = rmsnorm(h, norm_mix[i])
        j = i // N_MIXERS
        if i % N_MIXERS == 0:
            mix = diff_attention(hn, da_w_qkv[j], da_w_o[j], da_lambda_q1[j], da_lambda_k1[j],
                                 da_lambda_q2[j], da_lambda_k2[j], da_subln[j], i)
        else:
            mix = neighborhood_attention(hn, na_w_qkv[j], na_b_qkv[j], na_rpb[j], na_w_o[j])
        h = h + mix
        h = h + swiglu(rmsnorm(h, norm_ffn[i]), ffn_w_gate[i], ffn_w_up[i], ffn_w_down[i])
        gate = jax.nn.sigmoid(rmsnorm(h, norm_ple[i]) @ ple_w_gate[i])
        h = h + gate * (p[i] @ ple_w_proj[i])
    return rmsnorm(h, norm_final)


N_EVEN = (DEPTH + 1) // 2
N_ODD = DEPTH // 2
HEAD_DIM = 64
CONV_W = 3
A_W = D_MODEL // 2
B_W = D_MODEL - A_W
POOL_WINDOWS = (2, 4, 8, 16)
N_POOL = len(POOL_WINDOWS)
POOL_G = B_W // N_POOL
EV_IN_W = 3 * A_W + B_W
MIX_W = A_W + B_W
H_FOX = D_MODEL // (2 * HEAD_DIM)
H_MOBA = D_MODEL // (2 * HEAD_DIM)
H_ATT = H_FOX + H_MOBA
ATT_W = H_ATT * HEAD_DIM
OD_IN_W = 3 * ATT_W + H_FOX
ATTN_SCALE = HEAD_DIM ** -0.5
FOX_Q_BLOCK = 128
MOBA_BLOCK = 256
MOBA_TOPK = 3
MOBA_Q_CHUNK = 32
T5_BUCKETS = 32
T5_MAX_DIST = 128
FORGET_BIAS_INIT = 2.0
D_FF = 2816
RMS_EPS = 1e-6


def rmsnorm_2(x, g):
    xf = x.astype(jnp.float32)
    y = xf * lax.rsqrt(jnp.mean(xf * xf, axis=-1, keepdims=True) + RMS_EPS)
    return (y * g.astype(jnp.float32)).astype(x.dtype)

def causal_dwconv(u, w):
    s = u.shape[1]
    up = jnp.pad(u, ((0, 0), (CONV_W - 1, 0), (0, 0)))
    return sum(w[i] * up[:, i:i + s] for i in range(CONV_W))

def multiscale_pool(u, pool_w, pool_scale):
    bsz, s, _ = u.shape
    cs = jnp.cumsum(jnp.pad(u.astype(jnp.float32), ((0, 0), (1, 0), (0, 0))), axis=1)
    pos = jnp.arange(s)
    groups = []
    for g, w in enumerate(POOL_WINDOWS):
        csg = cs[..., g * POOL_G:(g + 1) * POOL_G]
        hi = csg[:, 1:]
        lo = jnp.pad(csg[:, :s + 1 - w], ((0, 0), (w - 1, 0), (0, 0)))
        cnt = jnp.minimum(pos + 1, w).astype(jnp.float32)[None, :, None]
        groups.append((hi - lo) / cnt - u[..., g * POOL_G:(g + 1) * POOL_G].astype(jnp.float32))
    p = jnp.stack(groups, axis=2).astype(u.dtype)
    y = jnp.einsum('bsgc,gcd->bsgd', p, pool_w).reshape(bsz, s, B_W)
    return y * pool_scale

def even_mixer(h, w_in, conv_w, pool_w, pool_scale, w_out):
    z = h @ w_in
    gate_b = z[..., :A_W]
    gate_c = z[..., A_W:2 * A_W]
    val = z[..., 2 * A_W:3 * A_W]
    pool_in = z[..., 3 * A_W:]
    y_a = gate_b * causal_dwconv(gate_c * val, conv_w)
    y_b = multiscale_pool(pool_in, pool_w, pool_scale)
    return jnp.concatenate([y_a, y_b], axis=-1) @ w_out

def t5_bucket(dist):
    dist = jnp.maximum(dist, 0)
    exact = T5_BUCKETS // 2
    d_f = jnp.maximum(dist, 1).astype(jnp.float32)
    log_b = exact + (jnp.log(d_f / exact) / math.log(T5_MAX_DIST / exact)
                     * (T5_BUCKETS - exact)).astype(jnp.int32)
    log_b = jnp.minimum(log_b, T5_BUCKETS - 1)
    return jnp.where(dist < exact, dist, log_b)

def forgetting_attention(q, k, v, log_f):
    bsz, nh, s, dh = q.shape
    fcum = jnp.cumsum(log_f, axis=-1)
    nq = s // FOX_Q_BLOCK
    q_blocks = q.reshape(bsz, nh, nq, FOX_Q_BLOCK, dh).transpose(2, 0, 1, 3, 4)
    f_blocks = fcum.reshape(bsz, nh, nq, FOX_Q_BLOCK).transpose(2, 0, 1, 3)
    kpos = jnp.arange(s)

    def one_block(args):
        i, q_i, f_i = args
        qpos = i * FOX_Q_BLOCK + jnp.arange(FOX_Q_BLOCK)
        logits = jnp.einsum('bhqd,bhkd->bhqk', q_i, k).astype(jnp.float32) * ATTN_SCALE
        logits = logits + f_i[..., :, None] - fcum[..., None, :]
        logits = jnp.where(kpos[None, :] <= qpos[:, None], logits, -jnp.inf)
        p = jax.nn.softmax(logits, axis=-1)
        return jnp.einsum('bhqk,bhkd->bhqd', p.astype(v.dtype), v)

    out = lax.map(one_block, (jnp.arange(nq), q_blocks, f_blocks))
    return out.transpose(1, 2, 0, 3, 4).reshape(bsz, nh, s, dh)

def moba_attention(q, k, v, rel_bias):
    bsz, nh, s, dh = q.shape
    n_blk = -(-s // MOBA_BLOCK)
    pad = n_blk * MOBA_BLOCK - s
    k_p = jnp.pad(k, ((0, 0), (0, 0), (0, pad), (0, 0)))
    v_p = jnp.pad(v, ((0, 0), (0, 0), (0, pad), (0, 0)))
    k_blk = k_p.reshape(bsz, nh, n_blk, MOBA_BLOCK, dh)
    v_blk = v_p.reshape(bsz, nh, n_blk, MOBA_BLOCK, dh)
    k_mean = jnp.mean(k_blk.astype(jnp.float32), axis=3)
    topk = min(MOBA_TOPK, n_blk)
    nq = s // MOBA_Q_CHUNK
    q_chunks = q.reshape(bsz, nh, nq, MOBA_Q_CHUNK, dh).transpose(2, 0, 1, 3, 4)
    blk_ids = jnp.arange(n_blk)
    kpos_in_blk = jnp.arange(MOBA_BLOCK)
    head_ids = jnp.arange(nh)[:, None, None, None]
    bias_t = rel_bias.T
    gather_blocks = jax.vmap(jax.vmap(lambda kb, ix: kb[ix]))

    def one_chunk(args):
        c, q_i = args
        start = c * MOBA_Q_CHUNK
        cur = start // MOBA_BLOCK
        qpos = start + jnp.arange(MOBA_Q_CHUNK)
        gate = jnp.einsum('bhqd,bhnd->bhqn', q_i.astype(jnp.float32), k_mean)
        gate = jnp.where(blk_ids < cur, gate, -jnp.inf)
        _, idx = lax.top_k(gate, topk)
        valid = idx < cur
        k_sel = gather_blocks(k_blk, idx)
        v_sel = gather_blocks(v_blk, idx)
        kpos_sel = idx[..., None] * MOBA_BLOCK + kpos_in_blk
        bias_sel = bias_t[head_ids, t5_bucket(qpos[:, None, None] - kpos_sel)]
        l_sel = jnp.einsum('bhqd,bhqtld->bhqtl', q_i, k_sel).astype(jnp.float32) * ATTN_SCALE
        l_sel = jnp.where(valid[..., None], l_sel + bias_sel, -jnp.inf)
        k_own = lax.dynamic_slice_in_dim(k_p, cur * MOBA_BLOCK, MOBA_BLOCK, axis=2)
        v_own = lax.dynamic_slice_in_dim(v_p, cur * MOBA_BLOCK, MOBA_BLOCK, axis=2)
        kpos_own = cur * MOBA_BLOCK + kpos_in_blk
        dist_own = qpos[:, None] - kpos_own[None, :]
        bias_own = rel_bias[t5_bucket(dist_own)].transpose(2, 0, 1)
        l_own = jnp.einsum('bhqd,bhld->bhql', q_i, k_own).astype(jnp.float32) * ATTN_SCALE
        l_own = jnp.where(dist_own >= 0, l_own + bias_own, -jnp.inf)
        logits = jnp.concatenate(
            [l_sel.reshape(bsz, nh, MOBA_Q_CHUNK, topk * MOBA_BLOCK), l_own], axis=-1)
        p = jax.nn.softmax(logits, axis=-1).astype(v.dtype)
        p_sel = p[..., :topk * MOBA_BLOCK].reshape(bsz, nh, MOBA_Q_CHUNK, topk, MOBA_BLOCK)
        p_own = p[..., topk * MOBA_BLOCK:]
        return (jnp.einsum('bhqtl,bhqtld->bhqd', p_sel, v_sel)
                + jnp.einsum('bhql,bhld->bhqd', p_own, v_own))

    out = lax.map(one_chunk, (jnp.arange(nq), q_chunks))
    return out.transpose(1, 2, 0, 3, 4).reshape(bsz, nh, s, dh)

def odd_mixer(h, w_in, b_f, w_out, rel_bias):
    bsz, s, _ = h.shape
    z = h @ w_in
    qkv = z[..., :3 * ATT_W].reshape(bsz, s, 3, H_ATT, HEAD_DIM).transpose(2, 0, 3, 1, 4)
    q, k, v = qkv[0], qkv[1], qkv[2]
    log_f = jax.nn.log_sigmoid((z[..., 3 * ATT_W:] + b_f).astype(jnp.float32)).transpose(0, 2, 1)
    y_c = forgetting_attention(q[:, :H_FOX], k[:, :H_FOX], v[:, :H_FOX], log_f)
    y_d = moba_attention(q[:, H_FOX:], k[:, H_FOX:], v[:, H_FOX:], rel_bias)
    y = jnp.concatenate([y_c, y_d], axis=1).transpose(0, 2, 1, 3).reshape(bsz, s, ATT_W)
    return y @ w_out

def conv_ffn(h, w_in, conv_w, conv_b, w_out):
    z = h @ w_in
    u, g = z[..., :D_FF], z[..., D_FF:]
    a = causal_dwconv(u, conv_w) + conv_b
    return (jax.nn.silu(a) * g) @ w_out

def second_inputs(seed: int = 0) -> dict:
    key = jax.random.key(seed)
    ks = jax.random.split(key, 17)
    f32 = jnp.float32

    def nrm(k, shape, scale):
        return jax.random.normal(k, shape, f32) * scale

    out_scale = (2 * DEPTH) ** -0.5
    return {
        "x": nrm(ks[0], (BATCH, SEQ, D_MODEL), 1.0),
        "mix_norm_g": 1.0 + nrm(ks[1], (DEPTH, D_MODEL), 0.05),
        "ffn_norm_g": 1.0 + nrm(ks[2], (DEPTH, D_MODEL), 0.05),
        "final_norm_g": 1.0 + nrm(ks[3], (D_MODEL,), 0.05),
        "ev_w_in": nrm(ks[4], (N_EVEN, D_MODEL, EV_IN_W), D_MODEL ** -0.5),
        "ev_conv_w": nrm(ks[5], (N_EVEN, CONV_W, A_W), CONV_W ** -0.5),
        "ev_pool_w": nrm(ks[6], (N_EVEN, N_POOL, POOL_G, POOL_G), POOL_G ** -0.5),
        "ev_pool_scale": 1.0 + nrm(ks[7], (N_EVEN, B_W), 0.1),
        "ev_w_out": nrm(ks[8], (N_EVEN, MIX_W, D_MODEL), MIX_W ** -0.5 * out_scale),
        "od_w_in": nrm(ks[9], (N_ODD, D_MODEL, OD_IN_W), D_MODEL ** -0.5),
        "od_b_f": FORGET_BIAS_INIT + nrm(ks[10], (N_ODD, H_FOX), 0.5),
        "od_w_out": nrm(ks[11], (N_ODD, ATT_W, D_MODEL), ATT_W ** -0.5 * out_scale),
        "rel_bias": nrm(ks[12], (T5_BUCKETS, H_MOBA), 0.5),
        "ffn_w_in": nrm(ks[13], (DEPTH, D_MODEL, 2 * D_FF), D_MODEL ** -0.5),
        "ffn_conv_w": nrm(ks[14], (DEPTH, CONV_W, D_FF), CONV_W ** -0.5),
        "ffn_conv_b": nrm(ks[15], (DEPTH, D_FF), 0.02),
        "ffn_w_out": nrm(ks[16], (DEPTH, D_FF, D_MODEL), D_FF ** -0.5 * out_scale),
    }

def second_block(x, mix_norm_g, ffn_norm_g, final_norm_g, ev_w_in, ev_conv_w, ev_pool_w,
              ev_pool_scale, ev_w_out, od_w_in, od_b_f, od_w_out, rel_bias,
              ffn_w_in, ffn_conv_w, ffn_conv_b, ffn_w_out):
    h = x
    for layer in range(DEPTH):
        hn = rmsnorm_2(h, mix_norm_g[layer])
        if layer % 2 == 0:
            e = layer // 2
            h = h + even_mixer(hn, ev_w_in[e], ev_conv_w[e], ev_pool_w[e],
                               ev_pool_scale[e], ev_w_out[e])
        else:
            o = layer // 2
            h = h + odd_mixer(hn, od_w_in[o], od_b_f[o], od_w_out[o], rel_bias)
        h = h + conv_ffn(rmsnorm_2(h, ffn_norm_g[layer]), ffn_w_in[layer],
                         ffn_conv_w[layer], ffn_conv_b[layer], ffn_w_out[layer])
    return rmsnorm_2(h, final_norm_g)


def setup_inputs(seed=0):
    out = dict(first_inputs(seed))
    for name, value in second_inputs(seed + 1).items():
        if name != "x":
            out[name + "_2"] = value
    return out


def reference(
    x, p, norm_mix, norm_ffn, norm_ple, norm_final, da_w_qkv, da_w_o, da_lambda_q1,
    da_lambda_k1, da_lambda_q2, da_lambda_k2, da_subln, na_w_qkv, na_b_qkv, na_rpb, na_w_o,
    ffn_w_gate, ffn_w_up, ffn_w_down, ple_w_proj, ple_w_gate, mix_norm_g_2, ffn_norm_g_2,
    final_norm_g_2, ev_w_in_2, ev_conv_w_2, ev_pool_w_2, ev_pool_scale_2, ev_w_out_2, od_w_in_2,
    od_b_f_2, od_w_out_2, rel_bias_2, ffn_w_in_2, ffn_conv_w_2, ffn_conv_b_2, ffn_w_out_2,
):
    x = first_block(
        x, p, norm_mix, norm_ffn, norm_ple, norm_final, da_w_qkv, da_w_o, da_lambda_q1,
        da_lambda_k1, da_lambda_q2, da_lambda_k2, da_subln, na_w_qkv, na_b_qkv, na_rpb, na_w_o,
        ffn_w_gate, ffn_w_up, ffn_w_down, ple_w_proj, ple_w_gate,
    )
    return second_block(
        x, mix_norm_g_2, ffn_norm_g_2, final_norm_g_2, ev_w_in_2, ev_conv_w_2, ev_pool_w_2,
        ev_pool_scale_2, ev_w_out_2, od_w_in_2, od_b_f_2, od_w_out_2, rel_bias_2, ffn_w_in_2,
        ffn_conv_w_2, ffn_conv_b_2, ffn_w_out_2,
    )


_drawn_inputs = setup_inputs


def setup_inputs(seed=0):
    import zlib

    import numpy as np

    out = dict(_drawn_inputs(seed))
    spreads = {}
    factors = {'norm_ple': 5.121,
     'da_lambda_k1': 8.0,
     'da_lambda_q2': 8.0,
     'na_b_qkv': 3.552,
     'ffn_conv_b_2': 7.629}
    for name, (base, spread) in spreads.items():
        noise = np.random.default_rng([zlib.crc32(name.encode()), seed]).standard_normal(out[name].shape)
        drawn = base * np.exp(spread * noise) if base else spread * noise
        out[name] = jnp.asarray(drawn.astype(out[name].dtype))
    for name, factor in factors.items():
        out[name] = (out[name] * factor).astype(out[name].dtype)
    return out
```

```python
from contextlib import ExitStack

import numpy as np
import concourse.bass as bass
from concourse import mybir

F32 = mybir.dt.float32
F32R = mybir.dt.float32r
ALU = mybir.AluOpType
ACT = mybir.ActivationFunctionType
X = mybir.AxisListType.X

P = 128
D = 1024
S = 256
KT = D // P
TT = S // P
FFN = 2816
FT = FFN // P
HEADS = 16
PAIRS = HEADS // 2
DH = 64
GRID_W = 64
LAM_INIT = 0.2
MASKED = -1e30

RING = 3
CHUNK = KT * 256
NORM_EPS = 1e-6
SUBLN_EPS = 1e-5

COL_BQK, COL_EVCONV, COL_PSCALE = 0, 16, 28
COL_CONV = (32, 32 + 3 * FT)
COL_CONVB = (32 + 6 * FT, 32 + 7 * FT)
COL_SUBLN = 32 + 8 * FT
COL_BF = COL_SUBLN + 1
NCOLS = COL_BF + 1

C_ID, C_DIST, C_COLM, C_CAUS, C_SEL, NCONST = 0, 128, 640, 704, 1088, 1104


def make_plan():
    plan = []
    for layer in (0, 1):
        plan += [(f"qk{layer}", "F", 8), (f"v{layer}", "T", 4), (f"wo{layer}", "T", 4),
                 (f"ffn{layer}", "F", FT), (f"down{layer}", "T", FT // 2),
                 (f"proj{layer}", "T", 1), (f"gate{layer}", "T", 4)]
    plan += [("ev", "F", 8), ("evout", "T", 4), ("ffn2", "F", FT), ("down2", "T", FT // 2),
             ("qk3", "F", 8), ("f3", "F", 1), ("v3", "T", 4), ("wo3", "T", 4),
             ("ffn3", "F", FT), ("down3", "T", FT // 2)]
    start, tindex, at, t = {}, {}, 0, 0
    for name, kind, n in plan:
        start[name] = at
        at += n
        if kind == "T":
            tindex[name] = t
            t += 1
    return plan, start, tindex, at


PLAN, START, TINDEX, NCHUNKS = make_plan()
COUNT = {name: n for name, _, n in PLAN}

NORMS = ("mix0", "ffn0", "ple0", "mix1", "ffn1", "ple1", "mid", "mix2", "ffn2", "mix3", "ffn3",
         "final")
NORM = {name: n for n, name in enumerate(NORMS)}
XNORM = {name: n for n, name in enumerate(m for m in NORMS if m != "mid")}
UNITS = 2 * PAIRS
SC_BASE = (0, UNITS, 2 * UNITS)
TR_BASE = (0, PAIRS, PAIRS + UNITS)
MIX_BASE = {"wo0": 0, "wo1": 4, "evout": 12, "wo3": 14}
MIX_COUNT = {"wo0": 4, "wo1": 8, "evout": 2, "wo3": 8}
COPY_BASE = {"qk0": 0, "qk1": 8, "ev": 16, "qk3": 24}


def mixer_kernel(nc, w, small, cols, consts, evconst, out):
    with ExitStack() as ctx:
        def sb(name, shape, dt=F32, c=ctx):
            return c.enter_context(nc.sbuf_tensor(name, shape, dt))

        def sem(name):
            return ctx.enter_context(nc.semaphore(name))

        raw = sb("raw", [P, RING, CHUNK])
        whi = sb("whi", [P, RING, CHUNK], F32R)
        wlo = sb("wlo", [P, RING, CHUNK], F32R)
        h = sb("h", [P, TT, D])
        hn = sb("hn", [P, TT, D])
        xhi = sb("xhi", [P, KT, S], F32R)
        xlo = sb("xlo", [P, KT, S], F32R)
        gam = sb("gam", [P, 2, D])
        vbias = sb("vbias", [P, D])
        praw = sb("praw", [P, 2, S])
        phi = sb("phi", [P, 2, S], F32R)
        plo = sb("plo", [P, 2, S], F32R)
        col = sb("col", [P, NCOLS])
        cst = sb("cst", [P, NCONST])
        lamv = sb("lamv", [P, 4, DH])
        tiny = sb("tiny", [P, 64])
        nmax = sb("nmax", [P, UNITS, TT])
        sums = sb("sums", [P, UNITS, TT])
        rsum = sb("rsum", [P, UNITS, TT])
        half = sb("half", [P, 16])
        with ExitStack() as c:
            nab = sb("nab", [P, HEADS, 6 * GRID_W], F32, c)
        with ExitStack() as c:
            t5b = sb("t5b", [P, 8, 384], F32, c)
            t5row = sb("t5row", [8, 384], F32, c)
            onehot = sb("onehot", [32, 384], F32, c)
            relb = sb("relb", [32, 8], F32, c)
        ctx.enter_context(nc.sbuf_tensor("bias_region", [P, HEADS * 6 * GRID_W], F32))
        with ExitStack() as c:
            hidhi = sb("hidhi", [P, FT, S], F32R, c)
            hidlo = sb("hidlo", [P, FT, S], F32R, c)
            act = sb("act", [P, 3, S], F32, c)
            mul = sb("mul", [P, 3, S], F32, c)
        with ExitStack() as c:
            qkT = sb("qkT", [P, 16, S], F32, c)
            v = sb("v", [P, TT, D], F32, c)
            prob = sb("prob", [P, 4, TT * S], F32, c)
            probT = sb("probT", [P, 2, TT * S], F32, c)
            with ExitStack() as c2:
                osb = sb("osb", [P, TT, D], F32, c2)
            with ExitStack() as c2:
                fstat = sb("fstat", [P, 8, S], F32, c2)
                fmov = sb("fmov", [P, 8, S], F32, c2)
        with ExitStack() as c:
            z = sb("z", [P, 12, S], F32, c)
            pool = sb("pool", [P, 3, 4, 16 + S], F32, c)
            cval = sb("cval", [P, 4, S], F32, c)
            ya = sb("ya", [P, 4, S], F32, c)
            pw = sb("pw", [P, 4, P], F32, c)
            icnt = sb("icnt", [P, 4, S], F32, c)
        region = max(2 * FT * S + 6 * S, 16 * S + TT * D + 6 * TT * S + 16 * S)
        ctx.enter_context(nc.sbuf_tensor("mix_region", [P, region], F32))
        bank = [ctx.enter_context(nc.psum_tensor(f"bank{b}", [P, 512], F32)) for b in range(8)]

        w_in = [sem(f"w_in{i}") for i in range(RING)]
        w_hi = sem("w_hi")
        w_lo = sem("w_lo")
        w_used = sem("w_used")
        t0_out = sem("t0_out")
        x_in = sem("x_in")
        const_in = sem("const_in")
        gam_in = [sem(f"gam_in{i}") for i in range(2)]
        p_in = sem("p_in")
        p_hi = sem("p_hi")
        p_lo = sem("p_lo")
        rpb_copied = sem("rpb_copied")
        nab_in = sem("nab_in")
        nab_ok = sem("nab_ok")
        ev_in = sem("ev_in")
        t5_in = sem("t5_in")
        t5_row = sem("t5_row")
        t5_sb = sem("t5_sb")
        t5_out = sem("t5_out")
        t5_back = sem("t5_back")
        t5_ok = sem("t5_ok")
        cst_ok = sem("cst_ok")
        ssq = sem("ssq")
        rstd_ok = sem("rstd_ok")
        hn_ok = sem("hn_ok")
        h_ok = sem("h_ok")
        tr_x = sem("tr_x")
        x_hi = sem("x_hi")
        x_lo = sem("x_lo")
        copied = sem("copied")
        v_ok = sem("v_ok")
        conv_a = sem("conv_a")
        conv_ok = sem("conv_ok")
        silu_ok = sem("silu_ok")
        mul_ok = sem("mul_ok")
        hid_hi = sem("hid_hi")
        hid_lo = sem("hid_lo")
        sc_out = sem("sc_out")
        sc_free = sem("sc_free")
        max_ok = sem("max_ok")
        exp_ok = sem("exp_ok")
        prob_ok = sem("prob_ok")
        prob_tr = sem("prob_tr")
        probT_ok = sem("probT_ok")
        pv_out = sem("pv_out")
        o_sb = sem("o_sb")
        o_sq = sem("o_sq")
        o_ss = sem("o_ss")
        o_rstd = sem("o_rstd")
        o_norm = sem("o_norm")
        o_tr = sem("o_tr")
        mix_hi = sem("mix_hi")
        mix_lo = sem("mix_lo")
        lam_sum = sem("lam_sum")
        lam_exp = sem("lam_exp")
        g_out = sem("g_out")
        pool_ok = sem("pool_ok")
        pool_out = sem("pool_out")
        ya_ok = sem("ya_ok")
        f_abs = sem("f_abs")
        f_log = sem("f_log")
        f_min = sem("f_min")
        f_ok = sem("f_ok")
        f_base = sem("f_base")
        store = sem("store")
        a_step = sem("a_step")
        d_step = sem("d_step")
        g_step = sem("g_step")

        rpb_dram = nc.dram_tensor("rpb_scratch", [GRID_W, HEADS * 15 * 31], F32,
                                  kind="Internal").ap()
        t5_dram = nc.dram_tensor("t5_scratch", [P, 8, 384], F32, kind="Internal").ap()

        ident = cst[:, C_ID:C_ID + P]
        dist = cst[:, C_DIST:C_DIST + 512]
        colmask = cst[:, C_COLM:C_COLM + GRID_W]
        causal = cst[:, C_CAUS:C_CAUS + 384]

        def pcol(i):
            return col[:, i:i + 1]

        def slot8(t, c):
            return t[:, c % RING, :].rearrange("p (k n) -> p k n", k=KT)

        def slot2(t, c):
            return t[:, c % RING, :].rearrange("p (k n) -> p k n", k=2)

        def tbank(t, n, proj=False):
            return bank[(0 if proj else 4) + 2 * t + n]

        def chunk_sources(name, i):
            W = w[name]
            if name[:3] == "ffn":
                first, second = W
                r = [m[:, P * i:P * (i + 1)].rearrange("(k p) n -> p k n", p=P)
                     for m in (first, second)]
                return r
            if dict((n, k) for n, k, _ in PLAN)[name] == "F":
                r = W[:, 256 * i:256 * (i + 1)].rearrange("(k p) n -> p k n", p=P)
                return [r[:, 0:4, :], r[:, 4:8, :]]
            r = W[256 * i:256 * (i + 1), :].rearrange("(k p) n -> p k n", p=P)
            return [r[:, 0:1, :], r[:, 1:2, :]]

        block = ctx.enter_context(nc.Block())

        @block.sync
        def _(sp):
            for t in range(TT):
                sp.dma_start(h[:, t, :], w["x"][t * P:(t + 1) * P, :]).then_inc(x_in, 16)
            for name, kind, n in PLAN:
                for i in range(n):
                    c = START[name] + i
                    if c >= RING:
                        sp.wait_ge(w_lo, c - RING + 1)
                    src = chunk_sources(name, i)
                    if name[:3] == "ffn":
                        dst = [slot8(raw, c)[:, :, P * a:P * (a + 1)] for a in range(2)]
                    elif kind == "F":
                        dst = [slot8(raw, c)[:, 4 * a:4 * (a + 1), :] for a in range(2)]
                    else:
                        dst = [slot2(raw, c)[:, a:a + 1, :] for a in range(2)]
                    for a in range(2):
                        sp.dma_start(dst[a], src[a]).then_inc(w_in[c % RING], 16)
            for t in range(TT):
                sp.wait_ge(hn_ok, 2 * XNORM["final"] + t + 1)
                sp.dma_start(out[t * P:(t + 1) * P, :], hn[:, t, :]).then_inc(store, 16)
            sp.wait_ge(store, 16 * TT)

        @block.gpsimd
        def _(gp):
            steps = [0]

            def link(ins):
                steps[0] += 1
                ins.then_inc(g_step, 1)
                gp.wait_ge(g_step, steps[0])

            gp.dma_start(cst[:], consts).then_inc(const_in, 16)
            gp.dma_start(col[:], cols).then_inc(const_in, 16)
            gp.dma_start(lamv[:], w["lam"].partition_broadcast(P)).then_inc(const_in, 16)
            gp.dma_start(vbias[:], w["v_bias"].partition_broadcast(P)).then_inc(const_in, 16)

            def load_gamma(n):
                gp.dma_start(gam[:, n % 2, :], w["gammas"][n].partition_broadcast(P)
                             ).then_inc(gam_in[n % 2], 16)

            def load_p(layer):
                gp.dma_start(praw[:], w["p"][layer].rearrange("(k p) t -> p k t", p=P)
                             ).then_inc(p_in, 16)

            load_gamma(0)
            load_gamma(1)
            load_p(0)
            rows, width = w["rpb"].shape[1:]
            size = HEADS * rows * width
            gp.dma_start(rpb_dram, w["rpb"].rearrange("h r c -> (h r c)").partition_broadcast(GRID_W)
                         ).then_inc(rpb_copied, 16)
            gp.wait_ge(rpb_copied, 16)
            for r in range(2):
                for m in range(6):
                    src = bass.AP(tensor=rpb_dram.tensor, offset=(m - 2 - r + 7) * width + 15,
                                  ap=[[size - 1, GRID_W], [rows * width, HEADS], [1, GRID_W]])
                    gp.dma_start(nab[GRID_W * r:GRID_W * (r + 1), :, GRID_W * m:GRID_W * (m + 1)],
                                 src).then_inc(nab_in, 16)
            link(nc.gpsimd.memset(half[:], -0.5))
            gp.wait_ge(const_in, 64)
            link(nc.gpsimd.tensor_scalar(col[:, COL_BQK:COL_BQK + 8], col[:, COL_BQK:COL_BQK + 8],
                                         0.125, None, ALU.mult))
            nc.gpsimd.tensor_scalar(pcol(COL_SUBLN), pcol(COL_SUBLN), 1.0 - LAM_INIT, None,
                                    ALU.mult).then_inc(cst_ok, 1)

            def rstd(n):
                for t in range(TT):
                    gp.wait_ge(ssq, 2 * n + t + 1)
                    link(nc.gpsimd.tensor_scalar(tiny[:, 2 + t:3 + t], tiny[:, t:t + 1],
                                                 1.0 / D, NORM_EPS, ALU.mult, ALU.add))
                    nc.gpsimd.tensor_tensor(tiny[:, 4 + t:5 + t], tiny[:, 2 + t:3 + t],
                                            half[:, 0:1], ALU.pow).then_inc(rstd_ok, 1)
                if n + 2 < len(NORMS):
                    if NORMS[n] == "mid":
                        gp.wait_ge(h_ok, 4 * n + 4)
                    else:
                        gp.wait_ge(hn_ok, 2 * XNORM[NORMS[n]] + 2)
                    load_gamma(n + 2)

            for layer in range(2):
                rstd(NORM[f"mix{layer}"])
                if layer == 0:
                    for t in range(TT):
                        gp.wait_ge(o_ss, t + 1)
                        link(nc.gpsimd.tensor_scalar(tiny[:, 24 + 8 * t:32 + 8 * t],
                                                     tiny[:, 8 + 8 * t:16 + 8 * t],
                                                     1.0 / P, SUBLN_EPS, ALU.mult, ALU.add))
                        nc.gpsimd.tensor_tensor(tiny[:, 40 + 8 * t:48 + 8 * t],
                                                tiny[:, 24 + 8 * t:32 + 8 * t], half[:, 0:8],
                                                ALU.pow).then_inc(o_rstd, 1)
                    gp.wait_ge(nab_in, 16 * 12)
                    view = nab[:].rearrange("p h (m c) -> p (h m) c", c=GRID_W)
                    mask = colmask.unsqueeze(1).to_broadcast([P, HEADS * 6, GRID_W])
                    nc.gpsimd.tensor_tensor(view, view, mask, ALU.add).then_inc(nab_ok, 1)
                rstd(NORM[f"ffn{layer}"])
                rstd(NORM[f"ple{layer}"])
                if layer == 0:
                    gp.wait_ge(w_used, START["proj0"] + 1)
                    load_p(1)
            rstd(NORM["mid"])
            rstd(NORM["mix2"])
            gp.wait_ge(w_used, START["gate1"] + COUNT["gate1"])
            gp.dma_start(onehot[:], w["onehot"]).then_inc(t5_in, 16)
            gp.dma_start(relb[:], w["rel_bias"]).then_inc(t5_in, 16)
            gp.dma_start(pw[:], w["pool_w"].rearrange("g c d -> c g d")).then_inc(ev_in, 16)
            gp.dma_start(icnt[:], evconst).then_inc(ev_in, 16)
            link(nc.gpsimd.memset(pool[:, :, :, 0:16], 0.0))
            gp.wait_ge(copied, COPY_BASE["ev"] + 8)
            at = 0
            for level in range(4):
                n, to = 1 << level, 2 if at == 1 else 1
                link(nc.gpsimd.tensor_tensor(pool[:, to, level:4, 16:16 + S],
                                             pool[:, at, level:4, 16:16 + S],
                                             pool[:, at, level:4, 16 - n:16 - n + S], ALU.add))
                at = to
            gp.wait_ge(ev_in, 32)
            for g in range(4):
                to = 1 if g % 2 == 0 else 2
                link(nc.gpsimd.tensor_tensor(pool[:, to, g, 16:16 + S], pool[:, to, g, 16:16 + S],
                                             icnt[:, g, :], ALU.mult))
                nc.gpsimd.tensor_tensor(pool[:, to, g, 16:16 + S], pool[:, to, g, 16:16 + S],
                                        pool[:, 0, g, 16:16 + S], ALU.subtract).then_inc(pool_ok, 1)
            gp.wait_ge(t5_sb, 1)
            gp.dma_start(t5_dram.rearrange("q h m -> h q m"),
                         t5row[:].unsqueeze(1).to_broadcast([8, P, 384])).then_inc(t5_out, 16)
            gp.wait_ge(t5_out, 16)
            for lo, n, src in ((0, P, P), (P, S, 0)):
                gp.dma_start(t5b[:, :, lo:lo + n],
                             bass.AP(tensor=t5_dram.tensor, offset=P - 1 + src,
                                     ap=[[8 * 384 - 1, P], [384, 8], [1, n]])).then_inc(t5_back, 16)
            gp.wait_ge(t5_back, 32)
            nc.gpsimd.tensor_tensor(t5b[:], t5b[:], causal.unsqueeze(1).to_broadcast([P, 8, 384]),
                                    ALU.add).then_inc(t5_ok, 1)
            rstd(NORM["ffn2"])
            rstd(NORM["mix3"])
            gp.wait_ge(w_used, START["down2"] + COUNT["down2"])
            nc.gpsimd.tensor_copy(fstat[:], cst[:, C_SEL:C_SEL + 8].unsqueeze(2)
                                  .to_broadcast([P, 8, S])).then_inc(f_base, 1)
            nc.gpsimd.tensor_copy(fmov[:], cst[:, C_SEL + 8:C_SEL + 16].unsqueeze(2)
                                  .to_broadcast([P, 8, S])).then_inc(f_base, 1)
            rstd(NORM["ffn3"])
            rstd(NORM["final"])

        @block.scalar
        def _(ac):
            steps = [0]

            def link(ins):
                steps[0] += 1
                ins.then_inc(a_step, 1)
                ac.wait_ge(a_step, steps[0])

            def split(c):
                if c >= NCHUNKS:
                    return
                ac.wait_ge(w_in[c % RING], 32 * (c // RING + 1))
                if c >= RING:
                    ac.wait_ge(w_used, c - RING + 1)
                nc.scalar.copy(whi[:, c % RING, :], raw[:, c % RING, :]).then_inc(w_hi, 1)

            def split_p(layer):
                ac.wait_ge(p_in, 16 * (layer + 1))
                if layer:
                    ac.wait_ge(w_used, START["proj0"] + 1)
                nc.scalar.copy(phi[:], praw[:]).then_inc(p_hi, 1)

            def norm(name, late):
                n = NORM[name]
                for t in range(TT):
                    if n == 0:
                        ac.wait_ge(x_in, 32)
                    else:
                        ac.wait_ge(h_ok, 4 * (n - 1) + 2 * t + 2)
                    nc.scalar.activation(hn[:, t, :], h[:, t, :], ACT.Square,
                                         accum_out=tiny[:, t:t + 1]).then_inc(ssq, 1)
                for c in late:
                    split(c)
                if name in ("mid", "final"):
                    return
                for t in range(TT):
                    ac.wait_ge(tr_x, 2 * XNORM[name] + t + 1)
                    for i in range(2):
                        nc.scalar.copy(xhi[:, 4 * i:4 * i + 4, t * P:(t + 1) * P],
                                       bank[4 + 2 * t + i][:].rearrange("p (k q) -> p k q", k=4)
                                       ).then_inc(x_hi, 1)

            def copy_out(name, i):
                c = START[name] + i
                src = bank[c % RING]
                ac.wait_ge(w_used, c + 1)
                if name == "qk1":
                    if i == 0:
                        ac.wait_ge(cst_ok, 1)
                    for f in range(2):
                        ins = nc.scalar.activation(qkT[:, 2 * i + f, :], src[:, f * S:(f + 1) * S],
                                                   ACT.Identity, bias=pcol(COL_BQK + 2 * i + f),
                                                   scale=0.125 if i < 4 else 1.0)
                    ins.then_inc(copied, 1)
                elif name == "ev":
                    if i < 6:
                        dst = z[:, 2 * i:2 * i + 2, :]
                    else:
                        dst = pool[:, 0, 2 * i - 12:2 * i - 10, 16:16 + S]
                    ins = nc.scalar.copy(dst, src[:].rearrange("p (f t) -> p f t", f=2))
                    ins.then_inc(copied, 1)
                else:
                    dst = qkT[:, 2 * i:2 * i + 2, :].rearrange("p f t -> p (f t)")
                    nc.scalar.activation(dst, src[:], ACT.Copy, scale=0.125 if i < 4 else 1.0
                                         ).then_inc(copied, 1)

            def t_splits(name, skip=1):
                for i in range(COUNT[name] - skip):
                    split(START[name] + i + RING)

            def attention(a):
                base, units = SC_BASE[a], UNITS

                def exps(u):
                    ac.wait_ge(max_ok, base + u + 1)
                    for t in range(TT):
                        off, n = span(a, t)
                        ins = nc.scalar.activation(prob[:, u % 4, off:off + n],
                                                   prob[:, u % 4, off:off + n], ACT.Exp,
                                                   bias=nmax[:, u, t:t + 1],
                                                   accum_out=sums[:, u, t:t + 1])
                    ins.then_inc(exp_ok, 1)

                def take_T(u):
                    k = TR_BASE[a] + u
                    ac.wait_ge(prob_tr, k + 1)
                    if k >= 2:
                        ac.wait_ge(pv_out, k - 1)
                    n = 512 if a < 2 else 384
                    nc.scalar.copy(probT[:, k % 2, 0:n], bank[4 + k % 2][:, 0:n]
                                   ).then_inc(probT_ok, 1)

                def take_o(j):
                    b = bank[6 + j % 2]
                    if a == 0:
                        ac.wait_ge(pv_out, j + 1)
                        nc.scalar.copy(osb[:, :, j * P:(j + 1) * P],
                                       b[:, 0:S].rearrange("p (t d) -> p t d", t=TT)
                                       ).then_inc(o_sb, 1)
                    else:
                        ac.wait_ge(pv_out, TR_BASE[a] + 2 * j + 2)
                        nc.scalar.copy(xhi[:, j, :], b[:, 0:S]).then_inc(mix_hi, 1)

                if a == 0:
                    for u in range(units + 4):
                        if u < units:
                            exps(u)
                        if u % 2 == 1 and 3 <= u < units + 2:
                            take_T((u - 3) // 2)
                        if u % 2 == 0 and u >= 4:
                            take_o((u - 4) // 2)
                    for t in range(TT):
                        ac.wait_ge(o_sb, PAIRS)
                        nc.scalar.activation(hn[:, t, :], osb[:, t, :], ACT.Square
                                             ).then_inc(o_sq, 1)
                    for t in range(TT):
                        ac.wait_ge(o_tr, t + 1)
                        for i in range(2):
                            nc.scalar.activation(xhi[:, 4 * i:4 * i + 4, t * P:(t + 1) * P],
                                                 bank[4 + 2 * t + i][:].rearrange(
                                                     "p (k q) -> p k q", k=4),
                                                 ACT.Copy, scale=pcol(COL_SUBLN)
                                                 ).then_inc(mix_hi, 1)
                else:
                    for u in range(units + 5):
                        if u < units:
                            exps(u)
                        if 2 <= u < units + 2:
                            take_T(u - 2)
                        if u >= 5 and u % 2 == 1 and (u - 5) // 2 < PAIRS:
                            take_o((u - 5) // 2)

            def ffn(layer):
                name = f"ffn{layer}"
                conv = layer >= 2
                c0, base = START[name], FT * layer

                def hi(j):
                    ac.wait_ge(mul_ok, base + j + 1)
                    nc.scalar.copy(hidhi[:, j, :], mul[:, j % 3, :]).then_inc(hid_hi, 1)

                for j in range(FT):
                    b = bank[(c0 + j) % RING]
                    ac.wait_ge(w_used, c0 + j + 1)
                    if j >= 3:
                        ac.wait_ge(mul_ok, base + j - 2)
                    if conv:
                        o = COL_CONV[layer - 2] + 3 * j
                        nc.scalar.activation(act[:, j % 3, :], b[:, 0:S], ACT.Identity,
                                             bias=pcol(COL_CONVB[layer - 2] + j),
                                             scale=pcol(o + 2)).then_inc(conv_a, 1)
                        if j:
                            hi(j - 1)
                        ac.wait_ge(conv_ok, FT * (layer - 2) + j + 1)
                        nc.scalar.activation(act[:, j % 3, :], act[:, j % 3, :], ACT.Silu
                                             ).then_inc(silu_ok, 1)
                    else:
                        nc.scalar.activation(act[:, j % 3, :], b[:, 0:S], ACT.Silu
                                             ).then_inc(silu_ok, 1)
                        if j:
                            hi(j - 1)
                    split(c0 + j + RING)
                hi(FT - 1)

            for c in range(RING):
                split(c)
            split_p(0)
            ac.wait_ge(lam_sum, 2)
            nc.scalar.activation(tiny[:, 58:60], tiny[:, 56:58], ACT.Exp).then_inc(lam_exp, 1)

            for layer in range(2):
                qk, vn, wo = f"qk{layer}", f"v{layer}", f"wo{layer}"
                if layer == 0:
                    norm("mix0", [])
                for i in range(8):
                    copy_out(qk, i)
                    split(START[qk] + i + RING)
                t_splits(vn, 0)
                attention(layer)
                t_splits(wo)
                norm(f"ffn{layer}", [START[wo] + 3 + RING])
                ffn(layer)
                if layer == 1:
                    split_p(1)
                t_splits(f"down{layer}")
                last = START[f"down{layer}"] + COUNT[f"down{layer}"] - 1
                norm(f"ple{layer}", [last + RING, last + 1 + RING])
                t_splits(f"gate{layer}")
                for t in range(TT):
                    if t == 0:
                        ac.wait_ge(t0_out, TINDEX[f"gate{layer}"] + 1)
                    else:
                        ac.wait_ge(w_used, START[f"gate{layer}"] + 4)
                    for n in range(2):
                        nc.scalar.activation(hn[:, t, n * 512:(n + 1) * 512], tbank(t, n)[:],
                                             ACT.Sigmoid).then_inc(g_out, 1)
                norm("mix1" if layer == 0 else "mid", [START[f"gate{layer}"] + 3 + RING])
            norm("mix2", [])

            for i in range(8):
                copy_out("ev", i)
                split(START["ev"] + i + RING)
            ac.wait_ge(ya_ok, 1)
            nc.scalar.copy(xhi[:, 0:4, :], ya[:]).then_inc(mix_hi, 1)
            ac.wait_ge(pool_out, 4)
            for g in range(4):
                ins = nc.scalar.activation(xhi[:, 4 + g, :], bank[4 + g][:, 0:S], ACT.Copy,
                                           scale=pcol(COL_PSCALE + g))
            ins.then_inc(mix_hi, 1)
            t_splits("evout")
            norm("ffn2", [START["evout"] + 3 + RING])
            ffn(2)
            t_splits("down2")
            norm("mix3", [START["down2"] + FT // 2 - 1 + RING])
            for i in range(8):
                copy_out("qk3", i)
                split(START["qk3"] + i + RING)
            cf = START["f3"]
            ac.wait_ge(w_used, cf + 1)
            fb = bank[cf % RING][:, 0:S]
            link(nc.scalar.activation(osb_f(prob)[0], fb, ACT.Abs, bias=pcol(COL_BF)))
            link(nc.scalar.activation(osb_f(prob)[0], osb_f(prob)[0], ACT.Exp, scale=-1.0))
            nc.scalar.activation(osb_f(prob)[0], osb_f(prob)[0], ACT.Ln, bias=1.0
                                 ).then_inc(f_log, 1)
            split(cf + RING)
            t_splits("v3", 0)
            attention(2)
            t_splits("wo3")
            norm("ffn3", [START["wo3"] + 3 + RING])
            ffn(3)
            t_splits("down3", 0)
            norm("final", [])

        @block.vector
        def _(ve):
            steps = [0]

            def link(ins):
                steps[0] += 1
                ins.then_inc(d_step, 1)
                ve.wait_ge(d_step, steps[0])

            def split(c):
                if c >= NCHUNKS:
                    return
                ve.wait_ge(w_hi, c + 1)
                nc.vector.tensor_tensor(wlo[:, c % RING, :], raw[:, c % RING, :],
                                        whi[:, c % RING, :].bitcast(F32), ALU.subtract
                                        ).then_inc(w_lo, 1)

            def split_p(layer):
                ve.wait_ge(p_hi, layer + 1)
                nc.vector.tensor_tensor(plo[:], praw[:], phi[:].bitcast(F32), ALU.subtract
                                        ).then_inc(p_lo, 1)

            def norm(name, late):
                n = NORM[name]
                for t in range(TT):
                    ve.wait_ge(gam_in[n % 2], 16 * (n // 2 + 1))
                    ve.wait_ge(rstd_ok, 2 * n + t + 1)
                    to = h if name == "mid" else hn
                    ins = nc.vector.scalar_tensor_tensor(out=to[:, t, :], in0=h[:, t, :],
                                                         scalar=tiny[:, 4 + t:5 + t],
                                                         in1=gam[:, n % 2, :], op0=ALU.mult,
                                                         op1=ALU.mult)
                    if name == "mid":
                        ins.then_inc(h_ok, 2)
                    else:
                        ins.then_inc(hn_ok, 1)
                if name not in ("mid", "final"):
                    for t in range(TT):
                        for i in range(2):
                            ve.wait_ge(x_hi, 4 * XNORM[name] + 2 * t + i + 1)
                            lo_of(xlo, xhi, t, i, None).then_inc(x_lo, 1)
                for c in late:
                    split(c)

            def lo_of(lo, hi, t, i, scale):
                src = bank[4 + 2 * t + i][:].rearrange("p (k q) -> p k q", k=4)
                to = lo[:, 4 * i:4 * i + 4, t * P:(t + 1) * P]
                sub = hi[:, 4 * i:4 * i + 4, t * P:(t + 1) * P].bitcast(F32)
                if scale is None:
                    return nc.vector.tensor_tensor(to, src, sub, ALU.subtract)
                return nc.vector.scalar_tensor_tensor(out=to, in0=src, scalar=scale, in1=sub,
                                                      op0=ALU.mult, op1=ALU.subtract)

            def t_ready(name, t):
                if t == 0:
                    ve.wait_ge(t0_out, TINDEX[name] + 1)
                else:
                    ve.wait_ge(w_used, START[name] + COUNT[name])

            def t_splits(name, skip=1):
                for i in range(COUNT[name] - skip):
                    split(START[name] + i + RING)

            def update(name):
                for t in range(TT):
                    t_ready(name, t)
                    for n in range(2):
                        hs = h[:, t, n * 512:(n + 1) * 512]
                        nc.vector.tensor_tensor(hs, tbank(t, n)[:], hs, ALU.add).then_inc(h_ok, 1)

            def take_v(name):
                for t in range(TT):
                    t_ready(name, t)
                    for n in range(2):
                        to = v[:, t, n * 512:(n + 1) * 512]
                        if name == "v1":
                            ins = nc.vector.tensor_tensor(to, tbank(t, n)[:],
                                                          vbias[:, n * 512:(n + 1) * 512], ALU.add)
                        else:
                            ins = nc.vector.tensor_copy(to, tbank(t, n)[:])
                        ins.then_inc(v_ok, 1)

            def attention(a):
                base, units = SC_BASE[a], UNITS

                def bias_max(u):
                    ve.wait_ge(sc_out, base + u + 1)
                    if a == 0:
                        if u >= 4:
                            ve.wait_ge(prob_tr, (u - 4) // 2 + 1)
                    elif u >= 4:
                        ve.wait_ge(prob_tr, TR_BASE[a] + u - 3)
                    b, pr = bank[u % 4], prob[:, u % 4, :]
                    if a == 0:
                        link_free(nc.vector.scalar_tensor_tensor(
                            out=pr, in0=dist, scalar=-(2.0 ** -(u // 2 + 1)), in1=b[:],
                            op0=ALU.mult, op1=ALU.add), base + u)
                    elif a == 1:
                        if u == 0:
                            ve.wait_ge(nab_ok, 1)
                        nc.vector.tensor_tensor(pr[:, 0:S], b[:, 0:S], nab[:, u, P:P + S], ALU.add)
                        link_free(nc.vector.tensor_tensor(pr[:, S:2 * S], b[:, S:2 * S],
                                                          nab[:, u, 0:S], ALU.add), base + u)
                    else:
                        if u == 8:
                            ve.wait_ge(t5_ok, 1)
                        bias = causal if u < 8 else t5b[:, u - 8, :]
                        link_free(nc.vector.tensor_tensor(pr[:, 0:384], b[:, 0:384], bias, ALU.add),
                                  base + u)
                    if a < 2:
                        ins = nc.vector.tensor_reduce(nmax[:, u, :],
                                                      pr.rearrange("p (t k) -> p t k", t=TT),
                                                      X, ALU.max, negate=True)
                    else:
                        for t in range(TT):
                            off, n = span(a, t)
                            ins = nc.vector.tensor_reduce(nmax[:, u, t:t + 1], pr[:, off:off + n],
                                                          X, ALU.max, negate=True)
                    ins.then_inc(max_ok, 1)

                def link_free(ins, k):
                    ins.then_inc(sc_free, 1)
                    ve.wait_ge(sc_free, k + 1)

                def normalise(u):
                    ve.wait_ge(exp_ok, base + u + 1)
                    link(nc.vector.reciprocal(rsum[:, u, :], sums[:, u, :]))
                    if a == 0:
                        if u % 2 == 0:
                            return
                        link(nc.vector.tensor_scalar(rsum[:, u, :], rsum[:, u, :], tiny[:, 60:61],
                                                     None, ALU.mult))
                        for t in range(TT):
                            off, n = span(a, t)
                            p0, p1 = (prob[:, (u - 1 + m) % 4, off:off + n] for m in range(2))
                            link(nc.vector.tensor_scalar(p0, p0, rsum[:, u - 1, t:t + 1], None,
                                                         ALU.mult))
                            ins = nc.vector.scalar_tensor_tensor(
                                out=p0, in0=p1, scalar=rsum[:, u, t:t + 1], in1=p0,
                                op0=ALU.mult, op1=ALU.add)
                    else:
                        for t in range(TT):
                            off, n = span(a, t)
                            pr = prob[:, u % 4, off:off + n]
                            ins = nc.vector.tensor_scalar(pr, pr, rsum[:, u, t:t + 1], None,
                                                          ALU.mult)
                    ins.then_inc(prob_ok, 1)

                def lo_out(j):
                    ve.wait_ge(mix_hi, MIX_BASE["wo1" if a == 1 else "wo3"] + j + 1)
                    nc.vector.tensor_tensor(xlo[:, j, :], bank[6 + j % 2][:, 0:S],
                                            xhi[:, j, :].bitcast(F32), ALU.subtract
                                            ).then_inc(mix_lo, 1)

                if a == 0:
                    ve.wait_ge(lam_exp, 1)
                    link(nc.vector.tensor_tensor(tiny[:, 61:62], tiny[:, 59:60], tiny[:, 58:59],
                                                 ALU.subtract))
                    link(nc.vector.tensor_scalar(tiny[:, 60:61], tiny[:, 61:62], -LAM_INIT, None,
                                                 ALU.add))
                    for u in range(units + 1):
                        if u < units:
                            bias_max(u)
                        if u:
                            normalise(u - 1)
                    for t in range(TT):
                        ve.wait_ge(o_sq, t + 1)
                        nc.vector.tensor_reduce(tiny[:, 8 + 8 * t:16 + 8 * t],
                                                hn[:, t, :].rearrange("p (j d) -> p j d", j=PAIRS),
                                                X, ALU.add).then_inc(o_ss, 1)
                    for t in range(TT):
                        ve.wait_ge(o_rstd, t + 1)
                        ot = osb[:, t, :].rearrange("p (j d) -> p j d", j=PAIRS)
                        r = tiny[:, 40 + 8 * t:48 + 8 * t].unsqueeze(2).to_broadcast([P, PAIRS, P])
                        nc.vector.tensor_tensor(ot, ot, r, ALU.mult).then_inc(o_norm, 1)
                    for t in range(TT):
                        for i in range(2):
                            ve.wait_ge(mix_hi, 2 * t + i + 1)
                            lo_of(xlo, xhi, t, i, pcol(COL_SUBLN)).then_inc(mix_lo, 1)
                else:
                    for u in range(units + 5):
                        if u < units:
                            bias_max(u)
                        if 1 <= u < units + 1:
                            normalise(u - 1)
                        if u >= 5 and u % 2 == 1 and (u - 5) // 2 < PAIRS:
                            lo_out((u - 5) // 2)

            def ffn(layer):
                name = f"ffn{layer}"
                conv = layer >= 2
                c0, base = START[name], FT * layer

                def lo(j):
                    ve.wait_ge(hid_hi, base + j + 1)
                    nc.vector.tensor_tensor(hidlo[:, j, :], mul[:, j % 3, :],
                                            hidhi[:, j, :].bitcast(F32), ALU.subtract
                                            ).then_inc(hid_lo, 1)

                for j in range(FT):
                    b = bank[(c0 + j) % RING]
                    if conv:
                        o = COL_CONV[layer - 2] + 3 * j
                        acc = act[:, j % 3, :]
                        ve.wait_ge(conv_a, FT * (layer - 2) + j + 1)
                        link(nc.vector.scalar_tensor_tensor(
                            out=acc[:, 1:S], in0=b[:, 0:S - 1], scalar=pcol(o + 1),
                            in1=acc[:, 1:S], op0=ALU.mult, op1=ALU.add))
                        nc.vector.scalar_tensor_tensor(
                            out=acc[:, 2:S], in0=b[:, 0:S - 2], scalar=pcol(o),
                            in1=acc[:, 2:S], op0=ALU.mult, op1=ALU.add).then_inc(conv_ok, 1)
                        if j:
                            lo(j - 1)
                    ve.wait_ge(silu_ok, base + j + 1)
                    if j >= 3:
                        ve.wait_ge(hid_lo, base + j - 2)
                    nc.vector.tensor_tensor(mul[:, j % 3, :], act[:, j % 3, :], b[:, S:2 * S],
                                            ALU.mult).then_inc(mul_ok, 1)
                    if j and not conv:
                        lo(j - 1)
                    split(c0 + j + RING)
                lo(FT - 1)

            for c in range(RING):
                split(c)
            split_p(0)
            ve.wait_ge(const_in, 64)
            for i in range(2):
                ins = nc.vector.tensor_tensor_reduce(
                    out=hn[:, 0, i * DH:(i + 1) * DH], in0=lamv[:, 2 * i, :],
                    in1=lamv[:, 2 * i + 1, :], scale=1.0, scalar=0.0, op0=ALU.mult, op1=ALU.add,
                    accum_out=tiny[:, 56 + i:57 + i])
                ins.then_inc(lam_sum, 1)

            for layer in range(2):
                qk, vn, wo = f"qk{layer}", f"v{layer}", f"wo{layer}"
                if layer == 0:
                    norm("mix0", [])
                for i in range(8):
                    split(START[qk] + i + RING)
                t_splits(vn)
                take_v(vn)
                split(START[vn] + 3 + RING)
                attention(layer)
                t_splits(wo)
                update(wo)
                norm(f"ffn{layer}", [START[wo] + 3 + RING])
                ffn(layer)
                if layer == 1:
                    split_p(1)
                t_splits(f"down{layer}")
                update(f"down{layer}")
                last = START[f"down{layer}"] + COUNT[f"down{layer}"] - 1
                norm(f"ple{layer}", [last + RING, last + 1 + RING])
                t_splits(f"gate{layer}")
                for t in range(TT):
                    for n in range(2):
                        ve.wait_ge(g_out, 4 * layer + 2 * t + n + 1)
                        g = hn[:, t, n * 512:(n + 1) * 512]
                        link(nc.vector.tensor_tensor(g, tbank(t, n, True)[:], g, ALU.mult))
                        hs = h[:, t, n * 512:(n + 1) * 512]
                        nc.vector.tensor_tensor(hs, g, hs, ALU.add).then_inc(h_ok, 1)
                norm("mix1" if layer == 0 else "mid", [START[f"gate{layer}"] + 3 + RING])
            norm("mix2", [])

            for i in range(8):
                split(START["ev"] + i + RING)
            ve.wait_ge(copied, COPY_BASE["ev"] + 6)
            link(nc.vector.tensor_tensor(cval[:], z[:, 4:8, :], z[:, 8:12, :], ALU.mult))
            for tap in range(3):
                for i in range(4):
                    wc = pcol(COL_EVCONV + 3 * i + 2 - tap)
                    if tap == 0:
                        ins = nc.vector.tensor_scalar(ya[:, i, :], cval[:, i, :], wc, None,
                                                      ALU.mult)
                    else:
                        ins = nc.vector.scalar_tensor_tensor(
                            out=ya[:, i, tap:S], in0=cval[:, i, 0:S - tap], scalar=wc,
                            in1=ya[:, i, tap:S], op0=ALU.mult, op1=ALU.add)
                    if i == 3:
                        link(ins)
            nc.vector.tensor_tensor(ya[:], ya[:], z[:, 0:4, :], ALU.mult).then_inc(ya_ok, 1)
            ve.wait_ge(t5_row, 1)
            nc.vector.tensor_copy(t5row[:], bank[3][0:8, 0:384]).then_inc(t5_sb, 1)
            ve.wait_ge(mix_hi, MIX_BASE["evout"] + 1)
            nc.vector.tensor_tensor(xlo[:, 0:4, :], ya[:], xhi[:, 0:4, :].bitcast(F32),
                                    ALU.subtract).then_inc(mix_lo, 1)
            ve.wait_ge(mix_hi, MIX_BASE["evout"] + 2)
            for g in range(4):
                ins = nc.vector.scalar_tensor_tensor(
                    out=xlo[:, 4 + g, :], in0=bank[4 + g][:, 0:S], scalar=pcol(COL_PSCALE + g),
                    in1=xhi[:, 4 + g, :].bitcast(F32), op0=ALU.mult, op1=ALU.subtract)
            ins.then_inc(mix_lo, 1)
            t_splits("evout")
            update("evout")
            norm("ffn2", [START["evout"] + 3 + RING])
            ffn(2)
            t_splits("down2")
            update("down2")
            norm("mix3", [START["down2"] + FT // 2 - 1 + RING])
            for i in range(8):
                split(START["qk3"] + i + RING)
            ve.wait_ge(f_log, 1)
            cf = START["f3"]
            lg, mn = osb_f(prob)
            link(nc.vector.tensor_scalar(mn, bank[cf % RING][:, 0:S], pcol(COL_BF), 0.0, ALU.add,
                                         ALU.min))
            link(nc.vector.tensor_tensor(mn, mn, lg, ALU.subtract))
            ones = prob[:, 2, 0:S]
            link(nc.vector.memset(ones, 1.0))
            link(nc.vector.tensor_tensor_scan(lg, ones, mn, 0.0, ALU.mult, ALU.add))
            ve.wait_ge(f_base, 2)
            nc.vector.tensor_copy(fmov[0:8, :, :], lg[0:8, :].unsqueeze(1).to_broadcast([8, 8, S])
                                  ).then_inc(f_ok, 1)
            nc.vector.tensor_copy(fstat[32:40, :, :],
                                  lg[32:40, :].unsqueeze(1).to_broadcast([8, 8, S])
                                  ).then_inc(f_ok, 1)
            split(cf + RING)
            t_splits("v3")
            take_v("v3")
            split(START["v3"] + 3 + RING)
            attention(2)
            t_splits("wo3")
            update("wo3")
            norm("ffn3", [START["wo3"] + 3 + RING])
            ffn(3)
            t_splits("down3", 0)
            update("down3")
            norm("final", [])

        @block.tensor
        def _(pe):
            mm = nc.tensor.matmul

            def norm(name):
                n = XNORM[name]
                for t in range(TT):
                    pe.wait_ge(hn_ok, 2 * n + t + 1)
                    if n == 0:
                        pe.wait_ge(const_in, 64)
                    for k in range(KT):
                        ins = nc.tensor.transpose(bank[4 + 2 * t + k // 4][:, (k % 4) * P:
                                                                          (k % 4 + 1) * P],
                                                  hn[:, t, k * P:(k + 1) * P], ident)
                    ins.then_inc(tr_x, 1)

            def x_ready(name):
                pe.wait_ge(x_lo, 4 * XNORM[name] + 4)

            def f_chunk(name, i, tiles=2):
                c = START[name] + i
                b, hi, lo = bank[c % RING], slot8(whi, c), slot8(wlo, c)
                pe.wait_ge(w_lo, c + 1)
                for f in range(tiles):
                    dst, cs = b[:, f * S:(f + 1) * S], slice(f * P, (f + 1) * P)
                    for k in range(KT):
                        mm(dst, hi[:, k, cs], xhi[:, k, :], start=(k == 0), stop=False)
                        mm(dst, hi[:, k, cs], xlo[:, k, :], start=False, stop=False)
                        ins = mm(dst, lo[:, k, cs], xhi[:, k, :], start=False, stop=(k == KT - 1))
                ins.then_inc(w_used, 1)

            def t_op(name, ah, al, ready=None, proj=False):
                n_chunks = COUNT[name]
                for i in range(n_chunks):
                    c = START[name] + i
                    hi, lo = slot2(whi, c), slot2(wlo, c)
                    if ready:
                        ready(i)
                    pe.wait_ge(w_lo, c + 1)
                    for t in range(TT):
                        for kk in range(2):
                            k = 2 * i + kk
                            first = i == 0 and kk == 0
                            last = i == n_chunks - 1 and kk == 1
                            ts = slice(t * P, (t + 1) * P)
                            for n in range(2):
                                mm(tbank(t, n, proj)[:], ah[:, k, ts],
                                   hi[:, kk, n * 512:(n + 1) * 512], start=first, stop=False)
                            for n in range(2):
                                mm(tbank(t, n, proj)[:], ah[:, k, ts],
                                   lo[:, kk, n * 512:(n + 1) * 512], start=False, stop=False)
                            for n in range(2):
                                ins = mm(tbank(t, n, proj)[:], al[:, k, ts],
                                         hi[:, kk, n * 512:(n + 1) * 512], start=False, stop=last)
                        if t == 0 and i == n_chunks - 1:
                            ins.then_inc(t0_out, 1)
                    ins.then_inc(w_used, 1)

            def f_copied(name):
                for i in range(COUNT[name]):
                    if i >= RING:
                        pe.wait_ge(copied, COPY_BASE[name] + i - RING + 1)
                    f_chunk(name, i)

            def ffn(layer):
                for j in range(FT):
                    if j >= RING:
                        pe.wait_ge(mul_ok, FT * layer + j - RING + 1)
                    f_chunk(f"ffn{layer}", j)

            def down(layer):
                def ready(i):
                    pe.wait_ge(hid_lo, FT * layer + 2 * i + 2)
                t_op(f"down{layer}", hidhi, hidlo, ready)

            def attention(a):
                base, units = SC_BASE[a], UNITS

                def scores(u):
                    j, m = u // 2, u % 2
                    rows = slice(DH * m, DH * (m + 1))
                    if u >= 4:
                        pe.wait_ge(sc_free, base + u - 3)
                    for t in range(TT):
                        off, n = span(a, t)
                        forget = a == 2 and u < 8
                        ts = slice(t * P, (t + 1) * P)
                        dst = bank[u % 4][:, off:off + n]
                        ins = mm(dst, qkT[rows, j, ts], qkT[rows, 8 + j, 0:n], start=True,
                                 stop=not forget)
                        if forget:
                            ins = mm(dst, fstat[:, u, ts], fmov[:, u, 0:n], start=False, stop=True)
                    ins.then_inc(sc_out, 1)

                def transposes(u):
                    k = TR_BASE[a] + u
                    pe.wait_ge(prob_ok, k + 1)
                    if k >= 2:
                        pe.wait_ge(probT_ok, k - 1)
                    src = prob[:, (2 * u if a == 0 else u) % 4, :]
                    for kt in range(TT):
                        for t in range(TT):
                            off, n = span(a, t)
                            if kt * P >= n:
                                continue
                            ins = nc.tensor.transpose(bank[4 + k % 2][:, tcol(a, kt, t):
                                                                      tcol(a, kt, t) + P],
                                                      src[:, off + kt * P:off + (kt + 1) * P],
                                                      ident)
                    ins.then_inc(prob_tr, 1)

                def times_v(u):
                    k = TR_BASE[a] + u
                    pe.wait_ge(probT_ok, k + 1)
                    pt = probT[:, k % 2, :]
                    if a == 0:
                        b = bank[6 + u % 2]
                        if u >= 2:
                            pe.wait_ge(o_sb, u - 1)
                        for t in range(TT):
                            for kt in range(TT):
                                ins = mm(b[:, t * P:(t + 1) * P],
                                         pt[:, tcol(a, kt, t):tcol(a, kt, t) + P],
                                         v[:, kt, u * P:(u + 1) * P], start=(kt == 0),
                                         stop=(kt == TT - 1))
                    else:
                        j, m = u // 2, u % 2
                        b = bank[6 + j % 2]
                        if j >= 2 and m == 0:
                            pe.wait_ge(mix_lo, MIX_BASE["wo1" if a == 1 else "wo3"] + j - 1)
                        rows = slice(DH * m, DH * (m + 1))
                        for kt in range(TT):
                            q0 = P if a == 2 and kt == 1 else 0
                            ins = mm(b[rows, q0:S], v[:, kt, u * DH:(u + 1) * DH],
                                     pt[:, tcol(a, kt, q0 // P):tcol(a, kt, 1) + P],
                                     start=(kt == 0), stop=(kt == TT - 1))
                    ins.then_inc(pv_out, 1)

                pe.wait_ge(v_ok, 4 * (a + 1))
                pe.wait_ge(copied, COPY_BASE[("qk0", "qk1", "qk3")[a]] + 8)
                if a == 2:
                    pe.wait_ge(f_ok, 2)
                if a == 0:
                    for u in range(units + 4):
                        if u < units:
                            scores(u)
                        if u % 2 == 1 and 3 <= u < units + 2:
                            transposes((u - 3) // 2)
                        if u % 2 == 0 and u >= 4:
                            times_v((u - 4) // 2)
                    for t in range(TT):
                        pe.wait_ge(o_norm, t + 1)
                        for k in range(KT):
                            ins = nc.tensor.transpose(
                                bank[4 + 2 * t + k // 4][:, (k % 4) * P:(k % 4 + 1) * P],
                                osb[:, t, k * P:(k + 1) * P], ident)
                        ins.then_inc(o_tr, 1)
                else:
                    for u in range(units + 3):
                        if u < units:
                            scores(u)
                        if 2 <= u < units + 2:
                            transposes(u - 2)
                        if u >= 3:
                            times_v(u - 3)

            def mixed(name):
                pe.wait_ge(mix_lo, MIX_BASE[name] + MIX_COUNT[name])

            for layer in range(2):
                norm(f"mix{layer}")
                x_ready(f"mix{layer}")
                f_copied(f"qk{layer}")
                t_op(f"v{layer}", xhi, xlo)
                attention(layer)
                mixed(f"wo{layer}")
                t_op(f"wo{layer}", xhi, xlo)
                norm(f"ffn{layer}")
                x_ready(f"ffn{layer}")
                ffn(layer)
                down(layer)
                pe.wait_ge(p_lo, layer + 1)
                pe.wait_ge(mul_ok, FT * (layer + 1))
                t_op(f"proj{layer}", phi, plo, proj=True)
                norm(f"ple{layer}")
                x_ready(f"ple{layer}")
                t_op(f"gate{layer}", xhi, xlo)
            norm("mix2")
            x_ready("mix2")
            f_copied("ev")
            pe.wait_ge(t5_in, 32)
            mm(bank[3][0:8, 0:384], relb[:], onehot[:], start=True, stop=True).then_inc(t5_row, 1)
            for g in range(4):
                pe.wait_ge(pool_ok, g + 1)
                if g == 0:
                    pe.wait_ge(ev_in, 32)
                mm(bank[4 + g][:, 0:S], pw[:, g, :], pool[:, 1 if g % 2 == 0 else 2, g, 16:16 + S],
                   start=True, stop=True).then_inc(pool_out, 1)
            mixed("evout")
            t_op("evout", xhi, xlo)
            norm("ffn2")
            x_ready("ffn2")
            ffn(2)
            down(2)
            norm("mix3")
            x_ready("mix3")
            f_copied("qk3")
            pe.wait_ge(copied, COPY_BASE["qk3"] + 6)
            f_chunk("f3", 0, tiles=1)
            t_op("v3", xhi, xlo)
            attention(2)
            mixed("wo3")
            t_op("wo3", xhi, xlo)
            norm("ffn3")
            x_ready("ffn3")
            ffn(3)
            down(3)


def span(a, t):
    return (t * S, S) if a < 2 else ((0, P) if t == 0 else (P, S))


def tcol(a, kt, t):
    return kt * S + t * P if a < 2 or kt == 0 else S


def osb_f(prob):
    return prob[:, 0, 0:S], prob[:, 1, 0:S]


def constants():
    c = np.zeros((P, NCONST), np.float32)
    p = np.arange(P)
    c[:, C_ID:C_ID + P] = np.eye(P)
    k = np.arange(S)
    for t in range(TT):
        c[:, C_DIST + t * S:C_DIST + (t + 1) * S] = np.abs(p[:, None] + t * P - k[None, :])
    cols = np.arange(GRID_W)
    start = np.clip(cols - 8, 0, GRID_W - 16)
    inside = (cols[None, :] >= start[:, None]) & (cols[None, :] < start[:, None] + 16)
    c[:, C_COLM:C_COLM + GRID_W] = np.where(np.tile(inside, (2, 1)), 0.0, MASKED)
    diag = np.where(p[None, :] <= p[:, None], 0.0, MASKED)
    c[:, C_CAUS:C_CAUS + P] = diag
    c[:, C_CAUS + 2 * P:C_CAUS + 3 * P] = diag
    for h in range(8):
        c[h, C_SEL + h] = -1.0
        c[32 + h, C_SEL + 8 + h] = 1.0
    d = np.maximum(255 - np.arange(384), 0)
    log_b = 16 + (np.log(np.maximum(d, 1) / 16.0) / np.log(8.0) * 16 + 1e-9).astype(np.int64)
    bucket = np.where(d < 16, d, np.minimum(log_b, 31))
    onehot = (np.arange(32)[:, None] == bucket[None, :]).astype(np.float32)
    inv = np.stack([1.0 / np.minimum(k + 1, wd) for wd in (2, 4, 8, 16)]).astype(np.float32)
    inv = np.broadcast_to(inv[None], (P, 4, S)).copy()
    return c, onehot, inv


def by_tile(a):
    a = a.reshape(a.shape[0] // P, P, -1)
    return a.transpose(1, 0, 2).reshape(P, -1)


def kernel(**inputs):
    import concourse.bacc as bacc
    from concourse.bass_utils import run_bass_kernel_spmd

    i = {k: np.ascontiguousarray(a) for k, a in inputs.items()}
    c, onehot, inv = constants()
    heads8 = np.zeros((P, 1), np.float32)
    heads8[0:8, 0] = i["od_b_f_2"][0]
    heads8[32:40, 0] = i["od_b_f_2"][0]
    cols = np.concatenate(
        [by_tile(i["na_b_qkv"][0, :2048])]
        + [by_tile(i["ev_conv_w_2"][0].T), by_tile(i["ev_pool_scale_2"][0])]
        + [by_tile(i["ffn_conv_w_2"][l].T) for l in range(2)]
        + [by_tile(i["ffn_conv_b_2"][l]) for l in range(2)]
        + [by_tile(i["da_subln"][0]), heads8], axis=1)
    w_f = np.zeros((D, 256), np.float32)
    w_f[:, 0:8] = i["od_w_in_2"][0, :, 3072:]
    w_f[:, 32:40] = i["od_w_in_2"][0, :, 3072:]
    arrays = {
        "x": i["x"][0],
        "p": i["p"][:, 0].transpose(0, 2, 1),
        "gammas": np.stack([i["norm_mix"][0], i["norm_ffn"][0], i["norm_ple"][0],
                            i["norm_mix"][1], i["norm_ffn"][1], i["norm_ple"][1],
                            i["norm_final"],
                            i["mix_norm_g_2"][0], i["ffn_norm_g_2"][0],
                            i["mix_norm_g_2"][1], i["ffn_norm_g_2"][1], i["final_norm_g_2"]]),
        "lam": np.stack([i[f"da_lambda_{n}"][0] for n in ("q1", "k1", "q2", "k2")]),
        "v_bias": i["na_b_qkv"][0, 2048:],
        "rpb": i["na_rpb"][0],
        "rel_bias": i["rel_bias_2"],
        "pool_w": i["ev_pool_w_2"][0],
        "da_w_qkv": i["da_w_qkv"][0], "da_w_o": i["da_w_o"][0],
        "na_w_qkv": i["na_w_qkv"][0], "na_w_o": i["na_w_o"][0],
        "ffn_w_gate": i["ffn_w_gate"], "ffn_w_up": i["ffn_w_up"], "ffn_w_down": i["ffn_w_down"],
        "ple_w_proj": i["ple_w_proj"], "ple_w_gate": i["ple_w_gate"],
        "ev_w_in": i["ev_w_in_2"][0], "ev_w_out": i["ev_w_out_2"][0],
        "od_w_in": i["od_w_in_2"][0], "od_w_out": i["od_w_out_2"][0], "w_f": w_f,
        "ffn_w_in": i["ffn_w_in_2"], "ffn_w_out": i["ffn_w_out_2"],
        "onehot": onehot, "consts": c, "cols": cols, "evconst": inv,
    }
    nc = bacc.Bacc("TRN2", target_bir_lowering=False, num_devices=1)
    arrays = {k: np.ascontiguousarray(a) for k, a in arrays.items()}
    w = {k: nc.dram_tensor(f"in_{k}", a.shape, mybir.dt.from_np(a.dtype),
                           kind="ExternalInput").ap() for k, a in arrays.items()}
    out = nc.dram_tensor("out", (S, D), F32, kind="ExternalOutput").ap()
    for layer, (qkv, wo) in enumerate((("da_w_qkv", "da_w_o"), ("na_w_qkv", "na_w_o"))):
        w[f"qk{layer}"], w[f"v{layer}"] = w[qkv], w[qkv][:, 2048:3072]
        w[f"wo{layer}"] = w[wo]
        w[f"ffn{layer}"] = (w["ffn_w_gate"][layer], w["ffn_w_up"][layer])
        w[f"down{layer}"] = w["ffn_w_down"][layer]
        w[f"proj{layer}"], w[f"gate{layer}"] = w["ple_w_proj"][layer], w["ple_w_gate"][layer]
    for layer in (2, 3):
        m = w["ffn_w_in"][layer - 2]
        w[f"ffn{layer}"] = (m[:, 0:FFN], m[:, FFN:2 * FFN])
        w[f"down{layer}"] = w["ffn_w_out"][layer - 2]
    w["ev"], w["evout"] = w["ev_w_in"], w["ev_w_out"]
    w["qk3"], w["v3"], w["wo3"] = w["od_w_in"], w["od_w_in"][:, 2048:3072], w["od_w_out"]
    w["f3"] = w["w_f"]
    mixer_kernel(nc, w, None, w["cols"], w["consts"], w["evconst"], out)
    r = run_bass_kernel_spmd(nc, [{f"in_{k}": a for k, a in arrays.items()}], core_ids=[0])
    return r.results[0]["out"].reshape(1, S, D)
```

```python
from contextlib import ExitStack

import numpy as np
import concourse.bass as bass
from concourse import mybir

F32 = mybir.dt.float32
F32R = mybir.dt.float32r
ALU = mybir.AluOpType
ACT = mybir.ActivationFunctionType
X = mybir.AxisListType.X

P = 128
D = 1024
S = 256
KT = D // P
TT = S // P
FFN = 2816
FT = FFN // P
HEADS = 16
PAIRS = HEADS // 2
DH = 64
GRID_W = 64
LAM_INIT = 0.2
MASKED = -1e30

RING = 3
CHUNK = KT * 256
NORM_EPS = 1e-6
SUBLN_EPS = 1e-5

COL_BQK, COL_EVCONV, COL_PSCALE = 0, 16, 28
COL_CONV = (32, 32 + 3 * FT)
COL_CONVB = (32 + 6 * FT, 32 + 7 * FT)
COL_SUBLN = 32 + 8 * FT
COL_BF = COL_SUBLN + 1
NCOLS = COL_BF + 1

C_ID, C_DIST, C_COLM, C_CAUS, C_SEL, NCONST = 0, 128, 640, 704, 1088, 1104


def make_plan():
    plan = []
    for layer in (0, 1):
        plan += [(f"v{layer}", "T", 4), (f"qk{layer}", "F", 8), (f"wo{layer}", "T", 4),
                 (f"ffn{layer}", "F", FT), (f"down{layer}", "T", FT // 2),
                 (f"proj{layer}", "T", 1), (f"gate{layer}", "T", 4)]
    plan += [("ev", "F", 8), ("evout", "T", 4), ("ffn2", "F", FT), ("down2", "T", FT // 2),
             ("f3", "F", 1), ("v3", "T", 4), ("qk3", "F", 8), ("wo3", "T", 4),
             ("ffn3", "F", FT), ("down3", "T", FT // 2)]
    start, tindex, at, t = {}, {}, 0, 0
    for name, kind, n in plan:
        start[name] = at
        at += n
        if kind == "T":
            tindex[name] = t
            t += 1
    return plan, start, tindex, at


PLAN, START, TINDEX, NCHUNKS = make_plan()
COUNT = {name: n for name, _, n in PLAN}

NORMS = ("mix0", "ffn0", "ple0", "mix1", "ffn1", "ple1", "mid", "mix2", "ffn2", "mix3", "ffn3",
         "final")
NORM = {name: n for n, name in enumerate(NORMS)}
XNORM = {name: n for n, name in enumerate(m for m in NORMS if m != "mid")}
UNITS = 2 * PAIRS
SC_BASE = (0, UNITS, 2 * UNITS)
TR_BASE = (0, PAIRS, PAIRS + UNITS)
MIX_BASE = {"wo0": 0, "wo1": 8, "evout": 16, "wo3": 18}
ATTENTIONS = (("qk0", "wo0"), ("qk1", "wo1"), ("qk3", "wo3"))
STEPS = 2 * (8 + 4)
COPY_BASE = {"qk0": 0, "qk1": 8, "ev": 16, "qk3": 24}


def mixer_kernel(nc, w, small, cols, consts, evconst, out):
    with ExitStack() as ctx:
        def sb(name, shape, dt=F32, c=ctx):
            return c.enter_context(nc.sbuf_tensor(name, shape, dt))

        def sem(name):
            return ctx.enter_context(nc.semaphore(name))

        raw = sb("raw", [P, RING, CHUNK])
        whi = sb("whi", [P, RING, CHUNK], F32R)
        wlo = sb("wlo", [P, RING, CHUNK], F32R)
        h = sb("h", [P, TT, D])
        hn = sb("hn", [P, TT, D])
        xhi = sb("xhi", [P, KT, S], F32R)
        xlo = sb("xlo", [P, KT, S], F32R)
        gam = sb("gam", [P, 2, D])
        vbias = sb("vbias", [P, D])
        praw = sb("praw", [P, 2, S])
        phi = sb("phi", [P, 2, S], F32R)
        plo = sb("plo", [P, 2, S], F32R)
        col = sb("col", [P, NCOLS])
        cst = sb("cst", [P, NCONST])
        lamv = sb("lamv", [P, 4, DH])
        tiny = sb("tiny", [P, 64])
        nmax = sb("nmax", [P, UNITS, TT])
        sums = sb("sums", [P, UNITS, TT])
        rsum = sb("rsum", [P, UNITS, TT])
        ostat = sb("ostat", [P, 3, PAIRS, TT])
        half = sb("half", [P, 16])
        with ExitStack() as c:
            nab = sb("nab", [P, HEADS, 6 * GRID_W], F32, c)
        with ExitStack() as c:
            t5b = sb("t5b", [P, 8, 384], F32, c)
            t5row = sb("t5row", [8, 384], F32, c)
            onehot = sb("onehot", [32, 384], F32, c)
            relb = sb("relb", [32, 8], F32, c)
            ol2 = sb("ol2", [P, KT, S], F32R, c)
        ctx.enter_context(nc.sbuf_tensor("bias_region", [P, HEADS * 6 * GRID_W], F32))
        with ExitStack() as c:
            hidhi = sb("hidhi", [P, FT, S], F32R, c)
            hidlo = sb("hidlo", [P, FT, S], F32R, c)
            act = sb("act", [P, 3, S], F32, c)
            mul = sb("mul", [P, 3, S], F32, c)
        with ExitStack() as c:
            qkT = sb("qkT", [P, 16, S], F32, c)
            v = sb("v", [P, TT, D], F32, c)
            prob = sb("prob", [P, 4, TT * S], F32, c)
            probT = sb("probT", [P, 2, TT * S], F32, c)
            with ExitStack() as c2:
                oh01 = sb("oh01", [P, KT, S], F32R, c2)
                ol01 = sb("ol01", [P, KT, S], F32R, c2)
            with ExitStack() as c2:
                oh2 = sb("oh2", [P, KT, S], F32R, c2)
                fstat = sb("fstat", [P, 8, S], F32, c2)
        ohi, olo = (oh01, oh01, oh2), (ol01, ol01, ol2)
        onrm, osq = (hn[:, t, 0:S].rearrange("p (t d) -> p t d", t=TT) for t in range(2))
        fmov = hn[:].rearrange("p t (g s) -> p (t g) s", g=4)
        with ExitStack() as c:
            z = sb("z", [P, 12, S], F32, c)
            pool = sb("pool", [P, 3, 4, 16 + S], F32, c)
            cval = sb("cval", [P, 4, S], F32, c)
            ya = sb("ya", [P, 4, S], F32, c)
            pw = sb("pw", [P, 4, P], F32, c)
            icnt = sb("icnt", [P, 4, S], F32, c)
        region = max(2 * FT * S + 6 * S, 16 * S + TT * D + 6 * TT * S + 16 * S)
        ctx.enter_context(nc.sbuf_tensor("mix_region", [P, region], F32))
        bank = [ctx.enter_context(nc.psum_tensor(f"bank{b}", [P, 512], F32)) for b in range(8)]

        w_in = [sem(f"w_in{i}") for i in range(RING)]
        w_hi = sem("w_hi")
        w_lo = sem("w_lo")
        w_used = sem("w_used")
        t0_out = sem("t0_out")
        x_in = sem("x_in")
        lam_in = sem("lam_in")
        vbias_in = sem("vbias_in")
        const_in = sem("const_in")
        gam_in = [sem(f"gam_in{i}") for i in range(2)]
        p_in = sem("p_in")
        p_hi = sem("p_hi")
        p_lo = sem("p_lo")
        rpb_copied = sem("rpb_copied")
        nab_in = sem("nab_in")
        nab_ok = sem("nab_ok")
        ev_in = sem("ev_in")
        t5_in = sem("t5_in")
        t5_row = sem("t5_row")
        t5_sb = sem("t5_sb")
        t5_out = sem("t5_out")
        t5_back = sem("t5_back")
        t5_ok = sem("t5_ok")
        cst_ok = sem("cst_ok")
        ssq = sem("ssq")
        rstd_ok = sem("rstd_ok")
        hn_ok = sem("hn_ok")
        h_ok = sem("h_ok")
        tr_x = sem("tr_x")
        x_hi = sem("x_hi")
        x_lo = sem("x_lo")
        copied = sem("copied")
        v_ok = sem("v_ok")
        conv_a = sem("conv_a")
        conv_ok = sem("conv_ok")
        silu_ok = sem("silu_ok")
        mul_ok = sem("mul_ok")
        hid_hi = sem("hid_hi")
        hid_lo = sem("hid_lo")
        sc_out = sem("sc_out")
        sc_free = sem("sc_free")
        max_ok = sem("max_ok")
        exp_ok = sem("exp_ok")
        prob_ok = sem("prob_ok")
        prob_tr = sem("prob_tr")
        probT_ok = sem("probT_ok")
        pv_out = sem("pv_out")
        o_sq = sem("o_sq")
        o_rstd = sem("o_rstd")
        o_norm = sem("o_norm")
        o_tr = sem("o_tr")
        mix_hi = sem("mix_hi")
        mix_lo = sem("mix_lo")
        lam_sum = sem("lam_sum")
        lam_exp = sem("lam_exp")
        g_out = sem("g_out")
        pool_ok = sem("pool_ok")
        pool_out = sem("pool_out")
        ya_ok = sem("ya_ok")
        f_abs = sem("f_abs")
        f_log = sem("f_log")
        f_min = sem("f_min")
        f_ok = sem("f_ok")
        f_base = sem("f_base")
        store = sem("store")
        a_step = sem("a_step")
        d_step = sem("d_step")
        g_step = sem("g_step")

        rpb_dram = nc.dram_tensor("rpb_scratch", [GRID_W, HEADS * 15 * 31], F32,
                                  kind="Internal").ap()
        t5_dram = nc.dram_tensor("t5_scratch", [P, 8, 384], F32, kind="Internal").ap()

        ident = cst[:, C_ID:C_ID + P]
        dist = cst[:, C_DIST:C_DIST + 512]
        colmask = cst[:, C_COLM:C_COLM + GRID_W]
        causal = cst[:, C_CAUS:C_CAUS + 384]

        def pcol(i):
            return col[:, i:i + 1]

        def slot8(t, c):
            return t[:, c % RING, :].rearrange("p (k n) -> p k n", k=KT)

        def slot2(t, c):
            return t[:, c % RING, :].rearrange("p (k n) -> p k n", k=2)

        def tbank(t, n, proj=False):
            return bank[(0 if proj else 4) + 2 * t + n]

        def chunk_sources(name, i):
            W = w[name]
            if name[:3] == "ffn":
                first, second = W
                r = [m[:, P * i:P * (i + 1)].rearrange("(k p) n -> p k n", p=P)
                     for m in (first, second)]
                return r
            if dict((n, k) for n, k, _ in PLAN)[name] == "F":
                if name[:2] == "qk":
                    col0 = P * qk_tile(i)
                else:
                    col0 = 256 * (EV_ORDER[i] if name == "ev" else i)
                r = W[:, col0:col0 + 256].rearrange("(k p) n -> p k n", p=P)
                return [r[:, 0:4, :], r[:, 4:8, :]]
            r = W[256 * i:256 * (i + 1), :].rearrange("(k p) n -> p k n", p=P)
            return [r[:, 0:1, :], r[:, 1:2, :]]

        EV_ORDER = (6, 7, 2, 3, 4, 5, 0, 1)

        def qk_tile(i):
            return 8 * (i % 2) + 2 * (i // 2)

        block = ctx.enter_context(nc.Block())

        @block.sync
        def _(sp):
            for t in range(TT):
                sp.dma_start(h[:, t, :], w["x"][t * P:(t + 1) * P, :]).then_inc(x_in, 16)
            for name, kind, n in PLAN:
                for i in range(n):
                    c = START[name] + i
                    if c >= RING:
                        sp.wait_ge(w_lo, c - RING + 1)
                    src = chunk_sources(name, i)
                    if name[:3] == "ffn":
                        dst = [slot8(raw, c)[:, :, P * a:P * (a + 1)] for a in range(2)]
                    elif kind == "F":
                        dst = [slot8(raw, c)[:, 4 * a:4 * (a + 1), :] for a in range(2)]
                    else:
                        dst = [slot2(raw, c)[:, a:a + 1, :] for a in range(2)]
                    for a in range(2):
                        sp.dma_start(dst[a], src[a]).then_inc(w_in[c % RING], 16)
            for t in range(TT):
                sp.wait_ge(hn_ok, 4 * XNORM["final"] + 2 * t + 2)
                sp.dma_start(out[t * P:(t + 1) * P, :], hn[:, t, :]).then_inc(store, 16)
            sp.wait_ge(store, 16 * TT)

        @block.gpsimd
        def _(gp):
            steps = [0]

            def link(ins):
                steps[0] += 1
                ins.then_inc(g_step, 1)
                gp.wait_ge(g_step, steps[0])

            gp.dma_start(cst[:], consts).then_inc(const_in, 16)
            gp.dma_start(col[:], cols).then_inc(const_in, 16)

            def load_gamma(n):
                gp.dma_start(gam[:, n % 2, :], w["gammas"][n].partition_broadcast(P)
                             ).then_inc(gam_in[n % 2], 16)

            def load_p(layer):
                gp.dma_start(praw[:], w["p"][layer].rearrange("(k p) t -> p k t", p=P)
                             ).then_inc(p_in, 16)

            load_gamma(0)
            link(nc.gpsimd.memset(half[:], -0.5))
            gp.wait_ge(const_in, 32)
            link(nc.gpsimd.tensor_scalar(col[:, COL_BQK:COL_BQK + 8], col[:, COL_BQK:COL_BQK + 8],
                                         0.125, None, ALU.mult))
            nc.gpsimd.tensor_scalar(pcol(COL_SUBLN), pcol(COL_SUBLN), 1.0 - LAM_INIT, None,
                                    ALU.mult).then_inc(cst_ok, 1)

            def load_neighbourhood():
                rows, width = w["rpb"].shape[1:]
                size = HEADS * rows * width
                gp.dma_start(rpb_dram, w["rpb"].rearrange("h r c -> (h r c)")
                             .partition_broadcast(GRID_W)).then_inc(rpb_copied, 16)
                gp.wait_ge(rpb_copied, 16)
                for r in range(2):
                    for m in range(6):
                        src = bass.AP(tensor=rpb_dram.tensor, offset=(m - 2 - r + 7) * width + 15,
                                      ap=[[size - 1, GRID_W], [rows * width, HEADS], [1, GRID_W]])
                        gp.dma_start(nab[GRID_W * r:GRID_W * (r + 1), :,
                                         GRID_W * m:GRID_W * (m + 1)], src).then_inc(nab_in, 16)

            def rstd(n):
                for t in range(TT):
                    gp.wait_ge(ssq, 2 * n + t + 1)
                    link(nc.gpsimd.tensor_scalar(tiny[:, 2 + t:3 + t], tiny[:, t:t + 1],
                                                 1.0 / D, NORM_EPS, ALU.mult, ALU.add))
                    nc.gpsimd.tensor_tensor(tiny[:, 4 + t:5 + t], tiny[:, 2 + t:3 + t],
                                            half[:, 0:1], ALU.pow).then_inc(rstd_ok, 1)
                if n + 2 < len(NORMS):
                    if NORMS[n] == "mid":
                        gp.wait_ge(h_ok, 4 * n + 4)
                    else:
                        gp.wait_ge(hn_ok, 4 * XNORM[NORMS[n]] + 4)
                    load_gamma(n + 2)

            for layer in range(2):
                rstd(NORM[f"mix{layer}"])
                if layer == 0:
                    load_gamma(1)
                    gp.dma_start(lamv[:], w["lam"].partition_broadcast(P)).then_inc(lam_in, 16)
                    load_p(0)
                    gp.dma_start(vbias[:], w["v_bias"].partition_broadcast(P)
                                 ).then_inc(vbias_in, 16)
                    load_neighbourhood()
                    for j in range(PAIRS):
                        gp.wait_ge(o_sq, j + 1)
                        link(nc.gpsimd.tensor_scalar(ostat[:, 1, j, :], ostat[:, 0, j, :],
                                                     1.0 / P, SUBLN_EPS, ALU.mult, ALU.add))
                        nc.gpsimd.tensor_tensor(ostat[:, 2, j, :], ostat[:, 1, j, :],
                                                half[:, 0:2], ALU.pow).then_inc(o_rstd, 1)
                    gp.wait_ge(nab_in, 16 * 12)
                    view = nab[:].rearrange("p h (m c) -> p (h m) c", c=GRID_W)
                    mask = colmask.unsqueeze(1).to_broadcast([P, HEADS * 6, GRID_W])
                    nc.gpsimd.tensor_tensor(view, view, mask, ALU.add).then_inc(nab_ok, 1)
                rstd(NORM[f"ffn{layer}"])
                rstd(NORM[f"ple{layer}"])
                if layer == 0:
                    gp.wait_ge(w_used, START["proj0"] + 1)
                    load_p(1)
            rstd(NORM["mid"])
            rstd(NORM["mix2"])
            gp.wait_ge(w_used, START["gate1"] + COUNT["gate1"])
            gp.dma_start(onehot[:], w["onehot"]).then_inc(t5_in, 16)
            gp.dma_start(relb[:], w["rel_bias"]).then_inc(t5_in, 16)
            gp.dma_start(pw[:], w["pool_w"].rearrange("g c d -> c g d")).then_inc(ev_in, 16)
            gp.dma_start(icnt[:], evconst).then_inc(ev_in, 16)
            link(nc.gpsimd.memset(pool[:, :, :, 0:16], 0.0))
            gp.wait_ge(copied, COPY_BASE["ev"] + 2)
            at = 0
            for level in range(4):
                n, to = 1 << level, 2 if at == 1 else 1
                link(nc.gpsimd.tensor_tensor(pool[:, to, level:4, 16:16 + S],
                                             pool[:, at, level:4, 16:16 + S],
                                             pool[:, at, level:4, 16 - n:16 - n + S], ALU.add))
                at = to
            gp.wait_ge(ev_in, 32)
            for g in range(4):
                to = 1 if g % 2 == 0 else 2
                link(nc.gpsimd.tensor_tensor(pool[:, to, g, 16:16 + S], pool[:, to, g, 16:16 + S],
                                             icnt[:, g, :], ALU.mult))
                nc.gpsimd.tensor_tensor(pool[:, to, g, 16:16 + S], pool[:, to, g, 16:16 + S],
                                        pool[:, 0, g, 16:16 + S], ALU.subtract).then_inc(pool_ok, 1)
            gp.wait_ge(t5_sb, 1)
            gp.dma_start(t5_dram.rearrange("q h m -> h q m"),
                         t5row[:].unsqueeze(1).to_broadcast([8, P, 384])).then_inc(t5_out, 16)
            gp.wait_ge(t5_out, 16)
            for lo, n, src in ((0, P, P), (P, S, 0)):
                gp.dma_start(t5b[:, :, lo:lo + n],
                             bass.AP(tensor=t5_dram.tensor, offset=P - 1 + src,
                                     ap=[[8 * 384 - 1, P], [384, 8], [1, n]])).then_inc(t5_back, 16)
            gp.wait_ge(t5_back, 32)
            nc.gpsimd.tensor_tensor(t5b[:], t5b[:], causal.unsqueeze(1).to_broadcast([P, 8, 384]),
                                    ALU.add).then_inc(t5_ok, 1)
            rstd(NORM["ffn2"])
            rstd(NORM["mix3"])
            gp.wait_ge(tr_x, 4 * XNORM["mix3"] + 4)
            nc.gpsimd.tensor_copy(fstat[:], cst[:, C_SEL:C_SEL + 8].unsqueeze(2)
                                  .to_broadcast([P, 8, S])).then_inc(f_base, 1)
            nc.gpsimd.tensor_copy(fmov, cst[:, C_SEL + 8:C_SEL + 16].unsqueeze(2)
                                  .to_broadcast([P, 8, S])).then_inc(f_base, 1)
            rstd(NORM["ffn3"])
            rstd(NORM["final"])

        @block.scalar
        def _(ac):
            steps = [0]

            def link(ins):
                steps[0] += 1
                ins.then_inc(a_step, 1)
                ac.wait_ge(a_step, steps[0])

            def split(c):
                if c >= NCHUNKS:
                    return
                ac.wait_ge(w_in[c % RING], 32 * (c // RING + 1))
                if c >= RING:
                    ac.wait_ge(w_used, c - RING + 1)
                nc.scalar.copy(whi[:, c % RING, :], raw[:, c % RING, :]).then_inc(w_hi, 1)

            def split_p(layer):
                ac.wait_ge(p_in, 16 * (layer + 1))
                if layer:
                    ac.wait_ge(w_used, START["proj0"] + 1)
                nc.scalar.copy(phi[:], praw[:]).then_inc(p_hi, 1)

            def norm(name, late):
                n = NORM[name]
                for t in range(TT):
                    if n == 0:
                        ac.wait_ge(x_in, 32)
                    else:
                        ac.wait_ge(h_ok, 4 * (n - 1) + 2 * t + 2)
                    nc.scalar.activation(hn[:, t, :], h[:, t, :], ACT.Square,
                                         accum_out=tiny[:, t:t + 1]).then_inc(ssq, 1)
                for c in late:
                    split(c)
                if name in ("mid", "final"):
                    return
                for t in range(TT):
                    for i in range(2):
                        ac.wait_ge(tr_x, 4 * XNORM[name] + 2 * t + i + 1)
                        nc.scalar.copy(xhi[:, 4 * i:4 * i + 4, t * P:(t + 1) * P],
                                       bank[4 + 2 * t + i][:].rearrange("p (k q) -> p k q", k=4)
                                       ).then_inc(x_hi, 1)

            def copy_out(name, i):
                c = START[name] + i
                src = bank[c % RING]
                ac.wait_ge(w_used, c + 1)
                if name == "qk1":
                    if i == 0:
                        ac.wait_ge(cst_ok, 1)
                    for f in range(2):
                        to = qk_tile(i) + f
                        ins = nc.scalar.activation(qkT[:, to, :], src[:, f * S:(f + 1) * S],
                                                   ACT.Identity, bias=pcol(COL_BQK + to),
                                                   scale=0.125 if i % 2 == 0 else 1.0)
                    ins.then_inc(copied, 1)
                elif name == "ev":
                    e = EV_ORDER[i]
                    if e < 6:
                        dst = z[:, 2 * e:2 * e + 2, :]
                    else:
                        dst = pool[:, 0, 2 * e - 12:2 * e - 10, 16:16 + S]
                    ins = nc.scalar.copy(dst, src[:].rearrange("p (f t) -> p f t", f=2))
                    ins.then_inc(copied, 1)
                else:
                    dst = qkT[:, qk_tile(i):qk_tile(i) + 2, :].rearrange("p f t -> p (f t)")
                    nc.scalar.activation(dst, src[:], ACT.Copy, scale=0.125 if i % 2 == 0 else 1.0
                                         ).then_inc(copied, 1)

            def t_splits(name, skip=1):
                for i in range(COUNT[name] - skip):
                    split(START[name] + i + RING)

            def attention(a):
                base, units = SC_BASE[a], UNITS

                def exps(u):
                    ac.wait_ge(max_ok, base + u + 1)
                    for t in range(TT):
                        off, n = span(a, t)
                        ins = nc.scalar.activation(prob[:, u % 4, off:off + n],
                                                   prob[:, u % 4, off:off + n], ACT.Exp,
                                                   bias=nmax[:, u, t:t + 1],
                                                   accum_out=sums[:, u, t:t + 1])
                    ins.then_inc(exp_ok, 1)

                def take_T(u):
                    k = TR_BASE[a] + u
                    ac.wait_ge(prob_tr, k + 1)
                    if k >= 2:
                        ac.wait_ge(pv_out, k - 1)
                    n = 512 if a < 2 else 384
                    nc.scalar.copy(probT[:, k % 2, 0:n], bank[6][:, 0:n]).then_inc(probT_ok, 1)

                def square_o(j):
                    ac.wait_ge(pv_out, j + 1)
                    for t in range(TT):
                        ins = nc.scalar.activation(osq[:, t, :], bank[7][:, t * P:(t + 1) * P],
                                                   ACT.Square, accum_out=ostat[:, 0, j, t:t + 1])
                    ins.then_inc(o_sq, 1)

                def take_o(j):
                    if a == 0:
                        if j == 0:
                            ac.wait_ge(cst_ok, 1)
                        ac.wait_ge(o_tr, j + 1)
                        nc.scalar.activation(ohi[a][:, j, :], bank[6][:, 0:S], ACT.Copy,
                                             scale=pcol(COL_SUBLN)).then_inc(mix_hi, 1)
                    else:
                        ac.wait_ge(pv_out, TR_BASE[a] + 2 * j + 2)
                        nc.scalar.copy(ohi[a][:, j, :], bank[7][:, 0:S]).then_inc(mix_hi, 1)

                qk = ATTENTIONS[a][0]
                for s in range(STEPS):
                    u = s - 4
                    if a == 0:
                        if s % 2 == 0 and s >= 8:
                            take_o((s - 8) // 2)
                        if s % 2 == 1 and 7 <= s < 23:
                            take_T((s - 7) // 2)
                    else:
                        if s % 2 == 1 and s >= 7 and (s - 7) // 2 < PAIRS:
                            take_o((s - 7) // 2)
                        if 1 <= u < units + 1:
                            take_T(u - 1)
                    if 0 <= u < units:
                        exps(u)
                    if a == 0 and s % 2 == 1 and 7 <= s < 23:
                        square_o((s - 7) // 2)
                    if s % 2 == 1:
                        if s < 16:
                            copy_out(qk, s // 2)
                        if s < STEPS - 1:
                            split(START[qk] + s // 2 + RING)

            def ffn(layer):
                name = f"ffn{layer}"
                conv = layer >= 2
                c0, base = START[name], FT * layer

                def hi(j):
                    ac.wait_ge(mul_ok, base + j + 1)
                    nc.scalar.copy(hidhi[:, j, :], mul[:, j % 3, :]).then_inc(hid_hi, 1)

                for j in range(FT):
                    b = bank[(c0 + j) % RING]
                    ac.wait_ge(w_used, c0 + j + 1)
                    if j >= 3:
                        ac.wait_ge(mul_ok, base + j - 2)
                    if conv:
                        o = COL_CONV[layer - 2] + 3 * j
                        nc.scalar.activation(act[:, j % 3, :], b[:, 0:S], ACT.Identity,
                                             bias=pcol(COL_CONVB[layer - 2] + j),
                                             scale=pcol(o + 2)).then_inc(conv_a, 1)
                        if j:
                            hi(j - 1)
                        ac.wait_ge(conv_ok, FT * (layer - 2) + j + 1)
                        nc.scalar.activation(act[:, j % 3, :], act[:, j % 3, :], ACT.Silu
                                             ).then_inc(silu_ok, 1)
                    else:
                        nc.scalar.activation(act[:, j % 3, :], b[:, 0:S], ACT.Silu
                                             ).then_inc(silu_ok, 1)
                        if j:
                            hi(j - 1)
                    split(c0 + j + RING)
                hi(FT - 1)

            norm("mix0", list(range(RING)))
            ac.wait_ge(lam_sum, 2)
            nc.scalar.activation(tiny[:, 58:60], tiny[:, 56:58], ACT.Exp).then_inc(lam_exp, 1)
            split_p(0)

            for layer in range(2):
                qk, vn, wo = f"qk{layer}", f"v{layer}", f"wo{layer}"
                t_splits(vn, 0)
                attention(layer)
                norm(f"ffn{layer}", [START[wo] + 3 + RING])
                ffn(layer)
                if layer == 1:
                    split_p(1)
                t_splits(f"down{layer}")
                last = START[f"down{layer}"] + COUNT[f"down{layer}"] - 1
                norm(f"ple{layer}", [last + RING, last + 1 + RING])
                t_splits(f"gate{layer}")
                for t in range(TT):
                    if t == 0:
                        ac.wait_ge(t0_out, TINDEX[f"gate{layer}"] + 1)
                    else:
                        ac.wait_ge(w_used, START[f"gate{layer}"] + 4)
                    for n in range(2):
                        nc.scalar.activation(hn[:, t, n * 512:(n + 1) * 512], tbank(t, n)[:],
                                             ACT.Sigmoid).then_inc(g_out, 1)
                norm("mix1" if layer == 0 else "mid", [START[f"gate{layer}"] + 3 + RING])
            norm("mix2", [])

            for i in range(8):
                copy_out("ev", i)
                split(START["ev"] + i + RING)
            ac.wait_ge(ya_ok, 1)
            nc.scalar.copy(xhi[:, 0:4, :], ya[:]).then_inc(mix_hi, 1)
            ac.wait_ge(pool_out, 4)
            for g in range(4):
                ins = nc.scalar.activation(xhi[:, 4 + g, :], bank[4 + g][:, 0:S], ACT.Copy,
                                           scale=pcol(COL_PSCALE + g))
            ins.then_inc(mix_hi, 1)
            t_splits("evout")
            norm("ffn2", [START["evout"] + 3 + RING])
            ffn(2)
            t_splits("down2")
            norm("mix3", [START["down2"] + FT // 2 - 1 + RING])
            cf = START["f3"]
            split(cf + RING)
            fb = bank[cf % RING][:, 0:S]
            link(nc.scalar.activation(osb_f(prob)[0], fb, ACT.Abs, bias=pcol(COL_BF)))
            link(nc.scalar.activation(osb_f(prob)[0], osb_f(prob)[0], ACT.Exp, scale=-1.0))
            nc.scalar.activation(osb_f(prob)[0], osb_f(prob)[0], ACT.Ln, bias=1.0
                                 ).then_inc(f_log, 1)
            t_splits("v3", 0)
            attention(2)
            norm("ffn3", [START["wo3"] + 3 + RING])
            ffn(3)
            t_splits("down3", 0)
            norm("final", [])

        @block.vector
        def _(ve):
            steps = [0]

            def link(ins):
                steps[0] += 1
                ins.then_inc(d_step, 1)
                ve.wait_ge(d_step, steps[0])

            def split(c):
                if c >= NCHUNKS:
                    return
                ve.wait_ge(w_hi, c + 1)
                nc.vector.tensor_tensor(wlo[:, c % RING, :], raw[:, c % RING, :],
                                        whi[:, c % RING, :].bitcast(F32), ALU.subtract
                                        ).then_inc(w_lo, 1)

            def split_p(layer):
                ve.wait_ge(p_hi, layer + 1)
                nc.vector.tensor_tensor(plo[:], praw[:], phi[:].bitcast(F32), ALU.subtract
                                        ).then_inc(p_lo, 1)

            def norm(name, late, early=()):
                n = NORM[name]
                for t in range(TT):
                    ve.wait_ge(gam_in[n % 2], 16 * (n // 2 + 1))
                    ve.wait_ge(rstd_ok, 2 * n + t + 1)
                    to = h if name == "mid" else hn
                    for i in range(2):
                        half_row = slice(i * 512, (i + 1) * 512)
                        nc.vector.scalar_tensor_tensor(
                            out=to[:, t, half_row], in0=h[:, t, half_row],
                            scalar=tiny[:, 4 + t:5 + t], in1=gam[:, n % 2, half_row],
                            op0=ALU.mult, op1=ALU.mult
                        ).then_inc(h_ok if name == "mid" else hn_ok, 1)
                for c in early:
                    split(c)
                if name not in ("mid", "final"):
                    for t in range(TT):
                        for i in range(2):
                            ve.wait_ge(x_hi, 4 * XNORM[name] + 2 * t + i + 1)
                            lo_of(xlo, xhi, t, i, None).then_inc(x_lo, 1)
                for c in late:
                    split(c)

            def lo_of(lo, hi, t, i, scale):
                src = bank[4 + 2 * t + i][:].rearrange("p (k q) -> p k q", k=4)
                to = lo[:, 4 * i:4 * i + 4, t * P:(t + 1) * P]
                sub = hi[:, 4 * i:4 * i + 4, t * P:(t + 1) * P].bitcast(F32)
                if scale is None:
                    return nc.vector.tensor_tensor(to, src, sub, ALU.subtract)
                return nc.vector.scalar_tensor_tensor(out=to, in0=src, scalar=scale, in1=sub,
                                                      op0=ALU.mult, op1=ALU.subtract)

            def t_ready(name, t):
                if t == 0:
                    ve.wait_ge(t0_out, TINDEX[name] + 1)
                else:
                    ve.wait_ge(w_used, START[name] + COUNT[name])

            def t_splits(name, skip=1):
                for i in range(COUNT[name] - skip):
                    split(START[name] + i + RING)

            def update(name, proj=False):
                for t in range(TT):
                    t_ready(name, t)
                    for n in range(2):
                        hs = h[:, t, n * 512:(n + 1) * 512]
                        nc.vector.tensor_tensor(hs, tbank(t, n, proj)[:], hs, ALU.add
                                                ).then_inc(h_ok, 1)

            def take_v(name):
                for t in range(TT):
                    t_ready(name, t)
                    for n in range(2):
                        to = v[:, t, n * 512:(n + 1) * 512]
                        if name == "v1":
                            ve.wait_ge(vbias_in, 16)
                            ins = nc.vector.tensor_tensor(to, tbank(t, n)[:],
                                                          vbias[:, n * 512:(n + 1) * 512], ALU.add)
                        else:
                            ins = nc.vector.tensor_copy(to, tbank(t, n)[:])
                        ins.then_inc(v_ok, 1)

            def attention(a):
                base, units = SC_BASE[a], UNITS

                def bias_max(u):
                    ve.wait_ge(sc_out, base + u + 1)
                    if a == 0:
                        if u >= 4:
                            ve.wait_ge(prob_tr, (u - 4) // 2 + 1)
                    elif u >= 4:
                        ve.wait_ge(prob_tr, TR_BASE[a] + u - 3)
                    b, pr = bank[4 + u % 2], prob[:, u % 4, :]
                    if a == 0:
                        link_free(nc.vector.scalar_tensor_tensor(
                            out=pr, in0=dist, scalar=-(2.0 ** -(u // 2 + 1)), in1=b[:],
                            op0=ALU.mult, op1=ALU.add), base + u)
                    elif a == 1:
                        if u == 0:
                            ve.wait_ge(nab_ok, 1)
                        nc.vector.tensor_tensor(pr[:, 0:S], b[:, 0:S], nab[:, u, P:P + S], ALU.add)
                        link_free(nc.vector.tensor_tensor(pr[:, S:2 * S], b[:, S:2 * S],
                                                          nab[:, u, 0:S], ALU.add), base + u)
                    else:
                        if u == 8:
                            ve.wait_ge(t5_ok, 1)
                        bias = causal if u < 8 else t5b[:, u - 8, :]
                        link_free(nc.vector.tensor_tensor(pr[:, 0:384], b[:, 0:384], bias, ALU.add),
                                  base + u)
                    if a < 2:
                        ins = nc.vector.tensor_reduce(nmax[:, u, :],
                                                      pr.rearrange("p (t k) -> p t k", t=TT),
                                                      X, ALU.max, negate=True)
                    else:
                        for t in range(TT):
                            off, n = span(a, t)
                            ins = nc.vector.tensor_reduce(nmax[:, u, t:t + 1], pr[:, off:off + n],
                                                          X, ALU.max, negate=True)
                    ins.then_inc(max_ok, 1)

                def link_free(ins, k):
                    ins.then_inc(sc_free, 1)
                    ve.wait_ge(sc_free, k + 1)

                def normalise(u):
                    ve.wait_ge(exp_ok, base + u + 1)
                    link(nc.vector.reciprocal(rsum[:, u, :], sums[:, u, :]))
                    if a == 0:
                        if u % 2 == 0:
                            return
                        link(nc.vector.tensor_scalar(rsum[:, u, :], rsum[:, u, :], tiny[:, 60:61],
                                                     None, ALU.mult))
                        for t in range(TT):
                            off, n = span(a, t)
                            p0, p1 = (prob[:, (u - 1 + m) % 4, off:off + n] for m in range(2))
                            link(nc.vector.tensor_scalar(p0, p0, rsum[:, u - 1, t:t + 1], None,
                                                         ALU.mult))
                            ins = nc.vector.scalar_tensor_tensor(
                                out=p0, in0=p1, scalar=rsum[:, u, t:t + 1], in1=p0,
                                op0=ALU.mult, op1=ALU.add)
                    else:
                        for t in range(TT):
                            off, n = span(a, t)
                            pr = prob[:, u % 4, off:off + n]
                            ins = nc.vector.tensor_scalar(pr, pr, rsum[:, u, t:t + 1], None,
                                                          ALU.mult)
                    ins.then_inc(prob_ok, 1)

                def norm_o(j):
                    ve.wait_ge(o_rstd, j + 1)
                    if j:
                        ve.wait_ge(o_tr, j)
                    for t in range(TT):
                        ins = nc.vector.tensor_scalar(onrm[:, t, :], bank[7][:, t * P:(t + 1) * P],
                                                      ostat[:, 2, j, t:t + 1], None, ALU.mult)
                    ins.then_inc(o_norm, 1)

                def lo_out(j):
                    ve.wait_ge(mix_hi, MIX_BASE[ATTENTIONS[a][1]] + j + 1)
                    if a == 0:
                        ins = nc.vector.scalar_tensor_tensor(
                            out=olo[a][:, j, :], in0=bank[6][:, 0:S], scalar=pcol(COL_SUBLN),
                            in1=ohi[a][:, j, :].bitcast(F32), op0=ALU.mult, op1=ALU.subtract)
                    else:
                        ins = nc.vector.tensor_tensor(olo[a][:, j, :], bank[7][:, 0:S],
                                                      ohi[a][:, j, :].bitcast(F32), ALU.subtract)
                    ins.then_inc(mix_lo, 1)

                if a == 0:
                    ve.wait_ge(lam_exp, 1)
                    link(nc.vector.tensor_tensor(tiny[:, 61:62], tiny[:, 59:60], tiny[:, 58:59],
                                                 ALU.subtract))
                    link(nc.vector.tensor_scalar(tiny[:, 60:61], tiny[:, 61:62], -LAM_INIT, None,
                                                 ALU.add))
                for s in range(STEPS):
                    u = s - 4
                    if a > 0 and s % 2 == 1 and s >= 7 and (s - 7) // 2 < PAIRS:
                        lo_out((s - 7) // 2)
                    if 0 <= u < units:
                        bias_max(u)
                    if a == 0:
                        if s % 2 == 0 and s >= 8:
                            lo_out((s - 8) // 2)
                        if s % 2 == 1 and 7 <= s < 23:
                            norm_o((s - 7) // 2)
                    if s % 2 == 0 and s >= 2:
                        split(START[ATTENTIONS[a][0]] + s // 2 - 1 + RING)
                    if 0 <= u < units:
                        normalise(u)

            def ffn(layer):
                name = f"ffn{layer}"
                conv = layer >= 2
                c0, base = START[name], FT * layer

                def lo(j):
                    ve.wait_ge(hid_hi, base + j + 1)
                    nc.vector.tensor_tensor(hidlo[:, j, :], mul[:, j % 3, :],
                                            hidhi[:, j, :].bitcast(F32), ALU.subtract
                                            ).then_inc(hid_lo, 1)

                for j in range(FT):
                    b = bank[(c0 + j) % RING]
                    if conv:
                        o = COL_CONV[layer - 2] + 3 * j
                        acc = act[:, j % 3, :]
                        ve.wait_ge(conv_a, FT * (layer - 2) + j + 1)
                        link(nc.vector.scalar_tensor_tensor(
                            out=acc[:, 1:S], in0=b[:, 0:S - 1], scalar=pcol(o + 1),
                            in1=acc[:, 1:S], op0=ALU.mult, op1=ALU.add))
                        nc.vector.scalar_tensor_tensor(
                            out=acc[:, 2:S], in0=b[:, 0:S - 2], scalar=pcol(o),
                            in1=acc[:, 2:S], op0=ALU.mult, op1=ALU.add).then_inc(conv_ok, 1)
                        if j:
                            lo(j - 1)
                    ve.wait_ge(silu_ok, base + j + 1)
                    if j >= 3:
                        ve.wait_ge(hid_lo, base + j - 2)
                    nc.vector.tensor_tensor(mul[:, j % 3, :], act[:, j % 3, :], b[:, S:2 * S],
                                            ALU.mult).then_inc(mul_ok, 1)
                    if j and not conv:
                        lo(j - 1)
                    split(c0 + j + RING)
                lo(FT - 1)

            norm("mix0", [1, 2], early=[0])
            ve.wait_ge(lam_in, 16)
            for i in range(2):
                ins = nc.vector.tensor_tensor_reduce(
                    out=onrm[:, 0, i * DH:(i + 1) * DH], in0=lamv[:, 2 * i, :],
                    in1=lamv[:, 2 * i + 1, :], scale=1.0, scalar=0.0, op0=ALU.mult, op1=ALU.add,
                    accum_out=tiny[:, 56 + i:57 + i])
                ins.then_inc(lam_sum, 1)
            split_p(0)

            for layer in range(2):
                qk, vn, wo = f"qk{layer}", f"v{layer}", f"wo{layer}"
                t_splits(vn)
                take_v(vn)
                split(START[vn] + 3 + RING)
                attention(layer)
                update(wo, proj=True)
                norm(f"ffn{layer}", [START[wo] + 3 + RING])
                ffn(layer)
                if layer == 1:
                    split_p(1)
                t_splits(f"down{layer}")
                update(f"down{layer}")
                last = START[f"down{layer}"] + COUNT[f"down{layer}"] - 1
                norm(f"ple{layer}", [last + RING, last + 1 + RING])
                t_splits(f"gate{layer}")
                for t in range(TT):
                    for n in range(2):
                        ve.wait_ge(g_out, 4 * layer + 2 * t + n + 1)
                        g = hn[:, t, n * 512:(n + 1) * 512]
                        link(nc.vector.tensor_tensor(g, tbank(t, n, True)[:], g, ALU.mult))
                        hs = h[:, t, n * 512:(n + 1) * 512]
                        nc.vector.tensor_tensor(hs, g, hs, ALU.add).then_inc(h_ok, 1)
                norm("mix1" if layer == 0 else "mid", [START[f"gate{layer}"] + 3 + RING])
            norm("mix2", [])

            for i in range(6):
                split(START["ev"] + i + RING)
            ve.wait_ge(copied, COPY_BASE["ev"] + 6)
            link(nc.vector.tensor_tensor(cval[:], z[:, 4:8, :], z[:, 8:12, :], ALU.mult))
            for tap in range(3):
                for i in range(4):
                    wc = pcol(COL_EVCONV + 3 * i + 2 - tap)
                    if tap == 0:
                        ins = nc.vector.tensor_scalar(ya[:, i, :], cval[:, i, :], wc, None,
                                                      ALU.mult)
                    else:
                        ins = nc.vector.scalar_tensor_tensor(
                            out=ya[:, i, tap:S], in0=cval[:, i, 0:S - tap], scalar=wc,
                            in1=ya[:, i, tap:S], op0=ALU.mult, op1=ALU.add)
                    if i == 3:
                        link(ins)
            for i in (6, 7):
                split(START["ev"] + i + RING)
            ve.wait_ge(copied, COPY_BASE["ev"] + 8)
            nc.vector.tensor_tensor(ya[:], ya[:], z[:, 0:4, :], ALU.mult).then_inc(ya_ok, 1)
            ve.wait_ge(t5_row, 1)
            nc.vector.tensor_copy(t5row[:], bank[3][0:8, 0:384]).then_inc(t5_sb, 1)
            ve.wait_ge(mix_hi, MIX_BASE["evout"] + 1)
            nc.vector.tensor_tensor(xlo[:, 0:4, :], ya[:], xhi[:, 0:4, :].bitcast(F32),
                                    ALU.subtract).then_inc(mix_lo, 1)
            ve.wait_ge(mix_hi, MIX_BASE["evout"] + 2)
            for g in range(4):
                ins = nc.vector.scalar_tensor_tensor(
                    out=xlo[:, 4 + g, :], in0=bank[4 + g][:, 0:S], scalar=pcol(COL_PSCALE + g),
                    in1=xhi[:, 4 + g, :].bitcast(F32), op0=ALU.mult, op1=ALU.subtract)
            ins.then_inc(mix_lo, 1)
            t_splits("evout")
            update("evout")
            norm("ffn2", [START["evout"] + 3 + RING])
            ffn(2)
            t_splits("down2")
            update("down2")
            norm("mix3", [START["down2"] + FT // 2 - 1 + RING])
            cf = START["f3"]
            split(cf + RING)
            ve.wait_ge(f_log, 1)
            lg, mn = osb_f(prob)
            link(nc.vector.tensor_scalar(mn, bank[cf % RING][:, 0:S], pcol(COL_BF), 0.0, ALU.add,
                                         ALU.min))
            link(nc.vector.tensor_tensor(mn, mn, lg, ALU.subtract))
            ones = prob[:, 2, 0:S]
            link(nc.vector.memset(ones, 1.0))
            link(nc.vector.tensor_tensor_scan(lg, ones, mn, 0.0, ALU.mult, ALU.add))
            ve.wait_ge(f_base, 2)
            nc.vector.tensor_copy(fmov[0:8, :, :], lg[0:8, :].unsqueeze(1).to_broadcast([8, 8, S])
                                  ).then_inc(f_ok, 1)
            nc.vector.tensor_copy(fstat[32:40, :, :],
                                  lg[32:40, :].unsqueeze(1).to_broadcast([8, 8, S])
                                  ).then_inc(f_ok, 1)
            t_splits("v3")
            take_v("v3")
            split(START["v3"] + 3 + RING)
            attention(2)
            update("wo3", proj=True)
            norm("ffn3", [START["wo3"] + 3 + RING])
            ffn(3)
            t_splits("down3", 0)
            update("down3")
            norm("final", [])

        @block.tensor
        def _(pe):
            mm = nc.tensor.matmul

            def norm(name):
                n = XNORM[name]
                for t in range(TT):
                    if n == 0:
                        pe.wait_ge(const_in, 32)
                    for i in range(2):
                        pe.wait_ge(hn_ok, 4 * n + 2 * t + i + 1)
                        for k in range(4 * i, 4 * i + 4):
                            ins = nc.tensor.transpose(
                                bank[4 + 2 * t + i][:, (k % 4) * P:(k % 4 + 1) * P],
                                hn[:, t, k * P:(k + 1) * P], ident)
                        ins.then_inc(tr_x, 1)

            def x_ready(name, t, i):
                pe.wait_ge(x_lo, 4 * XNORM[name] + 2 * t + i + 1)

            def f_tile(name, i, f, last, norm_name=None):
                c = START[name] + i
                hi, lo = slot8(whi, c), slot8(wlo, c)
                pe.wait_ge(w_lo, c + 1)
                dst, cs = bank[c % RING][:, f * S:(f + 1) * S], slice(f * P, (f + 1) * P)
                for k in range(KT):
                    if norm_name and k % 4 == 0:
                        x_ready(norm_name, 1, k // 4)
                    mm(dst, hi[:, k, cs], xhi[:, k, :], start=(k == 0), stop=False)
                    mm(dst, hi[:, k, cs], xlo[:, k, :], start=False, stop=False)
                    ins = mm(dst, lo[:, k, cs], xhi[:, k, :], start=False, stop=(k == KT - 1))
                if last:
                    ins.then_inc(w_used, 1)

            def f_chunk(name, i, norm_name=None):
                for f in range(2):
                    f_tile(name, i, f, f == 1, norm_name if f == 0 else None)

            def t_piece(name, i, t, ah, al, proj=False):
                c, n_chunks = START[name] + i, COUNT[name]
                hi, lo = slot2(whi, c), slot2(wlo, c)
                pe.wait_ge(w_lo, c + 1)
                ts = slice(t * P, (t + 1) * P)
                for kk in range(2):
                    k = 2 * i + kk
                    first, last = i == 0 and kk == 0, i == n_chunks - 1 and kk == 1
                    for n in range(2):
                        mm(tbank(t, n, proj)[:], ah[:, k, ts], hi[:, kk, n * 512:(n + 1) * 512],
                           start=first, stop=False)
                    for n in range(2):
                        mm(tbank(t, n, proj)[:], ah[:, k, ts], lo[:, kk, n * 512:(n + 1) * 512],
                           start=False, stop=False)
                    for n in range(2):
                        ins = mm(tbank(t, n, proj)[:], al[:, k, ts],
                                 hi[:, kk, n * 512:(n + 1) * 512], start=False, stop=last)
                if t == TT - 1:
                    ins.then_inc(w_used, 1)
                elif i == n_chunks - 1:
                    ins.then_inc(t0_out, 1)

            def t_op(name, ah, al, ready=None, proj=False):
                for i in range(COUNT[name]):
                    if ready:
                        ready(i)
                    for t in range(TT):
                        t_piece(name, i, t, ah, al, proj)

            def t_op_normed(name, norm_name):
                for i in range(0, COUNT[name], 2):
                    for t in range(TT):
                        for k in range(2):
                            x_ready(norm_name, t, 1)
                            t_piece(name, i + k, t, xhi, xlo)

            def f_copied(name, norm_name):
                for i in range(COUNT[name]):
                    if i >= RING:
                        pe.wait_ge(copied, COPY_BASE[name] + i - RING + 1)
                    f_chunk(name, i, norm_name if i == 0 else None)

            def ffn(layer, norm_name):
                for j in range(FT):
                    if j >= RING:
                        pe.wait_ge(mul_ok, FT * layer + j - RING + 1)
                    f_chunk(f"ffn{layer}", j, norm_name if j == 0 else None)

            def down(layer):
                def ready(i):
                    pe.wait_ge(hid_lo, FT * layer + 2 * i + 2)
                t_op(f"down{layer}", hidhi, hidlo, ready)

            def attention(a):
                base, units = SC_BASE[a], UNITS
                qk, wo = ATTENTIONS[a]

                def scores(u):
                    j, m = u // 2, u % 2
                    rows = slice(DH * m, DH * (m + 1))
                    if u % 4 == 0:
                        pe.wait_ge(copied, COPY_BASE[qk] + 2 * (u // 4) + 2)
                    if u >= 2:
                        pe.wait_ge(sc_free, base + u - 1)
                    for t in range(TT):
                        off, n = span(a, t)
                        forget = a == 2 and u < 8
                        ts = slice(t * P, (t + 1) * P)
                        dst = bank[4 + u % 2][:, off:off + n]
                        ins = mm(dst, qkT[rows, j, ts], qkT[rows, 8 + j, 0:n], start=True,
                                 stop=not forget)
                        if forget:
                            ins = mm(dst, fstat[:, u, ts], fmov[:, u, 0:n], start=False, stop=True)
                    ins.then_inc(sc_out, 1)

                def transposes(u):
                    k = TR_BASE[a] + u
                    pe.wait_ge(prob_ok, k + 1)
                    if k >= 1:
                        pe.wait_ge(probT_ok, k)
                    if a == 0 and u >= 1:
                        pe.wait_ge(mix_lo, u)
                    src = prob[:, (2 * u if a == 0 else u) % 4, :]
                    for kt in range(TT):
                        for t in range(TT):
                            off, n = span(a, t)
                            if kt * P >= n:
                                continue
                            ins = nc.tensor.transpose(bank[6][:, tcol(a, kt, t):
                                                              tcol(a, kt, t) + P],
                                                      src[:, off + kt * P:off + (kt + 1) * P],
                                                      ident)
                    ins.then_inc(prob_tr, 1)

                def times_v(u):
                    k = TR_BASE[a] + u
                    pe.wait_ge(probT_ok, k + 1)
                    pt, b = probT[:, k % 2, :], bank[7]
                    if a == 0:
                        if u:
                            pe.wait_ge(o_norm, u)
                        for t in range(TT):
                            for kt in range(TT):
                                ins = mm(b[:, t * P:(t + 1) * P],
                                         pt[:, tcol(a, kt, t):tcol(a, kt, t) + P],
                                         v[:, kt, u * P:(u + 1) * P], start=(kt == 0),
                                         stop=(kt == TT - 1))
                    else:
                        j, m = u // 2, u % 2
                        if j and m == 0:
                            pe.wait_ge(mix_lo, MIX_BASE[wo] + j)
                        rows = slice(DH * m, DH * (m + 1))
                        for kt in range(TT):
                            q0 = P if a == 2 and kt == 1 else 0
                            ins = mm(b[rows, q0:S], v[:, kt, u * DH:(u + 1) * DH],
                                     pt[:, tcol(a, kt, q0 // P):tcol(a, kt, 1) + P],
                                     start=(kt == 0), stop=(kt == TT - 1))
                    ins.then_inc(pv_out, 1)

                def o_transposes(j):
                    pe.wait_ge(o_norm, j + 1)
                    pe.wait_ge(probT_ok, j + 1)
                    for t in range(TT):
                        ins = nc.tensor.transpose(bank[6][:, t * P:(t + 1) * P], onrm[:, t, :],
                                                  ident)
                    ins.then_inc(o_tr, 1)

                for s in range(STEPS):
                    u = s - 4
                    if s == 4:
                        pe.wait_ge(v_ok, 4 * (a + 1))
                        if a == 2:
                            pe.wait_ge(f_ok, 2)
                    if 0 <= u < units:
                        scores(u)
                    if a == 0:
                        if s % 2 == 0 and s >= 8:
                            o_transposes((s - 8) // 2)
                        if s % 2 == 1 and 7 <= s < 23:
                            times_v((s - 7) // 2)
                    elif 1 <= u < units + 1:
                        transposes(u - 1)
                    if s < 16:
                        if s % 2 == 0 and s // 2 >= RING:
                            pe.wait_ge(copied, COPY_BASE[qk] + s // 2 - RING + 1)
                        f_tile(qk, s // 2, s % 2, s % 2 == 1)
                    else:
                        i = (s - 16) // 2
                        if s == 16:
                            pe.wait_ge(copied, COPY_BASE[qk] + 8)
                        pe.wait_ge(mix_lo, MIX_BASE[wo] + 2 * i + 2)
                        t_piece(wo, i, s % 2, ohi[a], olo[a], proj=True)
                    if a == 0:
                        if s % 2 == 0 and 6 <= s < 22:
                            transposes((s - 6) // 2)
                    elif 1 <= u < units + 1:
                        times_v(u - 1)

            for layer in range(2):
                norm(f"mix{layer}")
                t_op_normed(f"v{layer}", f"mix{layer}")
                attention(layer)
                norm(f"ffn{layer}")
                ffn(layer, f"ffn{layer}")
                down(layer)
                pe.wait_ge(p_lo, layer + 1)
                pe.wait_ge(mul_ok, FT * (layer + 1))
                t_op(f"proj{layer}", phi, plo, proj=True)
                norm(f"ple{layer}")
                t_op_normed(f"gate{layer}", f"ple{layer}")
            norm("mix2")
            f_copied("ev", "mix2")
            pe.wait_ge(t5_in, 32)
            mm(bank[3][0:8, 0:384], relb[:], onehot[:], start=True, stop=True).then_inc(t5_row, 1)
            for g in range(4):
                pe.wait_ge(pool_ok, g + 1)
                if g == 0:
                    pe.wait_ge(ev_in, 32)
                mm(bank[4 + g][:, 0:S], pw[:, g, :], pool[:, 1 if g % 2 == 0 else 2, g, 16:16 + S],
                   start=True, stop=True).then_inc(pool_out, 1)
            pe.wait_ge(mix_lo, MIX_BASE["evout"] + 2)
            t_op("evout", xhi, xlo)
            norm("ffn2")
            ffn(2, "ffn2")
            down(2)
            norm("mix3")
            x_ready("mix3", 1, 0)
            f_tile("f3", 0, 0, True, "mix3")
            t_op_normed("v3", "mix3")
            pe.wait_ge(f_ok, 2)
            attention(2)
            norm("ffn3")
            ffn(3, "ffn3")
            down(3)


def span(a, t):
    return (t * S, S) if a < 2 else ((0, P) if t == 0 else (P, S))


def tcol(a, kt, t):
    return kt * S + t * P if a < 2 or kt == 0 else S


def osb_f(prob):
    return prob[:, 0, 0:S], prob[:, 1, 0:S]


def constants():
    c = np.zeros((P, NCONST), np.float32)
    p = np.arange(P)
    c[:, C_ID:C_ID + P] = np.eye(P)
    k = np.arange(S)
    for t in range(TT):
        c[:, C_DIST + t * S:C_DIST + (t + 1) * S] = np.abs(p[:, None] + t * P - k[None, :])
    cols = np.arange(GRID_W)
    start = np.clip(cols - 8, 0, GRID_W - 16)
    inside = (cols[None, :] >= start[:, None]) & (cols[None, :] < start[:, None] + 16)
    c[:, C_COLM:C_COLM + GRID_W] = np.where(np.tile(inside, (2, 1)), 0.0, MASKED)
    diag = np.where(p[None, :] <= p[:, None], 0.0, MASKED)
    c[:, C_CAUS:C_CAUS + P] = diag
    c[:, C_CAUS + 2 * P:C_CAUS + 3 * P] = diag
    for h in range(8):
        c[h, C_SEL + h] = -1.0
        c[32 + h, C_SEL + 8 + h] = 1.0
    d = np.maximum(255 - np.arange(384), 0)
    log_b = 16 + (np.log(np.maximum(d, 1) / 16.0) / np.log(8.0) * 16 + 1e-9).astype(np.int64)
    bucket = np.where(d < 16, d, np.minimum(log_b, 31))
    onehot = (np.arange(32)[:, None] == bucket[None, :]).astype(np.float32)
    inv = np.stack([1.0 / np.minimum(k + 1, wd) for wd in (2, 4, 8, 16)]).astype(np.float32)
    inv = np.broadcast_to(inv[None], (P, 4, S)).copy()
    return c, onehot, inv


def by_tile(a):
    a = a.reshape(a.shape[0] // P, P, -1)
    return a.transpose(1, 0, 2).reshape(P, -1)


def kernel(**inputs):
    import concourse.bacc as bacc
    from concourse.bass_utils import run_bass_kernel_spmd

    i = {k: np.ascontiguousarray(a) for k, a in inputs.items()}
    c, onehot, inv = constants()
    heads8 = np.zeros((P, 1), np.float32)
    heads8[0:8, 0] = i["od_b_f_2"][0]
    heads8[32:40, 0] = i["od_b_f_2"][0]
    cols = np.concatenate(
        [by_tile(i["na_b_qkv"][0, :2048])]
        + [by_tile(i["ev_conv_w_2"][0].T), by_tile(i["ev_pool_scale_2"][0])]
        + [by_tile(i["ffn_conv_w_2"][l].T) for l in range(2)]
        + [by_tile(i["ffn_conv_b_2"][l]) for l in range(2)]
        + [by_tile(i["da_subln"][0]), heads8], axis=1)
    w_f = np.zeros((D, 256), np.float32)
    w_f[:, 0:8] = i["od_w_in_2"][0, :, 3072:]
    w_f[:, 32:40] = i["od_w_in_2"][0, :, 3072:]
    arrays = {
        "x": i["x"][0],
        "p": i["p"][:, 0].transpose(0, 2, 1),
        "gammas": np.stack([i["norm_mix"][0], i["norm_ffn"][0], i["norm_ple"][0],
                            i["norm_mix"][1], i["norm_ffn"][1], i["norm_ple"][1],
                            i["norm_final"],
                            i["mix_norm_g_2"][0], i["ffn_norm_g_2"][0],
                            i["mix_norm_g_2"][1], i["ffn_norm_g_2"][1], i["final_norm_g_2"]]),
        "lam": np.stack([i[f"da_lambda_{n}"][0] for n in ("q1", "k1", "q2", "k2")]),
        "v_bias": i["na_b_qkv"][0, 2048:],
        "rpb": i["na_rpb"][0],
        "rel_bias": i["rel_bias_2"],
        "pool_w": i["ev_pool_w_2"][0],
        "da_w_qkv": i["da_w_qkv"][0], "da_w_o": i["da_w_o"][0],
        "na_w_qkv": i["na_w_qkv"][0], "na_w_o": i["na_w_o"][0],
        "ffn_w_gate": i["ffn_w_gate"], "ffn_w_up": i["ffn_w_up"], "ffn_w_down": i["ffn_w_down"],
        "ple_w_proj": i["ple_w_proj"], "ple_w_gate": i["ple_w_gate"],
        "ev_w_in": i["ev_w_in_2"][0], "ev_w_out": i["ev_w_out_2"][0],
        "od_w_in": i["od_w_in_2"][0], "od_w_out": i["od_w_out_2"][0], "w_f": w_f,
        "ffn_w_in": i["ffn_w_in_2"], "ffn_w_out": i["ffn_w_out_2"],
        "onehot": onehot, "consts": c, "cols": cols, "evconst": inv,
    }
    nc = bacc.Bacc("TRN2", target_bir_lowering=False, num_devices=1)
    arrays = {k: np.ascontiguousarray(a) for k, a in arrays.items()}
    w = {k: nc.dram_tensor(f"in_{k}", a.shape, mybir.dt.from_np(a.dtype),
                           kind="ExternalInput").ap() for k, a in arrays.items()}
    out = nc.dram_tensor("out", (S, D), F32, kind="ExternalOutput").ap()
    for layer, (qkv, wo) in enumerate((("da_w_qkv", "da_w_o"), ("na_w_qkv", "na_w_o"))):
        w[f"qk{layer}"], w[f"v{layer}"] = w[qkv], w[qkv][:, 2048:3072]
        w[f"wo{layer}"] = w[wo]
        w[f"ffn{layer}"] = (w["ffn_w_gate"][layer], w["ffn_w_up"][layer])
        w[f"down{layer}"] = w["ffn_w_down"][layer]
        w[f"proj{layer}"], w[f"gate{layer}"] = w["ple_w_proj"][layer], w["ple_w_gate"][layer]
    for layer in (2, 3):
        m = w["ffn_w_in"][layer - 2]
        w[f"ffn{layer}"] = (m[:, 0:FFN], m[:, FFN:2 * FFN])
        w[f"down{layer}"] = w["ffn_w_out"][layer - 2]
    w["ev"], w["evout"] = w["ev_w_in"], w["ev_w_out"]
    w["qk3"], w["v3"], w["wo3"] = w["od_w_in"], w["od_w_in"][:, 2048:3072], w["od_w_out"]
    w["f3"] = w["w_f"]
    mixer_kernel(nc, w, None, w["cols"], w["consts"], w["evconst"], out)
    r = run_bass_kernel_spmd(nc, [{f"in_{k}": a for k, a in arrays.items()}], core_ids=[0])
    return r.results[0]["out"].reshape(1, S, D)
```

```python
from contextlib import ExitStack

import numpy as np
import concourse.bass as bass
from concourse import mybir

F32 = mybir.dt.float32
F32R = mybir.dt.float32r
ALU = mybir.AluOpType
ACT = mybir.ActivationFunctionType
X = mybir.AxisListType.X

P = 128
D = 1024
S = 256
KT = D // P
TT = S // P
FFN = 2816
FT = FFN // P
HEADS = 16
PAIRS = HEADS // 2
DH = 64
GRID_W = 64
LAM_INIT = 0.2
MASKED = -1e30

RING = 3
CHUNK = KT * 256
NORM_EPS = 1e-6
SUBLN_EPS = 1e-5

COL_BQK, COL_EVCONV, COL_PSCALE = 0, 16, 28
COL_CONV = (32, 32 + 3 * FT)
COL_CONVB = (32 + 6 * FT, 32 + 7 * FT)
COL_SUBLN = 32 + 8 * FT
COL_BF = COL_SUBLN + 1
NCOLS = COL_BF + 1

C_ID, C_DIST, C_COLM, C_CAUS, C_SEL, NCONST = 0, 128, 640, 704, 1088, 1104


def make_plan():
    plan = []
    for layer in (0, 1):
        plan += [(f"v{layer}", "T", 4), (f"qk{layer}", "F", 8), (f"wo{layer}", "T", 4),
                 (f"ffn{layer}", "F", FT), (f"down{layer}", "T", FT // 2),
                 (f"proj{layer}", "T", 1), (f"gate{layer}", "T", 4)]
    plan += [("ev", "F", 8), ("evout", "T", 4), ("ffn2", "F", FT), ("down2", "T", FT // 2),
             ("f3", "F", 1), ("v3", "T", 4), ("qk3", "F", 8), ("wo3", "T", 4),
             ("ffn3", "F", FT), ("down3", "T", FT // 2)]
    start, tindex, at, t = {}, {}, 0, 0
    for name, kind, n in plan:
        start[name] = at
        at += n
        if kind == "T":
            tindex[name] = t
            t += 1
    return plan, start, tindex, at


PLAN, START, TINDEX, NCHUNKS = make_plan()
KIND = {name: kind for name, kind, _ in PLAN}
COUNT = {name: n for name, _, n in PLAN}

NORMS = ("mix0", "ffn0", "ple0", "mix1", "ffn1", "ple1", "mid", "mix2", "ffn2", "mix3", "ffn3",
         "final")
NORM = {name: n for n, name in enumerate(NORMS)}
MID = NORM["mid"]


def place(n, t):
    return 2 * MID + 2 * t + n - MID if n in (MID, MID + 1) else 2 * n + t


XNORM = {name: n for n, name in enumerate(m for m in NORMS if m != "mid")}
UNITS = 2 * PAIRS
SC_BASE = (0, UNITS, 2 * UNITS)
TR_BASE = (0, PAIRS, PAIRS + UNITS)
STEPS = 2 * (8 + 4)
MIX_BASE = {"wo0": 0, "wo1": 8, "evout": 16, "wo3": 19}
ATTENTIONS = (("qk0", "wo0"), ("qk1", "wo1"), ("qk3", "wo3"))
LEADING = ("gate0", "gate1", "evout", "down2", "down3")
COPY_BASE = {"qk0": 0, "qk1": 8, "ev": 16, "qk3": 24}


def mixer_kernel(nc, w, cols, consts, evconst, out):
    with ExitStack() as ctx:
        def sb(name, shape, dt=F32, c=ctx):
            return c.enter_context(nc.sbuf_tensor(name, shape, dt))

        def sem(name):
            return ctx.enter_context(nc.semaphore(name))

        raw = sb("raw", [P, RING, CHUNK])
        whi = sb("whi", [P, RING, CHUNK], F32R)
        wlo = sb("wlo", [P, RING, CHUNK], F32R)
        h = sb("h", [P, TT, D])
        hn = sb("hn", [P, TT, D])
        xhi = sb("xhi", [P, KT, S], F32R)
        xlo = sb("xlo", [P, KT, S], F32R)
        gam = sb("gam", [P, 2, D])
        vbias = sb("vbias", [P, D])
        praw = sb("praw", [P, 2, S])
        phi = sb("phi", [P, 2, S], F32R)
        plo = sb("plo", [P, 2, S], F32R)
        col = sb("col", [P, NCOLS])
        cst = sb("cst", [P, NCONST])
        lamv = sb("lamv", [P, 4, DH])
        tiny = sb("tiny", [P, 64])
        diag = sb("diag", [P, TT, P])
        nmax = sb("nmax", [P, UNITS, TT])
        sums = sb("sums", [P, UNITS, TT])
        rsum = sb("rsum", [P, UNITS, TT])
        ostat = sb("ostat", [P, 3, PAIRS, TT])
        half = sb("half", [P, 16])
        with ExitStack() as c:
            nab = sb("nab", [P, HEADS, 6 * GRID_W], F32, c)
        with ExitStack() as c:
            t5b = sb("t5b", [P, 8, 384], F32, c)
            t5row = sb("t5row", [8, 384], F32, c)
            onehot = sb("onehot", [32, 384], F32, c)
            relb = sb("relb", [32, 8], F32, c)
            ol2 = sb("ol2", [P, KT, S], F32R, c)
        ctx.enter_context(nc.sbuf_tensor("bias_region", [P, HEADS * 6 * GRID_W], F32))
        with ExitStack() as c:
            hidhi = sb("hidhi", [P, FT, S], F32R, c)
            hidlo = sb("hidlo", [P, FT, S], F32R, c)
            act = sb("act", [P, 3, S], F32, c)
            mul = sb("mul", [P, 3, S], F32, c)
        with ExitStack() as c:
            qkT = sb("qkT", [P, 16, S], F32, c)
            v = sb("v", [P, TT, D], F32, c)
            prob = sb("prob", [P, 4, TT * S], F32, c)
            probT = sb("probT", [P, 2, TT * S], F32, c)
            with ExitStack() as c2:
                oh01 = sb("oh01", [P, KT, S], F32R, c2)
                ol01 = sb("ol01", [P, KT, S], F32R, c2)
            with ExitStack() as c2:
                oh2 = sb("oh2", [P, KT, S], F32R, c2)
                fstat = sb("fstat", [P, 8, S], F32, c2)
        ohi, olo = (oh01, oh01, oh2), (ol01, ol01, ol2)
        onrm, osq = (hn[:, t, 0:S].rearrange("p (t d) -> p t d", t=TT) for t in range(2))
        fmov = hn[:].rearrange("p t (g s) -> p (t g) s", g=4)
        with ExitStack() as c:
            z = sb("z", [P, 12, S], F32, c)
            pool = sb("pool", [P, 3, 4, 16 + S], F32, c)
            cval = sb("cval", [P, 4, S], F32, c)
            ya = sb("ya", [P, 4, S], F32, c)
            pw = sb("pw", [P, 4, P], F32, c)
            icnt = sb("icnt", [P, 4, S], F32, c)
        region = max(2 * FT * S + 6 * S, 16 * S + TT * D + 6 * TT * S + 16 * S)
        ctx.enter_context(nc.sbuf_tensor("mix_region", [P, region], F32))
        bank = [ctx.enter_context(nc.psum_tensor(f"bank{b}", [P, 512], F32)) for b in range(8)]

        w_in = [sem(f"w_in{i}") for i in range(RING)]
        w_hi = sem("w_hi")
        w_lo = sem("w_lo")
        w_used = sem("w_used")
        t_out = sem("t_out")
        x_in = sem("x_in")
        lam_in = sem("lam_in")
        vbias_in = sem("vbias_in")
        first_in = sem("first_in")
        const_in = sem("const_in")
        gam_in = [sem(f"gam_in{i}") for i in range(2)]
        p_in = sem("p_in")
        p_hi = sem("p_hi")
        p_lo = sem("p_lo")
        rpb_copied = sem("rpb_copied")
        nab_in = sem("nab_in")
        nab_ok = sem("nab_ok")
        ev_in = sem("ev_in")
        t5_in = sem("t5_in")
        t5_row = sem("t5_row")
        t5_sb = sem("t5_sb")
        t5_out = sem("t5_out")
        t5_back = sem("t5_back")
        t5_ok = sem("t5_ok")
        cst_ok = sem("cst_ok")
        ssq = sem("ssq")
        rstd_ok = sem("rstd_ok")
        hn_ok = sem("hn_ok")
        h_ok = sem("h_ok")
        tr_x = sem("tr_x")
        x_hi = sem("x_hi")
        x_lo = sem("x_lo")
        copied = sem("copied")
        v_ok = sem("v_ok")
        conv_a = sem("conv_a")
        conv_b = sem("conv_b")
        conv_ok = sem("conv_ok")
        silu_ok = sem("silu_ok")
        mul_ok = sem("mul_ok")
        hid_hi = sem("hid_hi")
        hid_lo = sem("hid_lo")
        sc_out = sem("sc_out")
        sc_free = sem("sc_free")
        max_ok = sem("max_ok")
        exp_ok = sem("exp_ok")
        prob_ok = sem("prob_ok")
        prob_tr = sem("prob_tr")
        probT_ok = sem("probT_ok")
        pv_out = sem("pv_out")
        o_sq = sem("o_sq")
        o_rstd = sem("o_rstd")
        o_norm = sem("o_norm")
        o_tr = sem("o_tr")
        mix_hi = sem("mix_hi")
        mix_lo = sem("mix_lo")
        lam_sum = sem("lam_sum")
        lam_exp = sem("lam_exp")
        g_out = sem("g_out")
        pool_ok = sem("pool_ok")
        pool_out = sem("pool_out")
        ya_ok = sem("ya_ok")
        f_log = sem("f_log")
        f_ok = sem("f_ok")
        f_base = sem("f_base")
        out_ok = sem("out_ok")
        store = sem("store")
        a_step = sem("a_step")
        d_step = sem("d_step")
        g_step = sem("g_step")

        rpb_dram = nc.dram_tensor("rpb_scratch", [GRID_W, HEADS * 15 * 31], F32,
                                  kind="Internal").ap()
        t5_dram = nc.dram_tensor("t5_scratch", [P, 8, 384], F32, kind="Internal").ap()

        ident = cst[:, C_ID:C_ID + P]
        dist = cst[:, C_DIST:C_DIST + 512]
        colmask = cst[:, C_COLM:C_COLM + GRID_W]
        causal = cst[:, C_CAUS:C_CAUS + 384]

        def pcol(i):
            return col[:, i:i + 1]

        def slot8(t, c):
            return t[:, c % RING, :].rearrange("p (k n) -> p k n", k=KT)

        def slot2(t, c):
            return t[:, c % RING, :].rearrange("p (k n) -> p k n", k=2)

        def tbank(t, n, proj=False):
            return bank[(0 if proj else 4) + 2 * t + n]

        def chunk_sources(name, i):
            W = w[name]
            if KIND[name] == "F":
                if name[:2] == "qk":
                    col0 = P * qk_tile(i)
                else:
                    col0 = 256 * (EV_ORDER[i] if name == "ev" else i)
                r = W[:, col0:col0 + 256].rearrange("(k p) n -> p k n", p=P)
                return [r[:, 0:4, :], r[:, 4:8, :]]
            row = 256 * (EVOUT_ORDER[i] if name == "evout" else i)
            r = W[row:row + 256, :].rearrange("(k p) n -> p k n", p=P)
            return [r[:, 0:1, :], r[:, 1:2, :]]

        EV_ORDER = (6, 7, 2, 3, 4, 5, 0, 1)
        EVOUT_ORDER = (2, 3, 0, 1)

        def qk_tile(i):
            return 8 * (i % 2) + 2 * (i // 2)

        def ffn_chunks(engine, body):
            for jj in range(RING):
                body(0, jj)
            with engine.Fori(1, FT // RING) as turn:
                for jj in range(RING):
                    body(turn, jj)
            body(FT // RING, 0)

        block = ctx.enter_context(nc.Block())

        @block.sync
        def _(sp):
            for t in range(TT):
                sp.dma_start(h[:, t, :], w["x"][t * P:(t + 1) * P, :]).then_inc(x_in, 16)
            sp.dma_start(gam[:, 0, :], w["gammas"][0].partition_broadcast(P)).then_inc(first_in, 16)
            sp.dma_start(ident, consts[:, C_ID:C_ID + P]).then_inc(first_in, 16)
            def ffn_chunk(name):
                c0 = START[name]

                def load(turn, jj):
                    j = RING * turn + jj
                    sp.wait_ge(w_lo, c0 - RING + 1 + j)
                    for a in range(2):
                        src = w[name][a][:, bass.ds(P * j, P)].rearrange("(k p) n -> p k n", p=P)
                        sp.dma_start(slot8(raw, c0 + jj)[:, :, P * a:P * (a + 1)], src
                                     ).then_inc(w_in[(c0 + jj) % RING], 16)
                return load

            for name, kind, n in PLAN:
                if name[:3] == "ffn":
                    ffn_chunks(sp, ffn_chunk(name))
                    continue
                for i in range(n):
                    c = START[name] + i
                    if c >= RING:
                        sp.wait_ge(w_lo, c - RING + 1)
                    src = chunk_sources(name, i)
                    if kind == "F":
                        dst = [slot8(raw, c)[:, 4 * a:4 * (a + 1), :] for a in range(2)]
                    else:
                        dst = [slot2(raw, c)[:, a:a + 1, :] for a in range(2)]
                    for a in range(2):
                        sp.dma_start(dst[a], src[a]).then_inc(w_in[c % RING], 16)
            for t in range(TT):
                for i in range(2):
                    sp.wait_ge(out_ok, 2 * t + i + 1)
                    cs = slice(i * 512, (i + 1) * 512)
                    sp.dma_start(out[t * P:(t + 1) * P, cs], hn[:, t, cs]).then_inc(store, 16)
            sp.wait_ge(store, 2 * 16 * TT)

        @block.gpsimd
        def _(gp):
            steps = [0]

            def link(ins):
                steps[0] += 1
                ins.then_inc(g_step, 1)
                gp.wait_ge(g_step, steps[0])

            gp.dma_start(cst[:, P:], consts[:, P:]).then_inc(const_in, 16)
            gp.dma_start(col[:], cols).then_inc(const_in, 16)

            def load_gamma(n):
                gp.dma_start(gam[:, n % 2, :], w["gammas"][n].partition_broadcast(P)
                             ).then_inc(gam_in[n % 2], 16)

            def load_p(layer):
                gp.dma_start(praw[:], w["p"][layer].rearrange("(k p) t -> p k t", p=P)
                             ).then_inc(p_in, 16)

            def rstd_tile(n, t):
                gp.wait_ge(ssq, place(n, t) + 1)
                link(nc.gpsimd.tensor_scalar(tiny[:, 4 + t:5 + t], tiny[:, 2 * t:2 * t + 1],
                                             tiny[:, 2 * t + 1:2 * t + 2], NORM_EPS,
                                             ALU.add, ALU.add))
                nc.gpsimd.tensor_tensor(tiny[:, 6 + t:7 + t], tiny[:, 4 + t:5 + t],
                                        half[:, 0:1], ALU.pow).then_inc(rstd_ok, 1)

            def next_gamma(n):
                if n + 2 < len(NORMS):
                    if n == MID:
                        gp.wait_ge(h_ok, 2 * place(n + 1, 1) - 2)
                    else:
                        gp.wait_ge(hn_ok, 2 * XNORM[NORMS[n]] + 2)
                    load_gamma(n + 2)

            def rstd(n):
                for t in range(TT):
                    rstd_tile(n, t)
                next_gamma(n)

            link(nc.gpsimd.memset(half[:], -0.5))
            rstd_tile(0, 0)
            rstd_tile(0, 1)
            gp.wait_ge(const_in, 32)
            link(nc.gpsimd.tensor_scalar(col[:, COL_BQK:COL_BQK + 8], col[:, COL_BQK:COL_BQK + 8],
                                         0.125, None, ALU.mult))
            nc.gpsimd.tensor_scalar(pcol(COL_SUBLN), pcol(COL_SUBLN), 1.0 - LAM_INIT, None,
                                    ALU.mult).then_inc(cst_ok, 1)

            def load_neighbourhood():
                rows, width = w["rpb"].shape[1:]
                size = HEADS * rows * width
                gp.dma_start(rpb_dram, w["rpb"].rearrange("h r c -> (h r c)")
                             .partition_broadcast(GRID_W)).then_inc(rpb_copied, 16)
                gp.wait_ge(rpb_copied, 16)
                for r in range(2):
                    for m in range(6):
                        src = bass.AP(tensor=rpb_dram.tensor, offset=(m - 2 - r + 7) * width + 15,
                                      ap=[[size - 1, GRID_W], [rows * width, HEADS], [1, GRID_W]])
                        gp.dma_start(nab[GRID_W * r:GRID_W * (r + 1), :,
                                         GRID_W * m:GRID_W * (m + 1)], src).then_inc(nab_in, 16)

            for layer in range(2):
                if layer:
                    rstd(NORM["mix1"])
                else:
                    next_gamma(0)
                    load_gamma(1)
                    gp.dma_start(lamv[:], w["lam"].partition_broadcast(P)).then_inc(lam_in, 16)
                    load_p(0)
                    gp.dma_start(vbias[:], w["v_bias"].partition_broadcast(P)
                                 ).then_inc(vbias_in, 16)
                    for j in range(PAIRS):
                        gp.wait_ge(o_sq, j + 1)
                        link(nc.gpsimd.tensor_scalar(ostat[:, 1, j, :], ostat[:, 0, j, :],
                                                     1.0 / P, SUBLN_EPS, ALU.mult, ALU.add))
                        nc.gpsimd.tensor_tensor(ostat[:, 2, j, :], ostat[:, 1, j, :],
                                                half[:, 0:2], ALU.pow).then_inc(o_rstd, 1)
                rstd(NORM[f"ffn{layer}"])
                if layer == 0:
                    load_neighbourhood()
                    gp.wait_ge(nab_in, 16 * 12)
                    view = nab[:].rearrange("p h (m c) -> p (h m) c", c=GRID_W)
                    mask = colmask.unsqueeze(1).to_broadcast([P, HEADS * 6, GRID_W])
                    nc.gpsimd.tensor_tensor(view, view, mask, ALU.add).then_inc(nab_ok, 1)
                rstd(NORM[f"ple{layer}"])
                if layer == 0:
                    gp.wait_ge(w_used, START["proj0"] + 1)
                    load_p(1)
            for t in range(TT):
                rstd_tile(MID, t)
                rstd_tile(MID + 1, t)
            next_gamma(MID)
            next_gamma(MID + 1)
            gp.wait_ge(w_used, START["gate1"] + COUNT["gate1"])
            gp.dma_start(onehot[:], w["onehot"]).then_inc(t5_in, 16)
            gp.dma_start(relb[:], w["rel_bias"]).then_inc(t5_in, 16)
            gp.dma_start(pw[:], w["pool_w"].rearrange("g c d -> c g d")).then_inc(ev_in, 16)
            gp.dma_start(icnt[:], evconst).then_inc(ev_in, 16)
            link(nc.gpsimd.memset(pool[:, :, :, 0:16], 0.0))
            gp.wait_ge(copied, COPY_BASE["ev"] + 2)
            at = 0
            for level in range(4):
                n, to = 1 << level, 2 if at == 1 else 1
                link(nc.gpsimd.tensor_tensor(pool[:, to, level:4, 16:16 + S],
                                             pool[:, at, level:4, 16:16 + S],
                                             pool[:, at, level:4, 16 - n:16 - n + S], ALU.add))
                at = to
            gp.wait_ge(ev_in, 32)
            for g in range(4):
                to = 1 if g % 2 == 0 else 2
                link(nc.gpsimd.tensor_tensor(pool[:, to, g, 16:16 + S], pool[:, to, g, 16:16 + S],
                                             icnt[:, g, :], ALU.mult))
                nc.gpsimd.tensor_tensor(pool[:, to, g, 16:16 + S], pool[:, to, g, 16:16 + S],
                                        pool[:, 0, g, 16:16 + S], ALU.subtract).then_inc(pool_ok, 1)
            rstd(NORM["ffn2"])
            gp.wait_ge(t5_sb, 1)
            gp.dma_start(t5_dram.rearrange("q h m -> h q m"),
                         t5row[:].unsqueeze(1).to_broadcast([8, P, 384])).then_inc(t5_out, 16)
            gp.wait_ge(t5_out, 16)
            for lo, n, src in ((0, P, P), (P, S, 0)):
                gp.dma_start(t5b[:, :, lo:lo + n],
                             bass.AP(tensor=t5_dram.tensor, offset=P - 1 + src,
                                     ap=[[8 * 384 - 1, P], [384, 8], [1, n]])).then_inc(t5_back, 16)
            gp.wait_ge(t5_back, 32)
            nc.gpsimd.tensor_tensor(t5b[:], t5b[:], causal.unsqueeze(1).to_broadcast([P, 8, 384]),
                                    ALU.add).then_inc(t5_ok, 1)
            rstd(NORM["mix3"])
            gp.wait_ge(tr_x, 4 * XNORM["mix3"] + 4)
            nc.gpsimd.tensor_copy(fstat[:], cst[:, C_SEL:C_SEL + 8].unsqueeze(2)
                                  .to_broadcast([P, 8, S])).then_inc(f_base, 1)
            nc.gpsimd.tensor_copy(fmov, cst[:, C_SEL + 8:C_SEL + 16].unsqueeze(2)
                                  .to_broadcast([P, 8, S])).then_inc(f_base, 1)
            rstd(NORM["ffn3"])
            rstd(NORM["final"])

        @block.scalar
        def _(ac):
            steps = [0]

            def link(ins):
                steps[0] += 1
                ins.then_inc(a_step, 1)
                ac.wait_ge(a_step, steps[0])

            def split(c, turn=0):
                if c >= NCHUNKS:
                    return
                ac.wait_ge(w_in[c % RING], 32 * (c // RING + 1) + 32 * turn)
                if c >= RING:
                    ac.wait_ge(w_used, c - RING + 1 + RING * turn)
                nc.scalar.copy(whi[:, c % RING, :], raw[:, c % RING, :]).then_inc(w_hi, 1)

            def split_p(layer):
                ac.wait_ge(p_in, 16 * (layer + 1))
                if layer:
                    ac.wait_ge(w_used, START["proj0"] + 1)
                nc.scalar.copy(phi[:], praw[:]).then_inc(p_hi, 1)

            def squares(n, t):
                name = NORMS[n]
                for i in range(2):
                    if n == 0:
                        ac.wait_ge(x_in, 32)
                    else:
                        ac.wait_ge(h_ok, 2 * place(n, t) - 4 + i + 1)
                    ins = nc.scalar.activation(
                        tbank(t, i, name in ("ffn0", "ffn1", "ffn3"))[:],
                        h[:, t, i * 512:(i + 1) * 512], ACT.Square, scale=D ** -0.5,
                        accum_out=tiny[:, 2 * t + i:2 * t + i + 1])
                ins.then_inc(ssq, 1)

            def take_x(name, t):
                for i in range(2):
                    ac.wait_ge(tr_x, 4 * XNORM[name] + 2 * t + i + 1)
                    nc.scalar.copy(xhi[:, 4 * i:4 * i + 4, t * P:(t + 1) * P],
                                   bank[4 + 2 * t + i][:].rearrange("p (k q) -> p k q", k=4)
                                   ).then_inc(x_hi, 1)

            def norm(name, produced=None, first=None, late=()):
                leading = produced in LEADING
                for t in range(TT):
                    if first:
                        first(t)
                    if name == "mix2":
                        squares(MID, t)
                    squares(NORM[name], t)
                    if t == 0 and produced in ("gate0", "down2"):
                        split(START[produced] + COUNT[produced] - 2 + RING)
                    if leading and name != "mix2":
                        take_x(name, t)
                if name == "final":
                    return
                if not leading or name == "mix2":
                    if name == "mix0":
                        split(0)
                    for t in range(TT):
                        take_x(name, t)
                        if t == 0 and name[:3] == "ple":
                            split(late[0])
                if produced in ("gate1", "evout"):
                    split(START[produced] + COUNT[produced] - 2 + RING)
                for c in late[name[:3] == "ple":]:
                    split(c)

            def copy_out(name, i):
                c = START[name] + i
                src = bank[c % RING]
                ac.wait_ge(w_used, c + 1)
                if name == "qk1":
                    if i == 0:
                        ac.wait_ge(cst_ok, 1)
                    for f in range(2):
                        to = qk_tile(i) + f
                        ins = nc.scalar.activation(qkT[:, to, :], src[:, f * S:(f + 1) * S],
                                                   ACT.Identity, bias=pcol(COL_BQK + to),
                                                   scale=0.125 if i % 2 == 0 else 1.0)
                    ins.then_inc(copied, 1)
                elif name == "ev":
                    e = EV_ORDER[i]
                    if e < 6:
                        dst = z[:, 2 * e:2 * e + 2, :]
                    else:
                        dst = pool[:, 0, 2 * e - 12:2 * e - 10, 16:16 + S]
                    ins = nc.scalar.copy(dst, src[:].rearrange("p (f t) -> p f t", f=2))
                    ins.then_inc(copied, 1)
                else:
                    dst = qkT[:, qk_tile(i):qk_tile(i) + 2, :].rearrange("p f t -> p (f t)")
                    nc.scalar.activation(dst, src[:], ACT.Copy, scale=0.125 if i % 2 == 0 else 1.0
                                         ).then_inc(copied, 1)

            def t_splits(name, skip=1):
                for i in range(COUNT[name] - skip):
                    split(START[name] + i + RING)

            def attention(a):
                base, units = SC_BASE[a], UNITS

                def exps(u):
                    ac.wait_ge(max_ok, base + u + 1)
                    for t in range(TT):
                        off, n = span(a, t)
                        ins = nc.scalar.activation(prob[:, u % 4, off:off + n],
                                                   prob[:, u % 4, off:off + n], ACT.Exp,
                                                   bias=nmax[:, u, t:t + 1],
                                                   accum_out=sums[:, u, t:t + 1])
                    ins.then_inc(exp_ok, 1)

                def take_T(u):
                    k = TR_BASE[a] + u
                    ac.wait_ge(prob_tr, k + 1)
                    if k >= 2:
                        ac.wait_ge(pv_out, k - 1)
                    n = 512 if a < 2 else 384
                    nc.scalar.copy(probT[:, k % 2, 0:n], bank[6][:, 0:n]).then_inc(probT_ok, 1)

                def square_o(j):
                    ac.wait_ge(pv_out, j + 1)
                    for t in range(TT):
                        ins = nc.scalar.activation(osq[:, t, :], bank[7][:, t * P:(t + 1) * P],
                                                   ACT.Square, accum_out=ostat[:, 0, j, t:t + 1])
                    ins.then_inc(o_sq, 1)

                def take_o(j):
                    if a == 0:
                        if j == 0:
                            ac.wait_ge(cst_ok, 1)
                        ac.wait_ge(o_tr, j + 1)
                        nc.scalar.activation(ohi[a][:, j, :], bank[6][:, 0:S], ACT.Copy,
                                             scale=pcol(COL_SUBLN)).then_inc(mix_hi, 1)
                    else:
                        ac.wait_ge(pv_out, TR_BASE[a] + 2 * j + 2)
                        nc.scalar.copy(ohi[a][:, j, :], bank[7][:, 0:S]).then_inc(mix_hi, 1)

                qk = ATTENTIONS[a][0]
                for s in range(STEPS):
                    u = s - 4
                    if a == 0:
                        if s % 2 == 0 and s >= 8:
                            take_o((s - 8) // 2)
                        if s % 2 == 1 and 7 <= s < 23:
                            take_T((s - 7) // 2)
                    else:
                        if s % 2 == 1 and s >= 7 and (s - 7) // 2 < PAIRS:
                            take_o((s - 7) // 2)
                        if 1 <= u < units + 1:
                            take_T(u - 1)
                    if a and s % 4 == 3 and s < 16:
                        copy_out(qk, s // 2)
                    if a == 0 and s % 2 == 1 and 7 <= s < 23:
                        square_o((s - 7) // 2)
                    if 0 <= u < units:
                        exps(u)
                    if s % 2 == 1:
                        if s < 16 and not (a and s % 4 == 3):
                            copy_out(qk, s // 2)
                        if s < STEPS - 3:
                            split(START[qk] + s // 2 + RING)
                    if s == STEPS - 2:
                        split(START[qk] + s // 2 - 1 + RING)

            def ffn(layer):
                name = f"ffn{layer}"
                conv = layer >= 2
                c0, base = START[name], FT * layer

                def hi(turn, jj):
                    j = RING * turn + jj
                    ac.wait_ge(mul_ok, base + 1 + j)
                    nc.scalar.copy(hidhi[:, bass.ds(j, 1), :], mul[:, jj:jj + 1, :]
                                   ).then_inc(hid_hi, 1)

                def chunk(turn, jj):
                    first = isinstance(turn, int) and turn == 0
                    j = RING * turn + jj
                    b = bank[(c0 + jj) % RING]
                    ac.wait_ge(w_used, c0 + 1 + j)
                    if not first:
                        ac.wait_ge(mul_ok, base + 1 + jj + RING * (turn - 1))
                    if conv:
                        tap = col[:, bass.ds(COL_CONV[layer - 2] + 2 + 3 * j, 1)]
                        nc.scalar.activation(act[:, jj, :], b[:, 0:S], ACT.Identity,
                                             bias=col[:, bass.ds(COL_CONVB[layer - 2] + j, 1)],
                                             scale=tap).then_inc(conv_a, 1)
                    else:
                        nc.scalar.activation(act[:, jj, :], b[:, 0:S], ACT.Silu
                                             ).then_inc(silu_ok, 1)
                    if jj:
                        hi(turn, jj - 1)
                    elif not first:
                        hi(turn - 1, RING - 1)
                    if conv:
                        ac.wait_ge(conv_ok, FT * (layer - 2) + 1 + j)
                        nc.scalar.activation(act[:, jj, :], act[:, jj, :], ACT.Silu
                                             ).then_inc(silu_ok, 1)
                    split(c0 + jj + RING, turn)

                ffn_chunks(ac, chunk)
                hi(FT // RING, 0)

            norm("mix0", late=[1, 2])
            ac.wait_ge(lam_sum, 2)
            nc.scalar.activation(tiny[:, 58:60], tiny[:, 56:58], ACT.Exp).then_inc(lam_exp, 1)
            split_p(0)

            for layer in range(2):
                qk, vn, wo = f"qk{layer}", f"v{layer}", f"wo{layer}"
                t_splits(vn, 0)
                attention(layer)
                norm(f"ffn{layer}", wo, late=[START[wo] + 3 + RING])
                ffn(layer)
                if layer == 1:
                    split_p(1)
                t_splits(f"down{layer}")
                last = START[f"down{layer}"] + COUNT[f"down{layer}"] - 1
                norm(f"ple{layer}", late=[last + RING, last + 1 + RING])
                gate = f"gate{layer}"
                t_splits(gate, 2)

                def sigmoids(t):
                    for n in range(2):
                        if 2 * t + n < 3:
                            ac.wait_ge(t_out, 3 * TINDEX[gate] + 2 * t + n + 1)
                        else:
                            ac.wait_ge(w_used, START[gate] + COUNT[gate])
                        nc.scalar.activation(hn[:, t, n * 512:(n + 1) * 512], tbank(t, n)[:],
                                             ACT.Sigmoid).then_inc(g_out, 1)

                norm("mix1" if layer == 0 else "mix2", gate, sigmoids, [START[gate] + 3 + RING])

            def pool_hi(g0):
                to = phi if g0 == 0 else xhi[:, 6:8, :]
                ac.wait_ge(pool_out, g0 + 2)
                for g in range(g0, g0 + 2):
                    ins = nc.scalar.activation(to[:, g - g0, :], bank[4 + g][:, 0:S], ACT.Copy,
                                               scale=pcol(COL_PSCALE + g))
                ins.then_inc(mix_hi, 1)

            for i in range(8):
                copy_out("ev", i)
                if i == 7:
                    pool_hi(2)
                    ac.wait_ge(ya_ok, 1)
                    nc.scalar.copy(xhi[:, 0:4, :], ya[:]).then_inc(mix_hi, 1)
                split(START["ev"] + i + RING)
                if i == 4:
                    pool_hi(0)
            t_splits("evout", 2)
            norm("ffn2", "evout", late=[START["evout"] + 3 + RING])
            ffn(2)
            t_splits("down2", 2)
            norm("mix3", "down2", late=[START["down2"] + FT // 2 - 1 + RING])
            cf = START["f3"]
            split(cf + RING)
            fb = bank[cf % RING][:, 0:S]
            link(nc.scalar.activation(osb_f(prob)[0], fb, ACT.Abs, bias=pcol(COL_BF)))
            link(nc.scalar.activation(osb_f(prob)[0], osb_f(prob)[0], ACT.Exp, scale=-1.0))
            nc.scalar.activation(osb_f(prob)[0], osb_f(prob)[0], ACT.Ln, bias=1.0
                                 ).then_inc(f_log, 1)
            t_splits("v3", 0)
            attention(2)
            norm("ffn3", "wo3", late=[START["wo3"] + 3 + RING])
            ffn(3)
            t_splits("down3", 0)
            norm("final")

        @block.vector
        def _(ve):
            steps = [0]

            def link(ins):
                steps[0] += 1
                ins.then_inc(d_step, 1)
                ve.wait_ge(d_step, steps[0])

            def split(c, turn=0):
                if c >= NCHUNKS:
                    return
                ve.wait_ge(w_hi, c + 1 + RING * turn)
                nc.vector.tensor_tensor(wlo[:, c % RING, :], raw[:, c % RING, :],
                                        whi[:, c % RING, :].bitcast(F32), ALU.subtract
                                        ).then_inc(w_lo, 1)

            def split_p(layer):
                ve.wait_ge(p_hi, layer + 1)
                nc.vector.tensor_tensor(plo[:], praw[:], phi[:].bitcast(F32), ALU.subtract
                                        ).then_inc(p_lo, 1)

            def norm_tile(n, t):
                if n == 0:
                    ve.wait_ge(first_in, 32)
                else:
                    ve.wait_ge(gam_in[n % 2], 16 * ((n + 1) // 2))
                direct = NORMS[n] in ("mid", "final")
                if direct:
                    ve.wait_ge(rstd_ok, place(n, t) + 1)
                for i in range(2):
                    half_row = slice(i * 512, (i + 1) * 512)
                    g, hs = gam[:, n % 2, half_row], h[:, t, half_row]
                    if direct:
                        ins = nc.vector.scalar_tensor_tensor(
                            out=(h if n == MID else hn)[:, t, half_row], in0=hs,
                            scalar=tiny[:, 6 + t:7 + t], in1=g, op0=ALU.mult, op1=ALU.mult)
                        ins.then_inc(h_ok if n == MID else out_ok, 1)
                    else:
                        if n:
                            ve.wait_ge(h_ok, 2 * place(n, t) - 4 + i + 1)
                        else:
                            ve.wait_ge(x_in, 32)
                        nc.vector.tensor_tensor(hn[:, t, half_row], hs, g, ALU.mult)
                if not direct:
                    ve.wait_ge(rstd_ok, place(n, t) + 1)
                    nc.vector.tensor_scalar(diag[:, t, :], ident, tiny[:, 6 + t:7 + t], None,
                                            ALU.mult).then_inc(hn_ok, 1)

            def lo_x(name, t):
                for i in range(2):
                    ve.wait_ge(x_hi, 4 * XNORM[name] + 2 * t + i + 1)
                    part = (slice(None), slice(4 * i, 4 * i + 4), slice(t * P, (t + 1) * P))
                    src = bank[4 + 2 * t + i][:].rearrange("p (k q) -> p k q", k=4)
                    nc.vector.tensor_tensor(xlo[part], src, xhi[part].bitcast(F32), ALU.subtract
                                            ).then_inc(x_lo, 1)

            def norm(name, produced=None, first=None, late=()):
                leading = produced in LEADING
                for t in range(TT):
                    if first:
                        first(t)
                    if name == "mix2":
                        norm_tile(MID, t)
                    norm_tile(NORM[name], t)
                    if leading and name != "mix2":
                        lo_x(name, t)
                    if t == 0 and produced == "gate0":
                        split(START[produced] + COUNT[produced] - 2 + RING)
                if name == "final":
                    return
                if not leading or name == "mix2":
                    if name == "mix0":
                        split(0)
                    for t in range(TT):
                        lo_x(name, t)
                        if t == 0 and name[:3] == "ple":
                            split(late[0])
                if produced and produced != "gate0":
                    split(START[produced] + COUNT[produced] - 2 + RING)
                for c in late[name[:3] == "ple":]:
                    split(c)

            def t_ready(name, t, n):
                if 2 * t + n < 3:
                    ve.wait_ge(t_out, 3 * TINDEX[name] + 2 * t + n + 1)
                else:
                    ve.wait_ge(w_used, START[name] + COUNT[name])

            def t_splits(name, skip=1):
                for i in range(COUNT[name] - skip):
                    split(START[name] + i + RING)

            def update(name, proj=False):
                def tile(t):
                    for n in range(2):
                        t_ready(name, t, n)
                        hs = h[:, t, n * 512:(n + 1) * 512]
                        nc.vector.tensor_tensor(hs, tbank(t, n, proj)[:], hs, ALU.add
                                                ).then_inc(h_ok, 1)
                return tile

            def take_v(name):
                for t in range(TT):
                    for n in range(2):
                        t_ready(name, t, n)
                        to = v[:, t, n * 512:(n + 1) * 512]
                        if name == "v1":
                            ve.wait_ge(vbias_in, 16)
                            ins = nc.vector.tensor_tensor(to, tbank(t, n)[:],
                                                          vbias[:, n * 512:(n + 1) * 512], ALU.add)
                        else:
                            ins = nc.vector.tensor_copy(to, tbank(t, n)[:])
                        ins.then_inc(v_ok, 1)

            def attention(a):
                base, units = SC_BASE[a], UNITS

                def bias_max(u):
                    ve.wait_ge(sc_out, base + u + 1)
                    if a == 0:
                        if u >= 4:
                            ve.wait_ge(prob_tr, (u - 4) // 2 + 1)
                    elif u >= 4:
                        ve.wait_ge(prob_tr, TR_BASE[a] + u - 3)
                    b, pr = bank[4 + u % 2], prob[:, u % 4, :]
                    if a == 0:
                        link_free(nc.vector.scalar_tensor_tensor(
                            out=pr, in0=dist, scalar=-(2.0 ** -(u // 2 + 1)), in1=b[:],
                            op0=ALU.mult, op1=ALU.add), base + u)
                    elif a == 1:
                        if u == 0:
                            ve.wait_ge(nab_ok, 1)
                        nc.vector.tensor_tensor(pr[:, 0:S], b[:, 0:S], nab[:, u, P:P + S], ALU.add)
                        link_free(nc.vector.tensor_tensor(pr[:, S:2 * S], b[:, S:2 * S],
                                                          nab[:, u, 0:S], ALU.add), base + u)
                    else:
                        if u == 8:
                            ve.wait_ge(t5_ok, 1)
                        bias = causal if u < 8 else t5b[:, u - 8, :]
                        link_free(nc.vector.tensor_tensor(pr[:, 0:384], b[:, 0:384], bias, ALU.add),
                                  base + u)
                    if a < 2:
                        ins = nc.vector.tensor_reduce(nmax[:, u, :],
                                                      pr.rearrange("p (t k) -> p t k", t=TT),
                                                      X, ALU.max, negate=True)
                    else:
                        for t in range(TT):
                            off, n = span(a, t)
                            ins = nc.vector.tensor_reduce(nmax[:, u, t:t + 1], pr[:, off:off + n],
                                                          X, ALU.max, negate=True)
                    ins.then_inc(max_ok, 1)

                def link_free(ins, k):
                    ins.then_inc(sc_free, 1)
                    ve.wait_ge(sc_free, k + 1)

                def normalise(u):
                    ve.wait_ge(exp_ok, base + u + 1)
                    link(nc.vector.reciprocal(rsum[:, u, :], sums[:, u, :]))
                    if a == 0:
                        if u % 2 == 0:
                            return
                        link(nc.vector.tensor_scalar(rsum[:, u, :], rsum[:, u, :], tiny[:, 60:61],
                                                     None, ALU.mult))
                        for t in range(TT):
                            off, n = span(a, t)
                            p0 = prob[:, (u - 1) % 4, off:off + n]
                            ins = nc.vector.tensor_scalar(p0, p0, rsum[:, u - 1, t:t + 1], None,
                                                          ALU.mult)
                        link(ins)
                        for t in range(TT):
                            off, n = span(a, t)
                            p0, p1 = (prob[:, (u - 1 + m) % 4, off:off + n] for m in range(2))
                            ins = nc.vector.scalar_tensor_tensor(
                                out=p0, in0=p1, scalar=rsum[:, u, t:t + 1], in1=p0,
                                op0=ALU.mult, op1=ALU.add)
                    else:
                        for t in range(TT):
                            off, n = span(a, t)
                            pr = prob[:, u % 4, off:off + n]
                            ins = nc.vector.tensor_scalar(pr, pr, rsum[:, u, t:t + 1], None,
                                                          ALU.mult)
                    ins.then_inc(prob_ok, 1)

                def norm_o(j):
                    ve.wait_ge(o_rstd, j + 1)
                    if j:
                        ve.wait_ge(o_tr, j)
                    for t in range(TT):
                        ins = nc.vector.tensor_scalar(onrm[:, t, :], bank[7][:, t * P:(t + 1) * P],
                                                      ostat[:, 2, j, t:t + 1], None, ALU.mult)
                    ins.then_inc(o_norm, 1)

                def lo_out(j):
                    ve.wait_ge(mix_hi, MIX_BASE[ATTENTIONS[a][1]] + j + 1)
                    if a == 0:
                        ins = nc.vector.scalar_tensor_tensor(
                            out=olo[a][:, j, :], in0=bank[6][:, 0:S], scalar=pcol(COL_SUBLN),
                            in1=ohi[a][:, j, :].bitcast(F32), op0=ALU.mult, op1=ALU.subtract)
                    else:
                        ins = nc.vector.tensor_tensor(olo[a][:, j, :], bank[7][:, 0:S],
                                                      ohi[a][:, j, :].bitcast(F32), ALU.subtract)
                    ins.then_inc(mix_lo, 1)

                if a == 0:
                    ve.wait_ge(lam_exp, 1)
                    link(nc.vector.tensor_tensor(tiny[:, 61:62], tiny[:, 59:60], tiny[:, 58:59],
                                                 ALU.subtract))
                    link(nc.vector.tensor_scalar(tiny[:, 60:61], tiny[:, 61:62], -LAM_INIT, None,
                                                 ALU.add))
                for s in range(STEPS):
                    u = s - 4
                    if a > 0 and s % 2 == 1 and s >= 7 and (s - 7) // 2 < PAIRS:
                        lo_out((s - 7) // 2)
                    if a == 0 and s >= 8 and u % 4 == 0:
                        lo_out((s - 8) // 2)
                    if 0 <= u < units:
                        bias_max(u)
                    if a == 0 and s >= 8 and u % 4 == 2:
                        lo_out((s - 8) // 2)
                    if a == 0 and s % 2 == 1 and 7 <= s < 23:
                        norm_o((s - 7) // 2)
                    if 0 <= u < units and a > 0:
                        normalise(u)
                    if s % 2 == 0 and 2 <= s < STEPS - 2:
                        split(START[ATTENTIONS[a][0]] + s // 2 - 1 + RING)
                    if 0 <= u < units and a == 0:
                        normalise(u)

            def ffn(layer):
                name = f"ffn{layer}"
                conv = layer >= 2
                c0, base = START[name], FT * layer

                def lo(turn, jj):
                    j = RING * turn + jj
                    ve.wait_ge(hid_hi, base + 1 + j)
                    nc.vector.tensor_tensor(hidlo[:, bass.ds(j, 1), :], mul[:, jj:jj + 1, :],
                                            hidhi[:, bass.ds(j, 1), :].bitcast(F32), ALU.subtract
                                            ).then_inc(hid_lo, 1)

                def lo_before(turn, jj, first):
                    if jj:
                        lo(turn, jj - 1)
                    elif not first:
                        lo(turn - 1, RING - 1)

                def chunk(turn, jj):
                    first = isinstance(turn, int) and turn == 0
                    j = RING * turn + jj
                    b = bank[(c0 + jj) % RING]
                    if conv:
                        def tap(i):
                            return col[:, bass.ds(COL_CONV[layer - 2] + i + 3 * j, 1)]
                        acc = act[:, jj, :]
                        ve.wait_ge(conv_a, FT * (layer - 2) + 1 + j)
                        ve_step(nc.vector.scalar_tensor_tensor(
                            out=acc[:, 1:S], in0=b[:, 0:S - 1], scalar=tap(1),
                            in1=acc[:, 1:S], op0=ALU.mult, op1=ALU.add), layer, 1 + j)
                        nc.vector.scalar_tensor_tensor(
                            out=acc[:, 2:S], in0=b[:, 0:S - 2], scalar=tap(0),
                            in1=acc[:, 2:S], op0=ALU.mult, op1=ALU.add).then_inc(conv_ok, 1)
                        lo_before(turn, jj, first)
                    ve.wait_ge(silu_ok, base + 1 + j)
                    if not first:
                        ve.wait_ge(hid_lo, base + 1 + jj + RING * (turn - 1))
                    nc.vector.tensor_tensor(mul[:, jj, :], act[:, jj, :], b[:, S:2 * S],
                                            ALU.mult).then_inc(mul_ok, 1)
                    if not conv:
                        lo_before(turn, jj, first)
                    split(c0 + jj + RING, turn)

                def ve_step(ins, layer, count):
                    ins.then_inc(conv_b, 1)
                    ve.wait_ge(conv_b, FT * (layer - 2) + count)

                ffn_chunks(ve, chunk)
                lo(FT // RING, 0)

            norm("mix0", late=[1, 2])
            ve.wait_ge(lam_in, 16)
            for i in range(2):
                ins = nc.vector.tensor_tensor_reduce(
                    out=onrm[:, 0, i * DH:(i + 1) * DH], in0=lamv[:, 2 * i, :],
                    in1=lamv[:, 2 * i + 1, :], scale=1.0, scalar=0.0, op0=ALU.mult, op1=ALU.add,
                    accum_out=tiny[:, 56 + i:57 + i])
                ins.then_inc(lam_sum, 1)
            split_p(0)

            for layer in range(2):
                qk, vn, wo = f"qk{layer}", f"v{layer}", f"wo{layer}"
                t_splits(vn)
                take_v(vn)
                split(START[vn] + 3 + RING)
                attention(layer)
                norm(f"ffn{layer}", wo, update(wo, proj=True), [START[wo] + 3 + RING])
                ffn(layer)
                if layer == 1:
                    split_p(1)
                down, gate = f"down{layer}", f"gate{layer}"
                t_splits(down)
                last = START[down] + COUNT[down] - 1
                norm(f"ple{layer}", None, update(down), [last + RING, last + 1 + RING])
                t_splits(gate, 2)

                def gated(t):
                    for n in range(2):
                        ve.wait_ge(g_out, 4 * layer + 2 * t + n + 1)
                        g = hn[:, t, n * 512:(n + 1) * 512]
                        link(nc.vector.tensor_tensor(g, tbank(t, n, True)[:], g, ALU.mult))
                        hs = h[:, t, n * 512:(n + 1) * 512]
                        nc.vector.tensor_tensor(hs, g, hs, ALU.add).then_inc(h_ok, 1)

                norm("mix1" if layer == 0 else "mix2", gate, gated, [START[gate] + 3 + RING])

            def pool_lo(g0):
                to, hi = (plo, phi) if g0 == 0 else (xlo[:, 6:8, :], xhi[:, 6:8, :])
                ve.wait_ge(mix_hi, MIX_BASE["evout"] + 1 + g0 // 2)
                for g in range(g0, g0 + 2):
                    ins = nc.vector.scalar_tensor_tensor(
                        out=to[:, g - g0, :], in0=bank[4 + g][:, 0:S],
                        scalar=pcol(COL_PSCALE + g), in1=hi[:, g - g0, :].bitcast(F32),
                        op0=ALU.mult, op1=ALU.subtract)
                ins.then_inc(mix_lo, 1)

            for i in range(6):
                split(START["ev"] + i + RING)
                if i == 4:
                    pool_lo(0)
            ve.wait_ge(copied, COPY_BASE["ev"] + 6)
            link(nc.vector.tensor_tensor(cval[:], z[:, 4:8, :], z[:, 8:12, :], ALU.mult))
            for tap in range(3):
                for i in range(4):
                    wc = pcol(COL_EVCONV + 3 * i + 2 - tap)
                    if tap == 0:
                        ins = nc.vector.tensor_scalar(ya[:, i, :], cval[:, i, :], wc, None,
                                                      ALU.mult)
                    else:
                        ins = nc.vector.scalar_tensor_tensor(
                            out=ya[:, i, tap:S], in0=cval[:, i, 0:S - tap], scalar=wc,
                            in1=ya[:, i, tap:S], op0=ALU.mult, op1=ALU.add)
                    if i == 3:
                        link(ins)
            ve.wait_ge(copied, COPY_BASE["ev"] + 8)
            nc.vector.tensor_tensor(ya[:], ya[:], z[:, 0:4, :], ALU.mult).then_inc(ya_ok, 1)
            pool_lo(2)
            split(START["ev"] + 6 + RING)
            ve.wait_ge(mix_hi, MIX_BASE["evout"] + 3)
            nc.vector.tensor_tensor(xlo[:, 0:4, :], ya[:], xhi[:, 0:4, :].bitcast(F32),
                                    ALU.subtract).then_inc(mix_lo, 1)
            split(START["ev"] + 7 + RING)
            ve.wait_ge(t5_row, 1)
            nc.vector.tensor_copy(t5row[:], bank[3][0:8, 0:384]).then_inc(t5_sb, 1)
            t_splits("evout", 2)
            norm("ffn2", "evout", update("evout"), [START["evout"] + 3 + RING])
            ffn(2)
            t_splits("down2", 2)
            norm("mix3", "down2", update("down2"), [START["down2"] + FT // 2 - 1 + RING])
            cf = START["f3"]
            split(cf + RING)
            ve.wait_ge(f_log, 1)
            lg, mn = osb_f(prob)
            link(nc.vector.tensor_scalar(mn, bank[cf % RING][:, 0:S], pcol(COL_BF), 0.0, ALU.add,
                                         ALU.min))
            link(nc.vector.tensor_tensor(mn, mn, lg, ALU.subtract))
            ones = prob[:, 2, 0:S]
            link(nc.vector.memset(ones, 1.0))
            link(nc.vector.tensor_tensor_scan(lg, ones, mn, 0.0, ALU.mult, ALU.add))
            ve.wait_ge(f_base, 2)
            nc.vector.tensor_copy(fmov[0:8, :, :], lg[0:8, :].unsqueeze(1).to_broadcast([8, 8, S])
                                  ).then_inc(f_ok, 1)
            nc.vector.tensor_copy(fstat[32:40, :, :],
                                  lg[32:40, :].unsqueeze(1).to_broadcast([8, 8, S])
                                  ).then_inc(f_ok, 1)
            t_splits("v3")
            take_v("v3")
            split(START["v3"] + 3 + RING)
            attention(2)
            norm("ffn3", "wo3", update("wo3", proj=True), [START["wo3"] + 3 + RING])
            ffn(3)
            t_splits("down3", 0)
            norm("final", None, update("down3"))

        @block.tensor
        def _(pe):
            mm = nc.tensor.matmul

            def norm(name, t):
                pe.wait_ge(hn_ok, 2 * XNORM[name] + t + 1)
                for i in range(2):
                    for k in range(4 * i, 4 * i + 4):
                        ins = mm(bank[4 + 2 * t + i][:, (k % 4) * P:(k % 4 + 1) * P],
                                 hn[:, t, k * P:(k + 1) * P], diag[:, t, :], start=True,
                                 stop=True)
                    ins.then_inc(tr_x, 1)

            def x_ready(name, t, i):
                pe.wait_ge(x_lo, 4 * XNORM[name] + 2 * t + i + 1)

            def f_tile(name, i, f, last, norm_name=None, between=None, turn=0):
                c = START[name] + i
                hi, lo = slot8(whi, c), slot8(wlo, c)
                pe.wait_ge(w_lo, c + 1 + RING * turn)
                dst, cs = bank[c % RING][:, f * S:(f + 1) * S], slice(f * P, (f + 1) * P)
                if norm_name:
                    n = 4 * XNORM[norm_name] + 2
                    for k0 in (0, 4):
                        pe.wait_ge(x_hi, n + k0 // 4 + 1)
                        for k in range(k0, k0 + 4):
                            mm(dst, hi[:, k, cs], xhi[:, k, :], start=(k == 0), stop=False)
                            mm(dst, lo[:, k, cs], xhi[:, k, :], start=False, stop=False)
                        pe.wait_ge(x_lo, n + k0 // 4 + 1)
                        for k in range(k0, k0 + 4):
                            ins = mm(dst, hi[:, k, cs], xlo[:, k, :], start=False,
                                     stop=(k == KT - 1))
                else:
                    for k in range(KT):
                        if between and k == 4:
                            between()
                        mm(dst, hi[:, k, cs], xhi[:, k, :], start=(k == 0), stop=False)
                        mm(dst, hi[:, k, cs], xlo[:, k, :], start=False, stop=False)
                        ins = mm(dst, lo[:, k, cs], xhi[:, k, :], start=False,
                                 stop=(k == KT - 1))
                if last:
                    ins.then_inc(w_used, 1)

            def f_chunk(name, i, norm_name=None, turn=0):
                for f in range(2):
                    f_tile(name, i, f, f == 1, norm_name if f == 0 else None, turn=turn)

            def t_piece(name, i, t, ah, al, proj=False, between=None):
                c, n_chunks = START[name] + i, COUNT[name]
                hi, lo = slot2(whi, c), slot2(wlo, c)
                pe.wait_ge(w_lo, c + 1)
                ts = slice(t * P, (t + 1) * P)
                for kk in range(2):
                    k = 2 * i + kk
                    if name == "evout":
                        ah, al = (xhi, xlo) if i else (phi, plo)
                        k = 2 * EVOUT_ORDER[i] + kk if i else kk
                    first, last = i == 0 and kk == 0, i == n_chunks - 1 and kk == 1
                    if between and kk == 1:
                        between()
                    if last:
                        for n in range(2):
                            dst, cs = tbank(t, n, proj)[:], slice(n * 512, (n + 1) * 512)
                            mm(dst, ah[:, k, ts], hi[:, kk, cs], start=first, stop=False)
                            mm(dst, ah[:, k, ts], lo[:, kk, cs], start=False, stop=False)
                            ins = mm(dst, al[:, k, ts], hi[:, kk, cs], start=False, stop=True)
                            if 2 * t + n < 3:
                                ins.then_inc(t_out, 1)
                        continue
                    for n in range(2):
                        mm(tbank(t, n, proj)[:], ah[:, k, ts], hi[:, kk, n * 512:(n + 1) * 512],
                           start=first, stop=False)
                    for n in range(2):
                        mm(tbank(t, n, proj)[:], ah[:, k, ts], lo[:, kk, n * 512:(n + 1) * 512],
                           start=False, stop=False)
                    for n in range(2):
                        ins = mm(tbank(t, n, proj)[:], al[:, k, ts],
                                 hi[:, kk, n * 512:(n + 1) * 512], start=False, stop=False)
                if t == TT - 1:
                    ins.then_inc(w_used, 1)

            def t_op(name, ah, al, ready=None, proj=False, fresh=None, following=None):
                count, lead = COUNT[name], name in LEADING
                i = 0
                while i < count:
                    paired = (fresh and fresh != "mix0") or (lead and i == count - 2)
                    group = range(i, i + 2) if paired else range(i, i + 1)
                    for t in range(TT):
                        for j in group:
                            if fresh:
                                x_ready(fresh, t, 1)
                            if ready:
                                ready(j, t)
                            between = None
                            if fresh and fresh != "mix0" and (j, t) == (1, 0):
                                between = lambda: norm(fresh, 1)
                            if lead and t == 1 and j == count - 1:
                                if name == "gate0":
                                    between = lambda: norm(following, 0)
                                elif following:
                                    norm(following, 0)
                            t_piece(name, j, t, ah, al, proj, between)
                    i += len(group)

            def ffn(layer, norm_name):
                def chunk(turn, jj):
                    first = isinstance(turn, int) and turn == 0
                    if not first:
                        pe.wait_ge(mul_ok, FT * layer + 1 + jj + RING * (turn - 1))
                    f_chunk(f"ffn{layer}", jj, norm_name if first and jj == 0 else None, turn)
                ffn_chunks(pe, chunk)

            def down(layer, following=None):
                def ready(i, t):
                    if t == 0:
                        pe.wait_ge(hid_lo, FT * layer + 2 * i + 2)
                t_op(f"down{layer}", hidhi, hidlo, ready, following=following)

            def attention(a):
                base, units = SC_BASE[a], UNITS
                qk, wo = ATTENTIONS[a]

                def scores(u):
                    j, m = u // 2, u % 2
                    rows = slice(DH * m, DH * (m + 1))
                    if u % 4 == 0:
                        pe.wait_ge(copied, COPY_BASE[qk] + 2 * (u // 4) + 2)
                    if u >= 2:
                        pe.wait_ge(sc_free, base + u - 1)
                    for t in range(TT):
                        off, n = span(a, t)
                        forget = a == 2 and u < 8
                        ts = slice(t * P, (t + 1) * P)
                        dst = bank[4 + u % 2][:, off:off + n]
                        ins = mm(dst, qkT[rows, j, ts], qkT[rows, 8 + j, 0:n], start=True,
                                 stop=not forget)
                        if forget:
                            ins = mm(dst, fstat[:, u, ts], fmov[:, u, 0:n], start=False, stop=True)
                    ins.then_inc(sc_out, 1)

                def transposes(u):
                    k = TR_BASE[a] + u
                    pe.wait_ge(prob_ok, k + 1)
                    if k >= 1:
                        pe.wait_ge(probT_ok, k)
                    if a == 0 and u >= 1:
                        pe.wait_ge(mix_lo, u)
                    src = prob[:, (2 * u if a == 0 else u) % 4, :]
                    for kt in range(TT):
                        for t in range(TT):
                            off, n = span(a, t)
                            if kt * P >= n:
                                continue
                            ins = nc.tensor.transpose(bank[6][:, tcol(a, kt, t):
                                                              tcol(a, kt, t) + P],
                                                      src[:, off + kt * P:off + (kt + 1) * P],
                                                      ident)
                    ins.then_inc(prob_tr, 1)

                def times_v(u):
                    k = TR_BASE[a] + u
                    pe.wait_ge(probT_ok, k + 1)
                    pt, b = probT[:, k % 2, :], bank[7]
                    if a == 0:
                        if u:
                            pe.wait_ge(o_norm, u)
                        for t in range(TT):
                            for kt in range(TT):
                                ins = mm(b[:, t * P:(t + 1) * P],
                                         pt[:, tcol(a, kt, t):tcol(a, kt, t) + P],
                                         v[:, kt, u * P:(u + 1) * P], start=(kt == 0),
                                         stop=(kt == TT - 1))
                    else:
                        j, m = u // 2, u % 2
                        if j and m == 0:
                            pe.wait_ge(mix_lo, MIX_BASE[wo] + j)
                        rows = slice(DH * m, DH * (m + 1))
                        for kt in range(TT):
                            q0 = P if a == 2 and kt == 1 else 0
                            ins = mm(b[rows, q0:S], v[:, kt, u * DH:(u + 1) * DH],
                                     pt[:, tcol(a, kt, q0 // P):tcol(a, kt, 1) + P],
                                     start=(kt == 0), stop=(kt == TT - 1))
                    ins.then_inc(pv_out, 1)

                def o_transposes(j):
                    pe.wait_ge(o_norm, j + 1)
                    pe.wait_ge(probT_ok, j + 1)
                    for t in range(TT):
                        ins = nc.tensor.transpose(bank[6][:, t * P:(t + 1) * P], onrm[:, t, :],
                                                  ident)
                    ins.then_inc(o_tr, 1)

                def at_scores(s):
                    if s == 4:
                        pe.wait_ge(v_ok, 4 * (a + 1))
                        if a == 2:
                            pe.wait_ge(f_ok, 2)
                    if 0 <= s - 4 < units:
                        scores(s - 4)

                def halfway(s):
                    u = s - 4
                    if a > 0 or u % 4 == 0:
                        at_scores(s)
                    if a == 0:
                        if s % 2 == 0 and s >= 8:
                            o_transposes((s - 8) // 2)
                        if s % 2 == 1 and 7 <= s < 23:
                            times_v((s - 7) // 2)
                    elif 1 <= u < units + 1:
                        transposes(u - 1)

                for s in range(STEPS):
                    u = s - 4
                    between = lambda: halfway(s)
                    if a == 0 and u % 4:
                        at_scores(s)
                    if a == 0 and s == STEPS - 2:
                        halfway(s)
                        between = None
                    if s < 16:
                        if s % 2 == 0 and s // 2 >= RING:
                            pe.wait_ge(copied, COPY_BASE[qk] + s // 2 - RING + 1)
                        f_tile(qk, s // 2, s % 2, s % 2 == 1, between=between)
                    else:
                        i = (s - 16) // 2
                        if s == 16:
                            pe.wait_ge(copied, COPY_BASE[qk] + 8)
                        pe.wait_ge(mix_lo, MIX_BASE[wo] + 2 * i + 2)
                        t_piece(wo, i, s % 2, ohi[a], olo[a], proj=True, between=between)
                    if a == 0:
                        if s % 2 == 0 and 6 <= s < 22:
                            transposes((s - 6) // 2)
                    elif 1 <= u < units + 1:
                        times_v(u - 1)

            for layer in range(2):
                vn, mix, ple, gate = (f"{m}{layer}" for m in ("v", "mix", "ple", "gate"))
                if layer == 0:
                    for t in range(TT):
                        norm(mix, t)
                t_op(vn, xhi, xlo, fresh=mix)
                attention(layer)
                for t in range(TT):
                    norm(f"ffn{layer}", t)
                ffn(layer, f"ffn{layer}")
                down(layer)
                pe.wait_ge(p_lo, layer + 1)
                pe.wait_ge(mul_ok, FT * (layer + 1))
                for t in range(TT):
                    t_piece(f"proj{layer}", 0, t, phi, plo, proj=True)
                    if t == 0:
                        norm(ple, 0)
                t_op(gate, xhi, xlo, fresh=ple, following="mix1" if layer == 0 else None)
            for t in range(TT):
                norm("mix2", t)
            for i in range(COUNT["ev"]):
                if i >= RING:
                    pe.wait_ge(copied, COPY_BASE["ev"] + i - RING + 1)
                f_chunk("ev", i, "mix2" if i == 0 else None)
                if i == 4:
                    pe.wait_ge(t5_in, 32)
                    mm(bank[3][0:8, 0:384], relb[:], onehot[:], start=True, stop=True
                       ).then_inc(t5_row, 1)
                    pe.wait_ge(ev_in, 32)
                    for g in range(4):
                        pe.wait_ge(pool_ok, g + 1)
                        mm(bank[4 + g][:, 0:S], pw[:, g, :],
                           pool[:, 1 if g % 2 == 0 else 2, g, 16:16 + S],
                           start=True, stop=True).then_inc(pool_out, 1)
            def ev_ready(i, t):
                pe.wait_ge(mix_lo, MIX_BASE["evout"] + (min(i, 2) + 1, min(max(i, 1), 2) + 1)[t])
            t_op("evout", None, None, ev_ready, following="ffn2")
            norm("ffn2", 1)
            ffn(2, "ffn2")
            down(2, "mix3")
            norm("mix3", 1)
            f_tile("f3", 0, 0, True, "mix3")
            t_op("v3", xhi, xlo)
            pe.wait_ge(f_ok, 2)
            attention(2)
            for t in range(TT):
                norm("ffn3", t)
            ffn(3, "ffn3")
            down(3)


def span(a, t):
    return (t * S, S) if a < 2 else ((0, P) if t == 0 else (P, S))


def tcol(a, kt, t):
    return kt * S + t * P if a < 2 or kt == 0 else S


def osb_f(prob):
    return prob[:, 0, 0:S], prob[:, 1, 0:S]


def constants():
    c = np.zeros((P, NCONST), np.float32)
    p = np.arange(P)
    c[:, C_ID:C_ID + P] = np.eye(P)
    k = np.arange(S)
    for t in range(TT):
        c[:, C_DIST + t * S:C_DIST + (t + 1) * S] = np.abs(p[:, None] + t * P - k[None, :])
    cols = np.arange(GRID_W)
    start = np.clip(cols - 8, 0, GRID_W - 16)
    inside = (cols[None, :] >= start[:, None]) & (cols[None, :] < start[:, None] + 16)
    c[:, C_COLM:C_COLM + GRID_W] = np.where(np.tile(inside, (2, 1)), 0.0, MASKED)
    diag = np.where(p[None, :] <= p[:, None], 0.0, MASKED)
    c[:, C_CAUS:C_CAUS + P] = diag
    c[:, C_CAUS + 2 * P:C_CAUS + 3 * P] = diag
    for h in range(8):
        c[h, C_SEL + h] = -1.0
        c[32 + h, C_SEL + 8 + h] = 1.0
    d = np.maximum(255 - np.arange(384), 0)
    log_b = 16 + (np.log(np.maximum(d, 1) / 16.0) / np.log(8.0) * 16 + 1e-9).astype(np.int64)
    bucket = np.where(d < 16, d, np.minimum(log_b, 31))
    onehot = (np.arange(32)[:, None] == bucket[None, :]).astype(np.float32)
    inv = np.stack([1.0 / np.minimum(k + 1, wd) for wd in (2, 4, 8, 16)]).astype(np.float32)
    inv = np.broadcast_to(inv[None], (P, 4, S)).copy()
    return c, onehot, inv


def by_tile(a):
    a = a.reshape(a.shape[0] // P, P, -1)
    return a.transpose(1, 0, 2).reshape(P, -1)


def kernel(**inputs):
    import concourse.bacc as bacc
    from concourse.bass_utils import run_bass_kernel_spmd

    i = {k: np.ascontiguousarray(a) for k, a in inputs.items()}
    c, onehot, inv = constants()
    heads8 = np.zeros((P, 1), np.float32)
    heads8[0:8, 0] = i["od_b_f_2"][0]
    heads8[32:40, 0] = i["od_b_f_2"][0]
    cols = np.concatenate(
        [by_tile(i["na_b_qkv"][0, :2048])]
        + [by_tile(i["ev_conv_w_2"][0].T), by_tile(i["ev_pool_scale_2"][0])]
        + [by_tile(i["ffn_conv_w_2"][l].T) for l in range(2)]
        + [by_tile(i["ffn_conv_b_2"][l]) for l in range(2)]
        + [by_tile(i["da_subln"][0]), heads8], axis=1)
    w_f = np.zeros((D, 256), np.float32)
    w_f[:, 0:8] = i["od_w_in_2"][0, :, 3072:]
    w_f[:, 32:40] = i["od_w_in_2"][0, :, 3072:]
    arrays = {
        "x": i["x"][0],
        "p": i["p"][:, 0].transpose(0, 2, 1),
        "gammas": np.stack([i["norm_mix"][0], i["norm_ffn"][0], i["norm_ple"][0],
                            i["norm_mix"][1], i["norm_ffn"][1], i["norm_ple"][1],
                            i["norm_final"],
                            i["mix_norm_g_2"][0], i["ffn_norm_g_2"][0],
                            i["mix_norm_g_2"][1], i["ffn_norm_g_2"][1], i["final_norm_g_2"]]),
        "lam": np.stack([i[f"da_lambda_{n}"][0] for n in ("q1", "k1", "q2", "k2")]),
        "v_bias": i["na_b_qkv"][0, 2048:],
        "rpb": i["na_rpb"][0],
        "rel_bias": i["rel_bias_2"],
        "pool_w": i["ev_pool_w_2"][0],
        "da_w_qkv": i["da_w_qkv"][0], "da_w_o": i["da_w_o"][0],
        "na_w_qkv": i["na_w_qkv"][0], "na_w_o": i["na_w_o"][0],
        "ffn_w_gate": i["ffn_w_gate"], "ffn_w_up": i["ffn_w_up"], "ffn_w_down": i["ffn_w_down"],
        "ple_w_proj": i["ple_w_proj"], "ple_w_gate": i["ple_w_gate"],
        "ev_w_in": i["ev_w_in_2"][0], "ev_w_out": i["ev_w_out_2"][0],
        "od_w_in": i["od_w_in_2"][0], "od_w_out": i["od_w_out_2"][0], "w_f": w_f,
        "ffn_w_in": i["ffn_w_in_2"], "ffn_w_out": i["ffn_w_out_2"],
        "onehot": onehot, "consts": c, "cols": cols, "evconst": inv,
    }
    nc = bacc.Bacc("TRN2", target_bir_lowering=False, num_devices=1)
    arrays = {k: np.ascontiguousarray(a) for k, a in arrays.items()}
    w = {k: nc.dram_tensor(f"in_{k}", a.shape, mybir.dt.from_np(a.dtype),
                           kind="ExternalInput").ap() for k, a in arrays.items()}
    out = nc.dram_tensor("out", (S, D), F32, kind="ExternalOutput").ap()
    for layer, (qkv, wo) in enumerate((("da_w_qkv", "da_w_o"), ("na_w_qkv", "na_w_o"))):
        w[f"qk{layer}"], w[f"v{layer}"] = w[qkv], w[qkv][:, 2048:3072]
        w[f"wo{layer}"] = w[wo]
        w[f"ffn{layer}"] = (w["ffn_w_gate"][layer], w["ffn_w_up"][layer])
        w[f"down{layer}"] = w["ffn_w_down"][layer]
        w[f"proj{layer}"], w[f"gate{layer}"] = w["ple_w_proj"][layer], w["ple_w_gate"][layer]
    for layer in (2, 3):
        m = w["ffn_w_in"][layer - 2]
        w[f"ffn{layer}"] = (m[:, 0:FFN], m[:, FFN:2 * FFN])
        w[f"down{layer}"] = w["ffn_w_out"][layer - 2]
    w["ev"], w["evout"] = w["ev_w_in"], w["ev_w_out"]
    w["qk3"], w["v3"], w["wo3"] = w["od_w_in"], w["od_w_in"][:, 2048:3072], w["od_w_out"]
    w["f3"] = w["w_f"]
    mixer_kernel(nc, w, w["cols"], w["consts"], w["evconst"], out)
    r = run_bass_kernel_spmd(nc, [{f"in_{k}": a for k, a in arrays.items()}], core_ids=[0])
    return r.results[0]["out"].reshape(1, S, D)
```
